# Optimizing a Trainium2 kernel written in Bass

```python
import math
import jax, jax.numpy as jnp
from jax import lax
import numpy as np

D_MODEL = 1024
BATCH = 1
SEQ = 256
DEPTH = 1

N_MEM = 256
DA_HEADS = 4
DA_HEAD_DIM = 64
DA_V_DIM = 2 * DA_HEAD_DIM
DA_WIDTH = DA_HEADS * 2 * DA_HEAD_DIM
ROPE_THETA = 10000.0
Q_BLOCK = 128
SSM_WIDTH = 512
SSM_GROUP = 16
SSM_GROUPS = SSM_WIDTH // SSM_GROUP
SSM_STATE = 64
X_HEADS = 4
X_HEAD_DIM = D_MODEL // X_HEADS
N_EXPERTS = 32
TOP_K = 4
D_FF = D_MODEL
SWIGLU_LIMIT = 7.0
SWIGLU_ALPHA = 1.702
MOE_BLOCK = 256
EPS = 1e-6
IN_WIDTH = 3 * DA_WIDTH + SSM_WIDTH + 2 * D_MODEL
IN_SPLITS = (DA_WIDTH, 2 * DA_WIDTH, 3 * DA_WIDTH, 3 * DA_WIDTH + SSM_WIDTH, 3 * DA_WIDTH + SSM_WIDTH + D_MODEL)

kernel_name = 'hybrid_diffattn_s5_moe_encoder_layer'

def rms_norm(x, g):
    xf = x.astype(jnp.float32)
    y = xf * lax.rsqrt(jnp.mean(xf * xf, axis=-1, keepdims=True) + EPS)
    return (y * g.astype(jnp.float32)).astype(x.dtype)

def rope(x, pos):
    dh = x.shape[-1]
    half = dh // 2
    inv = ROPE_THETA ** (-jnp.arange(half, dtype=jnp.float32) * (2.0 / dh))
    ang = pos.astype(jnp.float32)[:, None] * inv[None, :]
    shape = (1, pos.shape[0]) + (1,) * (x.ndim - 3) + (half,)
    cos = jnp.cos(ang).reshape(shape)
    sin = jnp.sin(ang).reshape(shape)
    xf = x.astype(jnp.float32)
    x1, x2 = xf[..., :half], xf[..., half:]
    return jnp.concatenate([x1 * cos - x2 * sin, x2 * cos + x1 * sin], axis=-1).astype(x.dtype)

def diff_attention(q, k, v, lam, subln_g, lambda_init):
    b, l = q.shape[:2]
    nb = l // Q_BLOCK
    scale = DA_HEAD_DIM ** -0.5
    qb = q.reshape(b, nb, Q_BLOCK, DA_HEADS, 2, DA_HEAD_DIM).swapaxes(0, 1)

    def one_block(qi):
        s = jnp.einsum('bqhcd,bkhcd->bhcqk', qi, k, preferred_element_type=jnp.float32) * scale
        p = jax.nn.softmax(s, axis=-1)
        w = p[:, :, 0] - lam * p[:, :, 1]
        return jnp.einsum('bhqk,bkhe->bqhe', w.astype(v.dtype), v)

    o = lax.map(one_block, qb)
    o = o.swapaxes(0, 1).reshape(b, l, DA_HEADS, DA_V_DIM)
    o = rms_norm(o, subln_g) * (1.0 - lambda_init)
    return o.reshape(b, l, DA_WIDTH)

def s5_direction(u, a_re, a_im, log_dt, b_re, b_im, c_re, c_im, reverse):
    f32 = jnp.float32
    a_re = a_re.astype(f32)
    a_im = a_im.astype(f32)
    dt = jnp.exp(log_dt.astype(f32))[:, None]
    mag = jnp.exp(a_re * dt)
    ang = a_im * dt
    ab_re = mag * jnp.cos(ang)
    ab_im = mag * jnp.sin(ang)
    den = a_re * a_re + a_im * a_im
    nr = ab_re - 1.0
    coef_re = (nr * a_re + ab_im * a_im) / den
    coef_im = (ab_im * a_re - nr * a_im) / den
    b_re = b_re.astype(f32)
    b_im = b_im.astype(f32)
    bb_re = coef_re[..., None] * b_re - coef_im[..., None] * b_im
    bb_im = coef_re[..., None] * b_im + coef_im[..., None] * b_re
    bu_re = jnp.einsum('lbgh,gph->lbgp', u, bb_re)
    bu_im = jnp.einsum('lbgh,gph->lbgp', u, bb_im)
    l = u.shape[0]
    sa_re = jnp.broadcast_to(ab_re[None, None], (l, 1) + ab_re.shape)
    sa_im = jnp.broadcast_to(ab_im[None, None], (l, 1) + ab_im.shape)

    def combine(e1, e2):
        a1r, a1i, b1r, b1i = e1
        a2r, a2i, b2r, b2i = e2
        return (a2r * a1r - a2i * a1i,
                a2r * a1i + a2i * a1r,
                a2r * b1r - a2i * b1i + b2r,
                a2r * b1i + a2i * b1r + b2i)

    _, _, xr, xi = lax.associative_scan(combine, (sa_re, sa_im, bu_re, bu_im), reverse=reverse, axis=0)
    return (jnp.einsum('lbgp,ghp->lbgh', xr, c_re.astype(f32))
            - jnp.einsum('lbgp,ghp->lbgh', xi, c_im.astype(f32)))

def s5_mixer(u, a_re, a_im, log_dt, b_re, b_im, c_re, c_im, d_skip, w_glu):
    b, l, _ = u.shape
    uf = u.astype(jnp.float32)
    ug = uf.reshape(b, l, SSM_GROUPS, SSM_GROUP).transpose(1, 0, 2, 3)
    y = (s5_direction(ug, a_re[0], a_im[0], log_dt[0], b_re[0], b_im[0], c_re[0], c_im[0], False)
         + s5_direction(ug, a_re[1], a_im[1], log_dt[1], b_re[1], b_im[1], c_re[1], c_im[1], True))
    y = y.transpose(1, 0, 2, 3).reshape(b, l, SSM_WIDTH) + d_skip.astype(jnp.float32) * uf
    y = jax.nn.gelu(y).astype(u.dtype)
    val, gate = jnp.split(y @ w_glu, 2, axis=-1)
    return val * jax.nn.sigmoid(gate)

def hybrid_mixer(hn, w_in, lambda_q1, lambda_k1, lambda_q2, lambda_k2, subln_g,
                 a_re, a_im, log_dt, b_re, b_im, c_re, c_im, d_skip, w_glu,
                 w_branch_attn, w_branch_ssm, w_mix_out, lambda_init):
    b, l, _ = hn.shape
    q, k, v, u, g_a, g_s = jnp.split(hn @ w_in, IN_SPLITS, axis=-1)
    pos = jnp.arange(l, dtype=jnp.int32)
    q = rope(q.reshape(b, l, DA_HEADS, 2, DA_HEAD_DIM), pos)
    k = rope(k.reshape(b, l, DA_HEADS, 2, DA_HEAD_DIM), pos)
    v = v.reshape(b, l, DA_HEADS, DA_V_DIM)
    f32 = jnp.float32
    lam = (jnp.exp(jnp.sum(lambda_q1.astype(f32) * lambda_k1.astype(f32)))
           - jnp.exp(jnp.sum(lambda_q2.astype(f32) * lambda_k2.astype(f32))) + lambda_init)
    o_a = diff_attention(q, k, v, lam, subln_g, lambda_init)
    o_s = s5_mixer(u, a_re, a_im, log_dt, b_re, b_im, c_re, c_im, d_skip, w_glu)
    merged = jax.nn.sigmoid(g_a) * (o_a @ w_branch_attn) + jax.nn.sigmoid(g_s) * (o_s @ w_branch_ssm)
    return merged @ w_mix_out

def cross_attention(hn, mem_n, w_xq, w_xkv, w_xo):
    b, l, _ = hn.shape
    q = (hn @ w_xq).reshape(b, l, X_HEADS, X_HEAD_DIM)
    k, v = jnp.split(mem_n @ w_xkv, 2, axis=-1)
    k = k.reshape(b, -1, X_HEADS, X_HEAD_DIM)
    v = v.reshape(b, -1, X_HEADS, X_HEAD_DIM)
    s = jnp.einsum('bqhd,bkhd->bhqk', q, k, preferred_element_type=jnp.float32) * (X_HEAD_DIM ** -0.5)
    p = jax.nn.softmax(s, axis=-1)
    o = jnp.einsum('bhqk,bkhd->bqhd', p.astype(v.dtype), v).reshape(b, l, D_MODEL)
    return o @ w_xo

def moe_ffn(hn, w_router, b_router, w_e1, b_e1, w_e2, b_e2):
    f32 = jnp.float32
    b, l, d = hn.shape
    t = hn.reshape(-1, d)
    n_tok = t.shape[0]
    n_asg = n_tok * TOP_K
    logits = jnp.dot(t, w_router, preferred_element_type=f32) + b_router.astype(f32)
    top_v, top_i = lax.top_k(logits, TOP_K)
    gates = jax.nn.softmax(top_v, axis=-1)
    flat_e = top_i.reshape(-1).astype(jnp.int32)
    flat_tok = jnp.arange(n_asg, dtype=jnp.int32) // TOP_K
    flat_w = gates.reshape(-1)
    order = jnp.argsort(flat_e)
    sorted_e = flat_e[order]
    counts = jnp.bincount(flat_e, length=N_EXPERTS).astype(jnp.int32)
    padded = (counts + MOE_BLOCK - 1) // MOE_BLOCK * MOE_BLOCK
    pad_end = jnp.cumsum(padded)
    pad_start = pad_end - padded
    grp_start = jnp.cumsum(counts) - counts
    rank = jnp.arange(n_asg, dtype=jnp.int32) - grp_start[sorted_e]
    dest = pad_start[sorted_e] + rank
    n_pad = n_asg + N_EXPERTS * MOE_BLOCK
    n_blk = n_pad // MOE_BLOCK
    row_tok = jnp.zeros((n_pad,), jnp.int32).at[dest].set(flat_tok[order])
    row_w = jnp.zeros((n_pad,), f32).at[dest].set(flat_w[order])
    blk_start = jnp.arange(n_blk, dtype=jnp.int32) * MOE_BLOCK
    blk_e = jnp.minimum(jnp.searchsorted(pad_end, blk_start, side='right'), N_EXPERTS - 1).astype(jnp.int32)
    xs = t[row_tok].reshape(n_blk, MOE_BLOCK, d)

    def expert_block(args):
        xb, e = args
        hid = xb @ w_e1[e] + b_e1[e]
        gate = jnp.minimum(hid[:, :D_FF], SWIGLU_LIMIT)
        lin = jnp.clip(hid[:, D_FF:], -SWIGLU_LIMIT, SWIGLU_LIMIT)
        act = gate * jax.nn.sigmoid(SWIGLU_ALPHA * gate) * (lin + 1.0)
        return act @ w_e2[e] + b_e2[e]

    ys = lax.map(expert_block, (xs, blk_e)).reshape(n_pad, d)
    out = jax.ops.segment_sum(ys.astype(f32) * row_w[:, None], row_tok, num_segments=n_tok)
    return out.astype(hn.dtype).reshape(b, l, d)

def setup_inputs(seed: int = 0) -> dict:
    key = jax.random.key(seed)
    ks = iter(jax.random.split(key, 40))
    f32 = jnp.float32
    L = DEPTH
    G, P, HG = SSM_GROUPS, SSM_STATE, SSM_GROUP

    def nrm(shape, fan_in):
        return jax.random.normal(next(ks), shape, f32) * (fan_in ** -0.5)

    def gain(shape):
        return 1.0 + 0.02 * jax.random.normal(next(ks), shape, f32)

    def small(shape, s):
        return s * jax.random.normal(next(ks), shape, f32)

    n_idx = jnp.arange(SSM_STATE, dtype=f32)
    return {
        'x': jax.random.normal(next(ks), (BATCH, SEQ, D_MODEL), f32),
        'mem': jax.random.normal(next(ks), (BATCH, N_MEM, D_MODEL), f32),
        'norm_mix_g': gain((L, D_MODEL)),
        'w_in': nrm((L, D_MODEL, IN_WIDTH), D_MODEL),
        'lambda_q1': small((L, DA_HEAD_DIM), 0.1),
        'lambda_k1': small((L, DA_HEAD_DIM), 0.1),
        'lambda_q2': small((L, DA_HEAD_DIM), 0.1),
        'lambda_k2': small((L, DA_HEAD_DIM), 0.1),
        'subln_g': gain((L, DA_V_DIM)),
        'ssm_a_re': -0.5 + small((L, 2, G, P), 0.01),
        'ssm_a_im': math.pi * n_idx + small((L, 2, G, P), 0.01),
        'ssm_log_dt': jax.random.uniform(next(ks), (L, 2, G), f32, math.log(1e-3), math.log(1e-1)),
        'ssm_b_re': nrm((L, 2, G, P, HG), 2 * HG),
        'ssm_b_im': nrm((L, 2, G, P, HG), 2 * HG),
        'ssm_c_re': nrm((L, 2, G, HG, P), 2 * P),
        'ssm_c_im': nrm((L, 2, G, HG, P), 2 * P),
        'ssm_d': jax.random.normal(next(ks), (L, SSM_WIDTH), f32),
        'w_glu': nrm((L, SSM_WIDTH, 2 * SSM_WIDTH), SSM_WIDTH),
        'w_branch_attn': nrm((L, DA_WIDTH, D_MODEL), DA_WIDTH),
        'w_branch_ssm': nrm((L, SSM_WIDTH, D_MODEL), SSM_WIDTH),
        'w_mix_out': nrm((L, D_MODEL, D_MODEL), D_MODEL),
        'norm_cross_g': gain((L, D_MODEL)),
        'norm_mem_g': gain((L, D_MODEL)),
        'w_xq': nrm((L, D_MODEL, D_MODEL), D_MODEL),
        'w_xkv': nrm((L, D_MODEL, 2 * D_MODEL), D_MODEL),
        'w_xo': nrm((L, D_MODEL, D_MODEL), D_MODEL),
        'norm_ffn_g': gain((L, D_MODEL)),
        'w_router': nrm((L, D_MODEL, N_EXPERTS), D_MODEL),
        'b_router': small((L, N_EXPERTS), 0.01),
        'w_e1': nrm((L, N_EXPERTS, D_MODEL, 2 * D_FF), D_MODEL),
        'b_e1': small((L, N_EXPERTS, 2 * D_FF), 0.01),
        'w_e2': nrm((L, N_EXPERTS, D_FF, D_MODEL), D_FF),
        'b_e2': small((L, N_EXPERTS, D_MODEL), 0.01),
        'norm_final_g': gain((D_MODEL,)),
    }

def reference(x, mem, norm_mix_g, w_in, lambda_q1, lambda_k1, lambda_q2, lambda_k2, subln_g,
              ssm_a_re, ssm_a_im, ssm_log_dt, ssm_b_re, ssm_b_im, ssm_c_re, ssm_c_im, ssm_d, w_glu,
              w_branch_attn, w_branch_ssm, w_mix_out, norm_cross_g, norm_mem_g, w_xq, w_xkv, w_xo,
              norm_ffn_g, w_router, b_router, w_e1, b_e1, w_e2, b_e2, norm_final_g):
    h = x
    for layer in range(DEPTH):
        lambda_init = 0.8 - 0.6 * math.exp(-0.3 * layer)
        hn = rms_norm(h, norm_mix_g[layer])
        h = h + hybrid_mixer(hn, w_in[layer], lambda_q1[layer], lambda_k1[layer], lambda_q2[layer],
                             lambda_k2[layer], subln_g[layer], ssm_a_re[layer], ssm_a_im[layer],
                             ssm_log_dt[layer], ssm_b_re[layer], ssm_b_im[layer], ssm_c_re[layer],
                             ssm_c_im[layer], ssm_d[layer], w_glu[layer], w_branch_attn[layer],
                             w_branch_ssm[layer], w_mix_out[layer], lambda_init)
        h = h + cross_attention(rms_norm(h, norm_cross_g[layer]), rms_norm(mem, norm_mem_g[layer]),
                                w_xq[layer], w_xkv[layer], w_xo[layer])
        h = h + moe_ffn(rms_norm(h, norm_ffn_g[layer]), w_router[layer], b_router[layer],
                        w_e1[layer], b_e1[layer], w_e2[layer], b_e2[layer])
    return rms_norm(h, norm_final_g)


_drawn_inputs = setup_inputs


def setup_inputs(seed=0):
    import zlib

    import numpy as np

    out = dict(_drawn_inputs(seed))
    spreads = {}
    factors = {'ssm_a_re': 64.0,
     'norm_cross_g': 3.899,
     'norm_mem_g': 2.883,
     'b_e1': 24.876,
     'b_e2': 28.639,
     'norm_final_g': 8.078,
     'ssm_b_re': 2.972,
     'ssm_b_im': 3.076,
     'ssm_c_re': 3.019,
     'ssm_c_im': 3.134,
     'norm_ffn_g': 3.027,
     'b_router': 3.953}
    for name, (base, spread) in spreads.items():
        noise = np.random.default_rng([zlib.crc32(name.encode()), seed]).standard_normal(out[name].shape)
        drawn = base * np.exp(spread * noise) if base else spread * noise
        out[name] = __import__('jax').numpy.asarray(drawn.astype(out[name].dtype))
    for name, factor in factors.items():
        out[name] = (out[name] * factor).astype(out[name].dtype)
    return out
```

```python
from contextlib import ExitStack

import concourse.bass as bass
from concourse import mybir

F32 = mybir.dt.float32
I32 = mybir.dt.int32
ALU = mybir.AluOpType
ACT = mybir.ActivationFunctionType
AX = mybir.AxisListType

P = 128
D = 1024
L = 256
KD = D // P
NT = L // P
HEADS = 4
DH = 64
WA = 512
G, NS, HG = 32, 64, 16
TC = 8
NC = L // TC
NE, TOPK = 32, 4
SLOTS = 64
EXTRA = (L * TOPK - 1) // SLOTS
MAXB = (L + SLOTS - 1) // SLOTS
EPS = 1e-6
LAMBDA_INIT = 0.2
TWO_PI = 6.283185307179586
PI_A, PI_B, PI_C = 6.28125, 0.0019350051879882812, 3.0199159819567e-07
ROUND = 12582912.0
GATE_MAX = 7.0
GATE_ALPHA = 1.702
STAGE = 4

C_ID = 0
C_UP = C_ID + P
C_ONE = C_UP + P
C_BLK = C_ONE + P
C_M16 = C_BLK + P
C_IOTA = C_M16 + HG
C_COS = C_IOTA + 64
C_SIN = C_COS + NT * 32
C_TRI = C_SIN + NT * 32
C_END = C_TRI + NE


def constants():
    import numpy as np

    c = np.zeros((P, C_END), np.float32)
    r = np.arange(P)
    c[:, C_ID:C_ID + P] = np.eye(P)
    c[:, C_UP:C_UP + P] = r[:, None] < r[None, :]
    c[:, C_ONE:C_ONE + P] = 1
    c[:, C_BLK:C_BLK + P] = r[:, None] // HG == r[None, :] // HG
    c[:, C_M16:C_M16 + HG] = r[:, None] % HG == np.arange(HG)[None, :]
    c[:, C_IOTA:C_IOTA + 64] = np.arange(64)[None, :]
    inv = (np.float32(10000.0) ** (-np.arange(32, dtype=np.float32) * np.float32(2.0 / DH))).astype(np.float32)
    for t in range(NT):
        ang = ((t * P + r).astype(np.float32)[:, None] * inv[None, :]).astype(np.float32)
        c[:, C_COS + 32 * t:C_COS + 32 * t + 32] = np.cos(ang)
        c[:, C_SIN + 32 * t:C_SIN + 32 * t + 32] = np.sin(ang)
    c[:, C_TRI:C_TRI + NE] = (r[:, None] <= np.arange(NE)[None, :]) & (r[:, None] < NE)
    return c


def build(nc, T, out):
    ctx = ExitStack()
    with ctx:
        def sb(name, cols, parts=P, dt=F32):
            return ctx.enter_context(nc.sbuf_tensor(name, [parts, cols], dt))

        def sem(name):
            return ctx.enter_context(nc.semaphore(name))

        ring = sb("ring", 8 * 2048 + 8 * 1024)
        w1 = ring[:, 0:16384].rearrange("p (k n) -> p k n", k=KD)
        w2 = ring[:, 16384:24576].rearrange("p (k n) -> p k n", k=KD)
        s5w = ring[:, 0:8192].rearrange("p (c g t h) -> p c g t h", c=2, g=G, t=TC)
        s5b = ring[:, 8192:16384].rearrange("p (g c t h) -> p g c t h", g=G, c=2, t=TC)
        lin = ring[:, 8192:16384].rearrange("p (g c m) -> p g c m", g=G, c=2)
        toep = ring[:, 16384:20480].rearrange("p (g m) -> p g m", g=G)
        bsplit = ring[:, 20480:22528].rearrange("p (c g d h) -> p c g d h", c=2, g=G, d=2)
        zst = ring[:, 20480:22528].rearrange("p (k c g) -> p k c g", k=NC, c=2)
        bbar = ring[:, 22528:23552].rearrange("p (c g h) -> p c g h", c=2, g=G)
        tmp_v = ring[:, 23552:24064].rearrange("p (g h) -> p g h", g=G)
        tmp_p = ring[:, 24064:24576].rearrange("p (g h) -> p g h", g=G)
        taps_t = ring[:, 23552:24576].rearrange("p (d g h) -> p d g h", d=2, g=G)
        xst = ring[:, 22528:24576].rearrange("p (k c g) -> p k c g", k=NC, c=2)
        enter = ring[:, 8192:10240].rearrange("p (c g k) -> p c g k", c=2, g=G)
        yg = ring[:, 10240:11264].rearrange("p (a n) -> p a n", a=8)
        craw = ring[:, 16384:17408].rearrange("p (c j m) -> p c j m", c=2, j=4)
        braw = ring[:, 17408:18432].rearrange("p (c g h) -> p c g h", c=2, g=G)
        y4 = ring[:, 11264:12288].rearrange("p (t a h) -> p t a h", t=TC, a=8)
        prep = ring[0:G, 8192:16384]

        stage = sb("stage", STAGE * 2048)
        slot = [stage[:, i * 2048:(i + 1) * 2048].rearrange("p (k n) -> p k n", k=4) for i in range(STAGE)]
        con = sb("con", C_END)
        ident = con[:, C_ID:C_ID + P]
        ones = con[:, C_ONE:C_ONE + P]
        hres = sb("hres", NT * D)
        h3 = hres[:, :].rearrange("p (t n) -> p t n", t=NT)
        hnt = sb("hnt", KD * L)
        hnT = hnt[:, :].rearrange("p (k l) -> p k l", k=KD)
        a1 = sb("a1", 2048)
        a2 = sb("a2", 2048)
        t1, t2, t3 = sb("t1", 2048), sb("t2", 2048), sb("t3", 2048)
        gaT = a1[:, :].rearrange("p (k l) -> p k l", k=KD)
        gsT = a2[:, :].rearrange("p (k l) -> p k l", k=KD)
        pw = a1[0:G, :].rearrange("p (c t m) -> p c t m", c=2, t=TC)
        xn = a2[:, :].rearrange("p (t n) -> p t n", t=NT)
        usb = a2[:, 0:1024].rearrange("p (t n) -> p t n", t=NT)
        u4 = a2[:, 1024:2048].rearrange("p (t n) -> p t n", t=TC)
        u5 = a2[:, 0:1024].rearrange("p (a t h) -> p a t h", a=8, t=TC)
        qn = t1[:, 0:1024].rearrange("p (t n) -> p t n", t=NT)
        kn = t1[:, 1024:2048].rearrange("p (t n) -> p t n", t=NT)
        vn = t2[:, 0:1024].rearrange("p (t n) -> p t n", t=NT)
        qT = t2[:, 1024:2048].rearrange("p (h l) -> p h l", h=HEADS)
        kT = t3[:, 0:1024].rearrange("p (h l) -> p h l", h=HEADS)
        wT = t3[:, 1024:2048].rearrange("p (b k l) -> p b k l", b=2, k=NT)
        prob = t1[:, 0:1024].rearrange("p (c t l) -> p c t l", c=2, t=NT)
        on = t1[:, 1024:2048].rearrange("p (t h e) -> p t h e", t=NT, h=HEADS)
        memT = t1[:, :].rearrange("p (k l) -> p k l", k=KD)
        mkT = t2[:, :].rearrange("p (k l) -> p k l", k=KD)
        mn = t3[:, :].rearrange("p (t n) -> p t n", t=NT)
        taps = sb("taps", 4 * 272)
        ksr = taps[:, :].rearrange("p (j n) -> p j n", j=4)
        uT_ = sb("uT_", 1024)
        uT = uT_[:, :].rearrange("p (a n) -> p a n", a=8)
        ct_ = sb("ct_", 1024)
        ct = ct_[:, :].rearrange("p (c j n) -> p c j n", c=2, j=4)
        wi_ = sb("wi_", 1024)
        wpow = wi_[:, 0:512].rearrange("p (c t g) -> p c t g", c=2, t=TC)
        ipow = wi_[:, 512:1024].rearrange("p (c t g) -> p c t g", c=2, t=TC)
        oT = wi_[:, :].rearrange("p (h l) -> p h l", h=HEADS)
        yT = ct_[:, :].rearrange("p (j l) -> p j l", j=4)
        osT = uT_[:, :].rearrange("p (j l) -> p j l", j=4)
        gains = sb("gains", 4 * KD)
        st = sb("st", 64)
        lamb = sb("lamb", 4 * DH)
        lam8 = sb("lam8", 2 * 2 * 2 * G)
        sm = sb("sm", 3 * NT * 4 + 8)
        idx = sb("idx", EXTRA + 1, dt=I32)

        pt = [ctx.enter_context(nc.psum_tensor(f"pt{i}", [P, 1024], F32)) for i in range(4)]
        PA, PB, PC, PD = range(4)

        taps_dram = nc.dram_tensor("taps_dram", [G, HG, 272], F32, kind="Internal").ap()

        s_con = sem("const_loaded"); s_x = sem("x_loaded"); s_gain = sem("gains_loaded"); s_small = sem("s5_small_loaded")
        s_braw = sem("b_loaded"); s_craw = sem("c_loaded"); s_lamb = sem("lambda_loaded"); s_mem = sem("mem_loaded")
        s_u4 = sem("u4_regrouped"); s_tapw = sem("taps_written"); s_toep = sem("toeplitz_loaded")
        s_rt = sem("router_loaded"); s_b1 = sem("expert_bias_loaded"); s_gf = sem("final_gain_loaded")
        s_out = sem("out_written"); s_dskip = sem("d_loaded")
        s_slot = [sem(f"slot{i}_loaded") for i in range(STAGE)]
        s_slab = sem("slabs_done")
        s_v = sem("dve_step"); s_a = sem("act_step"); s_p = sem("pool_step")
        names = """root epsv ssq u4r usb dtl mag red trig tabsrc tabp taba bspl vev utp uta ctp cta scp smx pex pwv wtp wta pvp on
            otp ota lamx laml bp s5wd k1p k1a k0p ktr kra kse ltp lta ltv zp zva zvv scan enta entv mka mva
            sgm bav yp ygel ytp yta gls osv bsv mh xqa xsp xmx xex xpn xtp xta xop xoa xh lgp lgv lex msk
            rkp rkv gdv gdp gda cup cuv ovp ovi b1p b1a acci gfin accd rope gates qkp qka sumsq normed tokp
            tokv""".split()
        S = {n: sem(n) for n in names}
        s_w1 = [sem(f"w1_chunk{k}_loaded") for k in range(KD)]
        s_w2 = [sem(f"w2_pair{k}_loaded") for k in range(KD // 2)]
        m_sel = sem("block_selected"); m_x = sem("block_gathered"); m_xev = sem("block_tokens_ready")
        m_w1u = sem("w1_chunks_consumed"); m_w2u = sem("w2_pairs_consumed"); m_st = sem("scatter_transposed")
        m_gs = sem("scatter_ready"); m_g2 = sem("gate_clamped"); m_sig = sem("gate_sigmoid"); m_act = sem("hidden_ready")
        m_yt = sem("yT_copied"); m_ytr = sem("y_turned"); m_y = sem("y_ready"); m_v = sem("block_dve_step")
        m_sc = sem("scattered")

        cols = {"u": ("w_in", 3 * WA), "q": ("w_in", 0), "k": ("w_in", WA), "v": ("w_in", 2 * WA)}
        SLABS = [(n, *cols[n], D) for n in "uqkv"]
        for n, w, c0, rows, count in (("ga", "w_in", 4 * WA, D, 2), ("gs", "w_in", 6 * WA, D, 2), ("mk", "w_xkv", 0, D, 2),
                                      ("mv", "w_xkv", D, D, 2), ("ba", "w_branch_attn", 0, WA, 2), ("gl", "w_glu", 0, WA, 2),
                                      ("bs", "w_branch_ssm", 0, WA, 2), ("mx", "w_mix_out", 0, D, 2),
                                      ("xq", "w_xq", 0, D, 2), ("xo", "w_xo", 0, D, 2)):
            SLABS += [(f"{n}{i}", w, c0 + WA * i, rows) for i in range(count)]
        SLAB_NO = {s[0]: i for i, s in enumerate(SLABS)}
        SLOT_USES = [(i, w, r, c) for i, (_, w, c, rows) in enumerate(SLABS) for r in range(0, rows, WA)]

        def slab_done(eng, name):
            eng.wait_ge(s_slab, SLAB_NO[name] + 1)

        w1_dram = T["w_e1"].rearrange("a e (k p) n -> (a e) k p n", p=P)
        w2_dram = T["w_e2"].rearrange("a e (k p) n -> (a e) p k n", p=P)

        def load_w1(eng, e, k):
            src = w1_dram[0, k] if e is None else w1_dram[bass.ds(e, 1), k].rearrange("a p n -> p (a n)")
            eng.dma_start(w1[:, k, :], src).then_inc(s_w1[k], 16)

        def load_w2(eng, e, kk):
            if e is None:
                src = w2_dram[0, :, 2 * kk:2 * kk + 2, :]
            else:
                src = w2_dram[bass.ds(e, 1), :, 2 * kk:2 * kk + 2, :].rearrange("a p k n -> p (a k) n")
            eng.dma_start(w2[:, 2 * kk:2 * kk + 2, :], src).then_inc(s_w2[kk], 16)

        block = ctx.enter_context(nc.Block())

        def part(a, n):
            return stage[:, a:a + n]
        xg = part(0, 8 * SLOTS).rearrange("p (k s) -> p k s", k=KD)
        sg1 = part(512, 512).rearrange("p (k s) -> p k s", k=KD)
        sg2 = part(1024, 512).rearrange("p (k s) -> p k s", k=KD)
        sl1 = part(1536, 512).rearrange("p (k s) -> p k s", k=KD)
        ssg = part(2048, 512).rearrange("p (k s) -> p k s", k=KD)
        hact = part(2560, 512).rearrange("p (k s) -> p k s", k=KD)
        sl2 = part(3072, 512).rearrange("p (k s) -> p k s", k=KD)
        ytb = part(3584, 512).rearrange("p (k s) -> p k s", k=KD)
        ysb = stage[0:SLOTS, 4096:5120]
        gsc = stage[0:SLOTS, 5120:5376]
        b1T = part(5376, 512).rearrange("p (m e) -> p m e", m=16)
        sel = part(5888, NT * SLOTS).rearrange("p (t s) -> p t s", t=NT)
        selw = part(6016, NT * SLOTS).rearrange("p (t s) -> p t s", t=NT)
        posn = part(6144, NT * NE).rearrange("p (t e) -> p t e", t=NT)
        gate = part(6208, NT * NE).rearrange("p (t e) -> p t e", t=NT)
        lg = part(6272, NT * NE).rearrange("p (t e) -> p t e", t=NT)
        msk = part(6336, NT * NE).rearrange("p (t e) -> p t e", t=NT)
        offs = part(6400, NE + EXTRA)
        pse = part(6464, 2 * NT).rearrange("p (a t) -> p a t", a=2)
        top8 = part(6472, NT * 8).rearrange("p (t e) -> p t e", t=NT)
        rep = part(6488, NT * NE).rearrange("p (t e) -> p t e", t=NT)
        ovf = part(6552, 2 * EXTRA + 1)
        gT = stage[0:NE, 6656:6656 + L]
        wr = uT_[:, 0:KD * NE].rearrange("p (k e) -> p k e", k=KD)
        nbx = part(7168, 2)[0:NE]
        blk = part(7176, 2 * EXTRA + 1)[0:NE]
        p2 = a1[:, :].rearrange("p (h t l) -> p h t l", h=HEADS, t=NT)
        p2T = t1[:, :].rearrange("p (h k l) -> p h k l", h=HEADS, k=NT)
        glu_flat = taps[:, 0:1024]
        b1T_flat = part(5376, 512)
        hnT_flat = hnt[:, :]
        gfin = t1[:, 0:D]
        be1 = t3[0:NE, 0:2048]
        be2 = t2[0:NE, 0:D]
        brt = t1[:, 1024:1024 + NE]

        @block.sync
        def _(sp):
            sp.dma_start(h3, T["x"].rearrange("a (t p) n -> p (a t) n", p=P)).then_inc(s_x, 16)
            sp.dma_start(con[:, :], T["consts"]).then_inc(s_con, 16)
            pre = [(load_w1, k) for k in range(KD)] + [(load_w2, k) for k in range(KD // 2)]
            for i, (slab, w, r, c) in enumerate(SLOT_USES):
                if i >= STAGE:
                    sp.wait_ge(s_slab, SLOT_USES[i - STAGE][0] + 1)
                src = T[w][0, r:r + WA, c:c + WA].rearrange("(k p) n -> p k n", p=P)
                sp.dma_start(slot[i % STAGE], src).then_inc(s_slot[i % STAGE], 16)
                if slab >= SLAB_NO["mx0"] and pre:
                    if len(pre) == KD + KD // 2:
                        sp.wait_ge(S["ytp"], 2)
                    load, k = pre.pop(0)
                    load(sp, None, k)
            for load, k in pre:
                load(sp, None, k)

            def refill(it, e):
                for k in range(KD):
                    sp.wait_ge(m_w1u, KD * (it - 1) + k + 1)
                    load_w1(sp, e, k)
                for kk in range(KD // 2):
                    sp.wait_ge(m_w2u, (KD // 2) * (it - 1) + kk + 1)
                    load_w2(sp, e, kk)

            with sp.Fori(1, NE) as e:
                refill(e, e)
            sp.wait_ge(S["ovi"], 1)
            n_extra = sp.value_load(idx[0:1, EXTRA:EXTRA + 1], min_val=0, max_val=EXTRA)
            with sp.Fori(0, EXTRA) as j:
                with sp.If(n_extra > j):
                    refill(NE + j, sp.value_load(idx[0:1, bass.ds(j, 1)], min_val=0, max_val=NE - 1))
            sp.wait_ge(S["gfin"], NT)
            sp.dma_start(out.rearrange("a (t p) n -> p (a t) n", p=P), h3).then_inc(s_out, 16)
            sp.wait_ge(s_out, 16)

        @block.gpsimd
        def _(pool):
            steps = [0]

            def link(ins):
                steps[0] += 1
                ins.then_inc(s_p, 1)
                pool.wait_ge(s_p, steps[0])

            for i, n in enumerate(("norm_mix_g", "norm_mem_g", "norm_cross_g", "norm_ffn_g")):
                pool.dma_start(gains[:, i * KD:(i + 1) * KD], T[n].rearrange("a (k p) -> p (a k)", p=P),
                               allow_slow_non_contiguous=True).then_inc(s_gain, 16)
            are = prep[:, 0:128].rearrange("p (d m) -> p d m", d=2)
            aim = prep[:, 128:256].rearrange("p (d m) -> p d m", d=2)
            ldt = prep[:, 256:258]
            pool.dma_start(are, T["ssm_a_re"].rearrange("a d g p -> g (a d) p")).then_inc(s_small, 16)
            pool.dma_start(aim, T["ssm_a_im"].rearrange("a d g p -> g (a d) p")).then_inc(s_small, 16)
            pool.dma_start(ldt, T["ssm_log_dt"].rearrange("a d g -> g (a d)"),
                           allow_slow_non_contiguous=True).then_inc(s_small, 16)
            for c, n in enumerate(("ssm_c_re", "ssm_c_im")):
                for d in range(2):
                    dst = craw[:, c, :, d * NS:(d + 1) * NS]
                    src = T[n][0, d].rearrange("(j a) h p -> (a h) j p", j=4)
                    pool.dma_start(dst, src).then_inc(s_craw, 16)
            for c, n in enumerate(("ssm_b_re", "ssm_b_im")):
                for d in range(2):
                    pool.dma_start(braw[d * NS:(d + 1) * NS, c], T[n][0, d].rearrange("g p h -> p g h")).then_inc(s_braw, 16)
            for i, n in enumerate(("lambda_q1", "lambda_k1", "lambda_q2", "lambda_k2")):
                pool.dma_start(lamb[:, i * DH:(i + 1) * DH], T[n].broadcast_to([P, DH])).then_inc(s_lamb, 16)
            pool.dma_start(st[:, 32:33], T["subln_g"].rearrange("a p -> p a"), allow_slow_non_contiguous=True).then_inc(s_dskip, 16)
            pool.dma_start(st[:, 36:40], T["ssm_d"].rearrange("a (j p) -> p (a j)", p=P),
                           allow_slow_non_contiguous=True).then_inc(s_dskip, 16)

            pool.wait_ge(S["taba"], 1)
            pool.wait_ge(S["cta"], 1)
            cr = ct[:, 0].rearrange("p j (a h) -> p (j a) h", h=HG)
            cn = ct[:, 1].rearrange("p j (a h) -> p (j a) h", h=HG)
            for t in range(TC):
                lr = wpow[:, 0, t, :].unsqueeze(2).to_broadcast([P, G, HG])
                li = wpow[:, 1, t, :].unsqueeze(2).to_broadcast([P, G, HG])
                link(pool.tensor_tensor(tmp_p, cr, lr, ALU.mult))
                link(pool.tensor_tensor(s5w[:, 0, :, t, :], cn, li, ALU.mult))
                link(pool.tensor_tensor(s5w[:, 0, :, t, :], tmp_p, s5w[:, 0, :, t, :], ALU.add))
                link(pool.tensor_tensor(tmp_p, cr, li, ALU.mult))
                link(pool.tensor_tensor(s5w[:, 1, :, t, :], cn, lr, ALU.mult))
                last = pool.tensor_tensor(s5w[:, 1, :, t, :], s5w[:, 1, :, t, :], tmp_p, ALU.subtract)
                if t < TC - 1:
                    link(last)
            last.then_inc(S["s5wd"], 1)

            pool.wait_ge(S["pvp"], HEADS)
            pool.dma_start(mn, T["mem"].rearrange("a (t p) n -> p (a t) n", p=P)).then_inc(s_mem, 16)
            pool.wait_ge(S["kse"], 1)
            pool.wait_ge(S["kra"], 1)
            for j in range(4):
                pool.dma_start(taps_dram[8 * j:8 * j + 8].rearrange("a h n -> (a h) n"), ksr[:, j, :]).then_inc(s_tapw, 16)
            pool.wait_ge(s_tapw, 64)
            for t in range(TC):
                pool.dma_start(toep[HG * t:HG * (t + 1)],
                               taps_dram[:, :, HG * (TC - t):HG * (TC - t) + P].rearrange("g h n -> h g n")).then_inc(s_toep, 16)
            slab_done(pool, "bs1")
            pool.dma_start(wr, T["w_router"].rearrange("a (k p) e -> p (a k) e", p=P)).then_inc(s_rt, 16)
            pool.wait_ge(S["xop"], 2)
            pool.dma_start(brt, T["b_router"].broadcast_to([P, NE])).then_inc(s_rt, 16)
            pool.dma_start(be1, T["b_e1"].rearrange("a e n -> (a e) n")).then_inc(s_b1, 16)
            pool.dma_start(be2, T["b_e2"].rearrange("a e n -> (a e) n")).then_inc(s_b1, 16)
            pool.dma_start(gfin, T["norm_final_g"].rearrange("(a n) -> a n", a=1).broadcast_to([P, D])).then_inc(s_gf, 16)

        @block.tensor
        def _(pe):
            readers = [[], [], [], []]
            slots_used = [0]

            def take(u, *who):
                for name, n in readers[u]:
                    pe.wait_ge(S[name], n)
                readers[u] = list(who)

            def turn(dst, src):
                n = src.shape[0]
                return pe.transpose(dst, src, ident[0:n, 0:n])

            def weights(slab):
                got = []
                while slots_used[0] < len(SLOT_USES) and SLOT_USES[slots_used[0]][0] == SLAB_NO[slab]:
                    i = slots_used[0]
                    pe.wait_ge(s_slot[i % STAGE], 16 * (i // STAGE + 1))
                    got.append(slot[i % STAGE])
                    slots_used[0] += 1
                return got

            def natural(slab, u, xT, *who):
                ws = weights(slab)
                take(u, *who)
                for t in range(NT):
                    for k in range(4 * len(ws)):
                        last = pe.matmul(pt[u][:, 512 * t:512 * t + 512], xT[:, k, t * P:(t + 1) * P],
                                         ws[k // 4][:, k % 4, :], start=(k == 0), stop=(k == 4 * len(ws) - 1))
                last.then_inc(s_slab, 1)

            def flipped(slab, u, xT, *who):
                ws = weights(slab)
                take(u, *who)
                for m in range(4):
                    for k in range(4 * len(ws)):
                        last = pe.matmul(pt[u][:, L * m:L * m + L], ws[k // 4][:, k % 4, m * P:(m + 1) * P], xT[:, k, :],
                                         start=(k == 0), stop=(k == 4 * len(ws) - 1))
                last.then_inc(s_slab, 1)

            def turn_tokens(src, units, norm):
                pe.wait_ge(S["normed"], NT * (norm + 1))
                for i, u in enumerate(units):
                    take(u, ("tokv", 2 * norm + i + 1))
                    for k in range(4):
                        for t in range(NT):
                            last = turn(pt[u][:, L * k + P * t:L * k + P * (t + 1)],
                                        src[:, t, P * (4 * i + k):P * (4 * i + k + 1)])
                    last.then_inc(S["tokp"], 1)

            pe.wait_ge(s_con, 16)
            turn_tokens(xn, (PC, PD), 0)
            pe.wait_ge(S["tokv"], 2)
            natural("u", PA, hnT, ("usb", 1))

            pe.wait_ge(S["tabsrc"], 1)
            take(PC, ("taba", 1))
            for c in range(2):
                for t in range(TC):
                    turn(pt[PC][:, (c * TC + t) * G:(c * TC + t + 1) * G], pw[:, c, t, :])
            for c in range(2):
                last = turn(pt[PC][:, 512 + c * G:512 + (c + 1) * G], prep[:, 4096 + c * P:4096 + (c + 1) * P])
            last.then_inc(S["tabp"], 1)
            pe.wait_ge(s_craw, 64)
            take(PD, ("cta", 1))
            for c in range(2):
                for j in range(4):
                    last = turn(pt[PD][:, (4 * c + j) * P:(4 * c + j + 1) * P], craw[:, c, j, :])
            last.then_inc(S["ctp"], 1)

            natural("q", PB, hnT, ("rope", 1))
            natural("k", PA, hnT, ("rope", 2))
            natural("v", PB, hnT, ("vev", 1))

            pe.wait_ge(S["u4r"], 1)
            take(PC, ("uta", 1))
            for a in range(8):
                last = turn(pt[PC][:, P * a:P * (a + 1)], u5[:, a])
            last.then_inc(S["utp"], 1)
            flipped("ga0", PA, hnT, ("gates", 1))

            for n, src, u in ((1, qn, PD), (2, kn, PC)):
                pe.wait_ge(S["rope"], n)
                take(u, ("qka", n))
                for h in range(HEADS):
                    for t in range(NT):
                        last = turn(pt[u][:, L * h + P * t:L * h + P * (t + 1)], src[:, t, P * h:P * (h + 1)])
                last.then_inc(S["qkp"], 1)

            def scores(h):
                take(PD, ("smx", h + 1), ("pex", 4 * (h + 1)))
                for t in range(NT):
                    for c in range(2):
                        last = pe.matmul(pt[PD][:, 512 * c + L * t:512 * c + L * (t + 1)],
                                         qT[DH * c:DH * (c + 1), h, P * t:P * (t + 1)], kT[DH * c:DH * (c + 1), h, :],
                                         start=True, stop=True)
                last.then_inc(S["scp"], 1)

            def turn_probs(h):
                pe.wait_ge(S["pwv"], h + 1)
                take(PC, ("wta", h + 1))
                for k in range(NT):
                    for t in range(NT):
                        last = turn(pt[PC][:, L * k + P * t:L * k + P * (t + 1)], prob[:, 0, t, P * k:P * (k + 1)])
                last.then_inc(S["wtp"], 1)

            def values(h):
                pe.wait_ge(S["wta"], h + 1)
                if h == 0:
                    take(PA, ("on", 1))
                for t in range(NT):
                    for k in range(NT):
                        last = pe.matmul(pt[PA][:, 512 * t + P * h:512 * t + P * (h + 1)], wT[:, h % 2, k, P * t:P * (t + 1)],
                                         vn[:, k, P * h:P * (h + 1)], start=(k == 0), stop=(k == NT - 1))
                last.then_inc(S["pvp"], 1)

            pe.wait_ge(S["qka"], 2)
            pe.wait_ge(S["vev"], 1)
            scores(0)
            flipped("ga1", PB, hnT, ("gates", 2))
            turn_probs(0)
            scores(1)
            flipped("gs0", PB, hnT, ("gates", 3))
            values(0)
            turn_probs(1)
            scores(2)
            flipped("gs1", PB, hnT, ("gates", 4))
            values(1)
            turn_probs(2)
            scores(3)

            pe.wait_ge(S["s5wd"], 1)
            pe.wait_ge(S["bspl"], 1)
            take(PB, ("k1a", 1))
            for g in range(G):
                for c in range(2):
                    last = pe.matmul(pt[PB][:, 2 * HG * g:2 * HG * (g + 1)], s5w[:, c, g], bsplit[:, c, g],
                                     start=(c == 0), stop=(c == 1))
            last.then_inc(S["k1p"], 1)
            values(2)
            turn_probs(3)

            pe.wait_ge(S["bp"], 1)
            for r in range(8):
                u, read = ((PB, "lta"), (PD, "ltv"))[r % 2]
                take(u, (read, r // 2 + 1))
                for i in range(8):
                    last = turn(pt[u][:, P * i:P * (i + 1)], s5b[:, 4 * r + i // 2, i % 2])
                last.then_inc(S["ltp"], 1)
            values(3)

            take(PC, ("kse", 1))
            for j in range(4):
                for c in range(2):
                    last = pe.matmul(pt[PC][:, P * j:P * (j + 1)], bbar[:, c, 8 * j:8 * j + 8], ct[:, c, j],
                                     start=(c == 0), stop=(c == 1))
            last.then_inc(S["k0p"], 1)

            pe.wait_ge(S["lta"], 4)
            pe.wait_ge(S["ltv"], 4)
            for c, u in enumerate((PB, PD)):
                take(u, ("zva", c + 1), ("zvv", c + 1))
                for g in range(G):
                    last = pe.matmul(pt[u][:, NC * g:NC * (g + 1)], lin[:, g, c], uT[:, g % 8, NC * (g // 8):NC * (g // 8 + 1)],
                                     start=True, stop=True)
                last.then_inc(S["zp"], 1)

            pe.wait_ge(S["k1a"], 1)
            take(PA, ("kra", 1))
            for d in range(2):
                for j in range(4):
                    last = turn(pt[PA][:, P * (4 * d + j):P * (4 * d + j + 1)], taps_t[:, d, 8 * j:8 * j + 8])
            last.then_inc(S["ktr"], 1)

            pe.wait_ge(S["on"], 2)
            take(PC, ("ota", 1))
            for h in range(HEADS):
                for t in range(NT):
                    last = turn(pt[PC][:, L * h + P * t:L * h + P * (t + 1)], on[:, t, h])
            last.then_inc(S["otp"], 1)

            turn_tokens(mn, (PA, PB), 1)
            pe.wait_ge(S["tokv"], 4)
            flipped("mk0", PC, memT, ("mka", 1))
            flipped("mk1", PD, memT, ("mka", 2))
            natural("mv0", PA, memT, ("mva", 1))
            natural("mv1", PB, memT, ("mva", 2))
            pe.wait_ge(S["ota"], 1)
            flipped("ba0", PC, oT, ("bav", 1))
            flipped("ba1", PD, oT, ("bav", 2))

            pe.wait_ge(s_toep, TC * 16)
            pe.wait_ge(S["enta"], 2)
            pe.wait_ge(S["entv"], 1)
            take(PA, ("ygel", 1))
            for g in range(G):
                a, j = g % 8, g // 8
                dst = pt[PA][:, P * a + NC * j:P * a + NC * (j + 1)]
                pe.matmul(dst, toep[:, g], uT[:, a, NC * j:NC * (j + 1)], start=True, stop=False)
                pe.matmul(dst, s5w[:, 0, g], enter[:, 0, g], start=False, stop=False)
                last = pe.matmul(dst, s5w[:, 1, g], enter[:, 1, g], start=False, stop=True)
            last.then_inc(S["yp"], 1)
            pe.wait_ge(S["ygel"], 1)
            take(PB, ("yta", 1))
            for a in range(8):
                last = turn(pt[PB][:, P * a:P * (a + 1)], yg[:, a])
            last.then_inc(S["ytp"], 1)
            pe.wait_ge(S["yta"], 1)
            take(PA, ("yta", 2))
            for t in range(TC):
                last = turn(pt[PA][:, P * t:P * (t + 1)], y4[:, t])
            last.then_inc(S["ytp"], 1)
            pe.wait_ge(S["yta"], 2)
            flipped("gl0", PC, yT, ("osv", 1))
            flipped("gl1", PD, yT, ("gls", 1))
            pe.wait_ge(S["osv"], 1)
            flipped("bs0", PA, osT, ("bsv", 2))
            flipped("bs1", PB, osT, ("bsv", 4))
            pe.wait_ge(S["bsv"], 4)
            natural("mx0", PC, gaT, ("mh", 1))
            natural("mx1", PD, gaT, ("mh", 2))

            turn_tokens(xn, (PA, PB), 2)
            pe.wait_ge(S["tokv"], 6)
            flipped("xq0", PC, hnT, ("xqa", 1))
            flipped("xq1", PD, hnT, ("xqa", 2))
            pe.wait_ge(S["mka"], 2)
            for i, u in enumerate((PA, PB)):
                pe.wait_ge(S["xqa"], i + 1)
                take(u, ("xmx", i + 1), ("xex", 4 * (i + 1)))
                for hh in range(2):
                    for t in range(NT):
                        for m in range(2):
                            k = 4 * i + 2 * hh + m
                            last = pe.matmul(pt[u][:, 512 * hh + L * t:512 * hh + L * (t + 1)], gsT[:, k, P * t:P * (t + 1)],
                                             mkT[:, k, :], start=(m == 0), stop=(m == 1))
                last.then_inc(S["xsp"], 1)
            for i, u in enumerate((PC, PD)):
                pe.wait_ge(S["xpn"], i + 1)
                take(u, ("xta", i + 1))
                for hh in range(2):
                    for k in range(NT):
                        for t in range(NT):
                            last = turn(pt[u][:, 512 * hh + L * k + P * t:512 * hh + L * k + P * (t + 1)],
                                        p2[:, 2 * i + hh, t, P * k:P * (k + 1)])
                last.then_inc(S["xtp"], 1)
            pe.wait_ge(S["mva"], 2)
            for i, u in enumerate((PA, PB)):
                pe.wait_ge(S["xta"], i + 1)
                take(u, ("xoa", i + 1))
                for hh in range(2):
                    h = 2 * i + hh
                    for m in range(2):
                        for k in range(NT):
                            last = pe.matmul(pt[u][:, 512 * hh + L * m:512 * hh + L * (m + 1)],
                                             mn[:, k, L * h + P * m:L * h + P * (m + 1)], p2T[:, h, k],
                                             start=(k == 0), stop=(k == NT - 1))
                last.then_inc(S["xop"], 1)
            pe.wait_ge(S["xoa"], 2)
            natural("xo0", PC, hnT, ("xh", 1))
            natural("xo1", PD, hnT, ("xh", 2))

            turn_tokens(xn, (PA, PB), 3)
            pe.wait_ge(S["tokv"], 8)
            pe.wait_ge(s_rt, 32)
            take(PD, ("lgv", 1))
            for t in range(NT):
                for k in range(KD):
                    last = pe.matmul(pt[PD][:, NE * t:NE * (t + 1)], hnT[:, k, P * t:P * (t + 1)], wr[:, k, :],
                                     start=(k == 0), stop=(k == KD - 1))
            last.then_inc(S["lgp"], 1)
            pe.wait_ge(s_b1, 32)
            take(PC, ("b1a", 1))
            for m in range(16):
                last = turn(pt[PC][:, NE * m:NE * (m + 1)], be1[:, P * m:P * (m + 1)])
            last.then_inc(S["b1p"], 1)
            pe.wait_ge(S["msk"], NT)
            take(PD, ("rkv", 1))
            up = con[:, C_UP:C_UP + P]
            pe.matmul(pt[PD][:, 0:NE], up, msk[:, 0, :], start=True, stop=True)
            pe.matmul(pt[PD][:, NE:2 * NE], ones, msk[:, 0, :], start=True, stop=False)
            pe.matmul(pt[PD][:, NE:2 * NE], up, msk[:, 1, :], start=False, stop=True)
            for t in range(NT):
                last = pe.matmul(pt[PD][0:NE, 512:513], msk[:, t, :], ones[:, 0:1], start=(t == 0), stop=(t == NT - 1))
            last.then_inc(S["rkp"], 1)
            pe.wait_ge(S["gdv"], NT)
            pe.wait_ge(S["b1a"], 1)
            for t in range(NT):
                last = turn(pt[PC][0:NE, P * t:P * (t + 1)], gate[:, t, :])
            last.then_inc(S["gdp"], 1)
            readers[PC] = [("gda", 1)]
            pe.wait_ge(S["rkv"], 1)
            pe.matmul(pt[PD][0:NE, 0:1], con[0:NE, C_TRI:C_TRI + NE], nbx[:, 0:1], start=True, stop=True).then_inc(S["cup"], 1)
            pe.wait_ge(S["cuv"], 1)
            pe.matmul(pt[PD][:, 512:512 + 2 * EXTRA + 1], ones[0:NE, :], blk[:, :], start=True, stop=True).then_inc(S["ovp"], 1)
            take(PA)
            take(PB)
            pe.wait_ge(S["gda"], 1)
            for t in range(NT):
                for n in range(2):
                    acc = pt[(PA, PB)[t]][:, 512 * n:512 * (n + 1)]
                    pe.matmul(acc, ident, h3[:, t, 512 * n:512 * (n + 1)], start=True, stop=False)
                    last = pe.matmul(acc, gT[:, P * t:P * (t + 1)], be2[:, 512 * n:512 * (n + 1)], start=False, stop=False)
            last.then_inc(S["acci"], 1)
            take(PC)
            take(PD)
            pe.wait_ge(S["ovi"], 1)

            def scatter(stop):
                for t in range(NT):
                    for n in range(2):
                        last = pe.matmul(pt[(PA, PB)[t]][:, 512 * n:512 * (n + 1)], gsc[:, P * t:P * (t + 1)],
                                         ysb[:, 512 * n:512 * (n + 1)], start=False, stop=stop)
                return last

            def block_of(it):
                pe.wait_ge(m_sel, it + 1)
                pe.wait_ge(m_xev, it)
                for k in range(KD):
                    for t in range(NT):
                        last = pe.matmul(pt[PD][:, SLOTS * k:SLOTS * (k + 1)], xn[:, t, P * k:P * (k + 1)], sel[:, t, :],
                                         start=(t == 0), stop=(t == NT - 1))
                last.then_inc(m_x, 1)
                pe.wait_ge(m_xev, it + 1)
                pe.wait_ge(m_y, it)
                for k in range(KD):
                    pe.wait_ge(s_w1[k], 16 * (it + 1))
                    for m in range(16):
                        last = pe.matmul(pt[PC][:, 512 * (m // 8) + SLOTS * (m % 8):512 * (m // 8) + SLOTS * (m % 8 + 1)],
                                         w1[:, k, P * m:P * (m + 1)], xg[:, k, :], start=(k == 0 and m % 8 == 0),
                                         stop=(k == KD - 1 and m % 8 == 7))
                    last.then_inc(m_w1u, 1)
                pe.wait_ge(m_yt, it)
                pe.wait_ge(m_gs, it + 1)
                scatter(False).then_inc(m_sc, 1)
                for t in range(NT):
                    last = turn(pt[PD][0:SLOTS, 512 + P * t:512 + P * (t + 1)], selw[:, t, :])
                last.then_inc(m_st, 1)
                pe.wait_ge(m_act, it + 1)
                pe.wait_ge(m_gs, it + 2)
                for k in range(KD):
                    if k % 2 == 0:
                        pe.wait_ge(s_w2[k // 2], 16 * (it + 1))
                    for m in range(8):
                        last = pe.matmul(pt[PD][:, 512 + SLOTS * m:512 + SLOTS * (m + 1)], w2[:, k, P * m:P * (m + 1)],
                                         hact[:, k, :], start=(k == 0 and m == 0), stop=(k == KD - 1 and m == 7))
                    if k % 2:
                        last.then_inc(m_w2u, 1)
                pe.wait_ge(S["acci"], 1)
                pe.wait_ge(m_yt, it + 1)
                for m in range(KD):
                    last = turn(pt[PC][0:SLOTS, P * m:P * (m + 1)], ytb[:, m, :])
                last.then_inc(m_ytr, 1)

            with pe.Fori(0, NE) as e:
                block_of(e)
            n_extra = pe.value_load(idx[0:1, EXTRA:EXTRA + 1], min_val=0, max_val=EXTRA)
            with pe.Fori(0, EXTRA) as j:
                with pe.If(n_extra > j):
                    block_of(NE + j)
            pe.wait_ge(m_y, NE + n_extra)
            scatter(True).then_inc(S["accd"], 1)

        @block.scalar
        def _(act):
            def square(src, scratch, col):
                act.activation(scratch, src, ACT.Square, accum_out=st[:, col:col + 1]).then_inc(S["sumsq"], 1)

            def root(src, dst, n, width, count=None):
                if count is not None:
                    act.wait_ge(S["sumsq"], count)
                act.activation(st[:, dst:dst + n], st[:, src:src + n], ACT.Sqrt, scale=1.0 / width,
                               bias=st[:, 60:61]).then_inc(S["root"], 1)

            def copy(dst, src):
                return act.activation(dst, src, ACT.Copy)

            def unit(u, pat=None, **kw):
                return pt[u][:, :] if pat is None else pt[u][:, :].rearrange(pat, **kw)

            act.wait_ge(s_x, 16)
            for t in range(NT):
                square(h3[:, t], hnT_flat[:, t * D:(t + 1) * D], t)
            act.wait_ge(S["epsv"], 1)
            root(0, 2, NT, D, NT)
            act.wait_ge(s_small, 48)
            act.activation(prep[:, 258:260], prep[:, 256:258], ACT.Exp).then_inc(S["dtl"], 1)
            act.wait_ge(S["lamx"], 1)
            act.activation(st[:, 43:45], st[:, 41:43], ACT.Exp).then_inc(S["laml"], 1)
            act.wait_ge(S["mag"], 1)
            act.activation(prep[:, 640:768], prep[:, 384:512], ACT.Exp)
            act.wait_ge(S["red"], 1)
            act.activation(prep[:, 1024:1152], prep[:, 896:1024], ACT.Sin)
            act.activation(prep[:, 1280:1408], prep[:, 1152:1280], ACT.Sin).then_inc(S["trig"], 1)

            slab_done(act, "u")
            copy(usb, unit(PA, "p (t n) -> p t n", t=NT)).then_inc(S["usb"], 1)
            act.wait_ge(S["usb"], 1)
            for t in range(NT):
                for j in range(4):
                    act.dma_start(u4[32 * j + 16 * t:32 * j + 16 * t + 16], usb[:, t, P * j:P * (j + 1)]).then_inc(s_u4, 16)
            act.wait_ge(S["tabp"], 1)
            copy(wi_[:, 0:512], pt[PC][:, 0:512])
            copy(lam8[:, 0:2 * G], pt[PC][:, 512:512 + 2 * G]).then_inc(S["taba"], 1)
            act.wait_ge(S["ctp"], 1)
            copy(ct_[:, 0:512], pt[PD][:, 0:512])
            act.activation(ct_[:, 512:1024], pt[PD][:, 512:1024], ACT.Copy, scale=-1.0).then_inc(S["cta"], 1)
            act.wait_ge(s_u4, 8 * 16)
            copy(u5, u4.rearrange("p t (a h) -> p a t h", a=8)).then_inc(S["u4r"], 1)
            slab_done(act, "v")
            copy(vn, unit(PB, "p (t n) -> p t n", t=NT)).then_inc(S["vev"], 1)
            act.wait_ge(S["utp"], 1)
            copy(uT_[:, :], unit(PC)).then_inc(S["uta"], 1)
            slab_done(act, "ga0")
            act.wait_ge(S["tabp"], 1)
            copy(a1[:, 0:1024], unit(PA)).then_inc(S["gates"], 1)
            act.wait_ge(S["qkp"], 1)
            copy(t2[:, 1024:2048], unit(PD)).then_inc(S["qka"], 1)
            act.wait_ge(S["qkp"], 2)
            copy(t3[:, 0:1024], unit(PC)).then_inc(S["qka"], 1)

            def exps(h):
                act.wait_ge(S["smx"], h + 1)
                if h:
                    act.wait_ge(S["wtp"], h)
                for c in range(2):
                    for t in range(NT):
                        i = 2 * c + t
                        act.activation(prob[:, c, t], pt[PD][:, 512 * c + L * t:512 * c + L * (t + 1)], ACT.Exp,
                                       bias=sm[:, i:i + 1], scale=DH ** -0.5, accum_out=sm[:, 8 + i:9 + i]).then_inc(S["pex"], 1)

            def copy_probs(h):
                act.wait_ge(S["wtp"], h + 1)
                if h >= 2:
                    act.wait_ge(S["pvp"], h - 1)
                copy(wT[:, h % 2], pt[PC][:, 0:512].rearrange("p (k l) -> p k l", k=NT)).then_inc(S["wta"], 1)

            exps(0)
            slab_done(act, "ga1")
            copy(a1[:, 1024:2048], unit(PB)).then_inc(S["gates"], 1)
            copy_probs(0)
            exps(1)
            slab_done(act, "gs0")
            copy(a2[:, 0:1024], unit(PB)).then_inc(S["gates"], 1)
            copy_probs(1)
            exps(2)
            slab_done(act, "gs1")
            copy(a2[:, 1024:2048], unit(PB)).then_inc(S["gates"], 1)
            copy_probs(2)
            exps(3)
            act.wait_ge(S["k1p"], 1)
            act.wait_ge(S["bp"], 1)
            for d in range(2):
                last = copy(taps_t[:, d], unit(PB, "p (g d h) -> p d g h", g=G, d=2)[:, d])
            last.then_inc(S["k1a"], 1)
            copy_probs(3)
            for r in range(0, 8, 2):
                act.wait_ge(S["ltp"], r + 1)
                copy(ring[:, 8192 + 1024 * r:8192 + 1024 * (r + 1)], unit(PB)).then_inc(S["lta"], 1)
            act.wait_ge(S["ssq"], 1)
            root(20, 46, 8, 2 * DH)
            for c, u in enumerate((PB, PD)):
                act.wait_ge(S["zp"], c + 1)
                if c == 0:
                    act.wait_ge(S["k1p"], 1)
                copy(zst[0:NS, :, c, :], pt[u][0:NS, :].rearrange("p (g k) -> p k g", g=G)).then_inc(S["zva"], 1)
            act.wait_ge(S["ktr"], 1)
            copy(ksr[:, :, 144:272], pt[PA][:, 512:1024].rearrange("p (j n) -> p j n", j=4))
            copy(ksr[:, :, 0:128], pt[PA][:, 0:512].rearrange("p (j n) -> p j n", j=4)).then_inc(S["kra"], 1)
            act.wait_ge(S["otp"], 1)
            act.activation(wi_[:, :], unit(PC), ACT.Copy, scale=st[:, 33:34]).then_inc(S["ota"], 1)
            act.wait_ge(s_mem, 16)
            for t in range(NT):
                square(mn[:, t], t2[:, t * D:(t + 1) * D], 4 + t)
            root(4, 6, NT, D, 2 * NT)
            act.activation(a1[:, :], a1[:, :], ACT.Sigmoid)
            act.activation(a2[:, :], a2[:, :], ACT.Sigmoid).then_inc(S["sgm"], 1)
            for i, u in enumerate((PC, PD)):
                slab_done(act, f"mk{i}")
                copy(t2[:, 1024 * i:1024 * (i + 1)], unit(u)).then_inc(S["mka"], 1)
            for i, u in enumerate((PA, PB)):
                slab_done(act, f"mv{i}")
                copy(mn[:, :, 512 * i:512 * (i + 1)], unit(u, "p (t n) -> p t n", t=NT)).then_inc(S["mva"], 1)
            act.wait_ge(S["scan"], 1)
            for c in range(2):
                copy(enter[0:NS, c, :, 1:NC], xst[0:NS, 0:NC - 1, c, :].rearrange("p k g -> p g k")).then_inc(S["enta"], 1)
            act.wait_ge(S["yp"], 1)
            act.activation(yg, unit(PA, "p (a n) -> p a n", a=8), ACT.Gelu_apprx_tanh).then_inc(S["ygel"], 1)
            act.wait_ge(S["ytp"], 1)
            copy(y4, unit(PB, "p (a t h) -> p t a h", a=8, t=TC)).then_inc(S["yta"], 1)
            act.wait_ge(S["ytp"], 2)
            for j in range(4):
                last = copy(yT[:, j].rearrange("p (k t) -> p t k", t=TC),
                            unit(PA, "p (t j k) -> p j t k", t=TC, j=4)[:, j])
            last.then_inc(S["yta"], 1)
            slab_done(act, "gl1")
            act.activation(glu_flat, unit(PD), ACT.Sigmoid).then_inc(S["gls"], 1)
            act.wait_ge(S["mh"], 2)
            for t in range(NT):
                square(h3[:, t], hnT_flat[:, t * D:(t + 1) * D], 8 + t)
            root(8, 10, NT, D, 3 * NT)
            for i, u in enumerate((PC, PD)):
                slab_done(act, f"xq{i}")
                copy(a2[:, 1024 * i:1024 * (i + 1)], unit(u)).then_inc(S["xqa"], 1)
            for i, u in enumerate((PA, PB)):
                act.wait_ge(S["xmx"], i + 1)
                for hh in range(2):
                    for t in range(NT):
                        n = 2 * hh + t
                        act.activation(p2[:, 2 * i + hh, t], pt[u][:, 512 * hh + L * t:512 * hh + L * (t + 1)], ACT.Exp,
                                       bias=sm[:, 4 * i + n:4 * i + n + 1], scale=(D // HEADS) ** -0.5,
                                       accum_out=sm[:, 8 + 4 * i + n:9 + 4 * i + n]).then_inc(S["xex"], 1)
            for i, u in enumerate((PC, PD)):
                act.wait_ge(S["xtp"], i + 1)
                copy(t1[:, 1024 * i:1024 * (i + 1)], unit(u)).then_inc(S["xta"], 1)
            for i, u in enumerate((PA, PB)):
                act.wait_ge(S["xop"], i + 1)
                copy(hnt[:, 1024 * i:1024 * (i + 1)], unit(u)).then_inc(S["xoa"], 1)
            act.wait_ge(S["xh"], 2)
            for t in range(NT):
                square(h3[:, t], a1[:, 0:D], 12 + t)
                act.wait_ge(S["sumsq"], 3 * NT + t + 1)
            root(12, 14, NT, D)
            act.wait_ge(S["b1p"], 1)
            copy(b1T_flat, pt[PC][:, 0:512]).then_inc(S["b1a"], 1)
            for t in range(NT):
                act.wait_ge(S["msk"], t + 1)
                act.activation(gate[:, t, :], lg[:, t, :], ACT.Exp, bias=pse[:, 0, t:t + 1]).then_inc(S["lex"], 1)
            act.wait_ge(S["gdp"], 1)
            copy(gT, pt[PC][0:NE, 0:L]).then_inc(S["gda"], 1)
            act.wait_ge(S["ovi"], 1)
            act.activation(ysb, con[0:SLOTS, 0:1].to_broadcast([SLOTS, D]), ACT.Copy, scale=0.0)
            act.activation(gsc, con[0:SLOTS, 0:1].to_broadcast([SLOTS, L]), ACT.Copy, scale=0.0).then_inc(m_gs, 1)

            def block_of(it):
                act.wait_ge(m_st, it + 1)
                copy(gsc, pt[PD][0:SLOTS, 512:512 + L]).then_inc(m_gs, 1)
                act.wait_ge(m_g2, it + 1)
                act.activation(ssg, sg2, ACT.Sigmoid, scale=GATE_ALPHA).then_inc(m_sig, 1)
                act.wait_ge(m_w2u, (KD // 2) * (it + 1))
                copy(ytb, pt[PD][:, 512:1024].rearrange("p (k s) -> p k s", k=KD)).then_inc(m_yt, 1)
                act.wait_ge(m_ytr, it + 1)
                copy(ysb, pt[PC][0:SLOTS, :]).then_inc(m_y, 1)

            with act.Fori(0, NE) as e:
                block_of(e)
            n_extra = act.value_load(idx[0:1, EXTRA:EXTRA + 1], min_val=0, max_val=EXTRA)
            with act.Fori(0, EXTRA) as j:
                with act.If(n_extra > j):
                    block_of(NE + j)
            act.wait_ge(S["accd"], 1)
            for t in range(NT):
                square(pt[(PA, PB)[t]][:, :], a1[:, 0:D], 16 + t)
                act.wait_ge(S["sumsq"], 4 * NT + t + 1)
            root(16, 18, NT, D)

        @block.vector
        def _(dve):
            steps = [0]

            def link(ins):
                steps[0] += 1
                ins.then_inc(s_v, 1)
                dve.wait_ge(s_v, steps[0])

            def bc(x, shape):
                return x.to_broadcast(shape)

            def normed(norm, src, dst):
                col = 4 * norm
                dve.wait_ge(S["root"], (1, 3, 4, 5)[norm])
                link(dve.reciprocal(st[:, col + 2:col + 2 + NT], st[:, col + 2:col + 2 + NT]))
                for t in range(NT):
                    dve.tensor_scalar(dst[:, t], src[:, t], st[:, col + 2 + t:col + 3 + t], None, ALU.mult).then_inc(S["normed"], 1)

            def gained(norm, units, dst):
                for i, u in enumerate(units):
                    dve.wait_ge(S["tokp"], 2 * norm + i + 1)
                    g = gains[:, norm * KD + 4 * i:norm * KD + 4 * i + 4].unsqueeze(2).to_broadcast([P, 4, L])
                    dve.tensor_tensor(dst[:, 4 * i:4 * i + 4], pt[u][:, :].rearrange("p (k l) -> p k l", k=4), g,
                                      ALU.mult).then_inc(S["tokv"], 1)

            dve.memset(st[:, 60:61], EPS).then_inc(S["epsv"], 1)
            normed(0, h3, xn)
            dve.wait_ge(s_gain, 64)
            gained(0, (PC, PD), hnT)

            dve.wait_ge(s_lamb, 64)
            for i in range(2):
                last = dve.tensor_tensor_reduce(lamb[:, 2 * i * DH:(2 * i + 1) * DH], lamb[:, 2 * i * DH:(2 * i + 1) * DH],
                                                lamb[:, (2 * i + 1) * DH:(2 * i + 2) * DH], 1.0, 0.0, ALU.mult, ALU.add,
                                                st[:, 41 + i:42 + i])
            last.then_inc(S["lamx"], 1)

            are, aim, dt = prep[:, 0:128], prep[:, 128:256], prep[:, 258:260]
            ad, th, mag, kk, red, sn, ab, cs = (prep[:, 384 + 128 * i:512 + 128 * i] for i in range(8))
            d2 = lambda x: x.rearrange("p (d m) -> p d m", d=2)
            dve.wait_ge(s_small, 48)
            dve.wait_ge(S["dtl"], 1)
            dtb = dt.unsqueeze(2).to_broadcast([G, 2, NS])
            dve.tensor_tensor(d2(ad), d2(are), dtb, ALU.mult).then_inc(S["mag"], 1)
            link(dve.tensor_tensor(d2(th), d2(aim), dtb, ALU.mult))
            link(dve.tensor_scalar(kk, th, 1.0 / TWO_PI, ROUND, ALU.mult, ALU.add))
            link(dve.tensor_scalar(kk, kk, ROUND, None, ALU.subtract))
            link(dve.scalar_tensor_tensor(red, kk, -PI_A, th, ALU.mult, ALU.add))
            link(dve.scalar_tensor_tensor(red, kk, -PI_B, red, ALU.mult, ALU.add))
            link(dve.scalar_tensor_tensor(red, kk, -PI_C, red, ALU.mult, ALU.add))
            link(dve.tensor_scalar(red, red, 3.1415925, -3.1415925, ALU.min, ALU.max))
            link(dve.scalar_tensor_tensor(ab, red, -1.0, red, ALU.mult, ALU.min))
            dve.tensor_scalar(ab, ab, TWO_PI / 4, None, ALU.add).then_inc(S["red"], 1)
            dve.wait_ge(S["trig"], 1)
            pwn = prep[:, 2048:4096].rearrange("p (c t m) -> p c t m", c=2, t=TC)
            link(dve.tensor_tensor(pwn[:, 0, 0], mag, cs, ALU.mult))
            link(dve.tensor_tensor(pwn[:, 1, 0], mag, sn, ALU.mult))

            def powers(a, b, n):
                tm = prep[:, 4608:4608 + n * P].rearrange("p (t m) -> p t m", t=n)
                pr, pi = (pwn[:, c, b - 1:b].to_broadcast([G, n, P]) for c in range(2))
                xr, xi = pwn[:, 0, 0:n], pwn[:, 1, 0:n]
                zr, zi = pwn[:, 0, a:a + n], pwn[:, 1, a:a + n]
                link(dve.tensor_tensor(tm, xr, pr, ALU.mult))
                link(dve.tensor_tensor(zr, xi, pi, ALU.mult))
                link(dve.tensor_tensor(zr, tm, zr, ALU.subtract))
                link(dve.tensor_tensor(tm, xr, pi, ALU.mult))
                link(dve.tensor_tensor(zi, xi, pr, ALU.mult))
                link(dve.tensor_tensor(zi, tm, zi, ALU.add))

            powers(1, 1, 1)
            powers(2, 2, 2)
            powers(4, 4, 4)
            nr, den, t0 = prep[:, 5632:5760], prep[:, 5760:5888], prep[:, 5888:6016]
            cf = prep[:, 4096:4352].rearrange("p (c m) -> p c m", c=2)
            link(dve.tensor_scalar(nr, pwn[:, 0, 0], 1.0, None, ALU.subtract))
            link(dve.tensor_tensor(den, are, are, ALU.mult))
            link(dve.tensor_tensor(t0, aim, aim, ALU.mult))
            link(dve.tensor_tensor(den, den, t0, ALU.add))
            link(dve.reciprocal(den, den))
            for c, (x, y, op) in enumerate(((nr, pwn[:, 1, 0], ALU.add), (pwn[:, 1, 0], nr, ALU.subtract))):
                link(dve.tensor_tensor(cf[:, c], x, are, ALU.mult))
                link(dve.tensor_tensor(t0, y, aim, ALU.mult))
                link(dve.tensor_tensor(cf[:, c], cf[:, c], t0, op))
                link(dve.tensor_tensor(cf[:, c], cf[:, c], den, ALU.mult))
            dve.tensor_copy(pw[:, :, :, 0:NS], pwn[:, :, :, 0:NS])
            for c in range(2):
                last = dve.tensor_copy(pw[:, c, :, NS:P], pwn[:, c, ::-1, NS:P])
            last.then_inc(S["tabsrc"], 1)

            cos = con[:, C_COS:C_COS + NT * 32].rearrange("p (t i) -> p t i", t=NT)
            sin = con[:, C_SIN:C_SIN + NT * 32].rearrange("p (t i) -> p t i", t=NT)
            dve.wait_ge(s_con, 16)
            rt1 = t3[:, 0:512].rearrange("p (c f i) -> p c f i", c=8, f=2)
            rt2 = t3[:, 512:1024].rearrange("p (c f i) -> p c f i", c=8, f=2)
            for n, slab, u, dst in ((1, "q", PB, qn), (2, "k", PA, kn)):
                slab_done(dve, slab)
                for t in range(NT):
                    x = pt[u][:, 512 * t:512 * (t + 1)].rearrange("p (c f i) -> p c f i", c=8, f=2)
                    y = dst[:, t].rearrange("p (c f i) -> p c f i", c=8, f=2)
                    cb = cos[:, t].unsqueeze(1).unsqueeze(1).to_broadcast([P, 8, 2, 32])
                    sb_ = sin[:, t].unsqueeze(1).unsqueeze(1).to_broadcast([P, 8, 2, 32])
                    dve.tensor_tensor(rt1, x, cb, ALU.mult)
                    link(dve.tensor_tensor(rt2, x, sb_, ALU.mult))
                    dve.tensor_tensor(y[:, :, 0], rt1[:, :, 0], rt2[:, :, 1], ALU.subtract)
                    last = dve.tensor_tensor(y[:, :, 1], rt1[:, :, 1], rt2[:, :, 0], ALU.add)
                    if t < NT - 1:
                        link(last)
                last.then_inc(S["rope"], 1)
                dve.wait_ge(S["rope"], n)

            dve.wait_ge(S["taba"], 1)
            for c in range(2):
                dve.tensor_copy(ipow[0:NS, c, 0:7], wpow[0:NS, c, 6::-1])
                dve.tensor_copy(ipow[NS:P, c, 1:8], wpow[NS:P, c, 7:0:-1])
                dve.memset(ipow[0:NS, c, 7], 1.0 - c)
                link(dve.memset(ipow[NS:P, c, 0], 1.0 - c))
            dve.wait_ge(s_braw, 64)
            cfr, cfi = (lam8[:, c * G:(c + 1) * G].unsqueeze(2).to_broadcast([P, G, HG]) for c in range(2))
            link(dve.tensor_tensor(tmp_v, braw[:, 0], cfr, ALU.mult))
            link(dve.tensor_tensor(bbar[:, 0], braw[:, 1], cfi, ALU.mult))
            link(dve.tensor_tensor(bbar[:, 0], tmp_v, bbar[:, 0], ALU.subtract))
            link(dve.tensor_tensor(tmp_v, braw[:, 1], cfr, ALU.mult))
            link(dve.tensor_tensor(bbar[:, 1], braw[:, 0], cfi, ALU.mult))
            link(dve.tensor_tensor(bbar[:, 1], tmp_v, bbar[:, 1], ALU.add))
            link(dve.memset(ring[:, 20480:22528], 0.0))
            for c in range(2):
                dve.tensor_copy(bsplit[0:NS, c, :, 1], bbar[0:NS, c])
                last = dve.tensor_copy(bsplit[NS:P, c, :, 0], bbar[NS:P, c])
            last.then_inc(S["bspl"], 1)
            l8 = lam8[:, 0:128].rearrange("p (f c g) -> p f c g", f=2, c=2)
            for lo, hi, t in ((0, NS, TC - 1), (NS, P, 0)):
                dve.tensor_copy(l8[lo:hi, 0, 0], wpow[lo:hi, 0, t])
                dve.tensor_copy(l8[lo:hi, 1, 1], wpow[lo:hi, 0, t])
                dve.tensor_copy(l8[lo:hi, 0, 1], wpow[lo:hi, 1, t])
                link(dve.tensor_scalar(l8[lo:hi, 1, 0], wpow[lo:hi, 1, t], -1.0, None, ALU.mult))
            dve.wait_ge(S["tabp"], 1)
            for t in range(TC):
                ir, ii = (ipow[:, c, t, :].unsqueeze(2).to_broadcast([P, G, HG]) for c in range(2))
                zr, zi = s5b[:, :, 0, t], s5b[:, :, 1, t]
                link(dve.tensor_tensor(tmp_v, bbar[:, 0], ir, ALU.mult))
                link(dve.tensor_tensor(zr, bbar[:, 1], ii, ALU.mult))
                link(dve.tensor_tensor(zr, tmp_v, zr, ALU.subtract))
                link(dve.tensor_tensor(tmp_v, bbar[:, 1], ir, ALU.mult))
                link(dve.tensor_tensor(zi, bbar[:, 0], ii, ALU.mult))
                last = dve.tensor_tensor(zi, tmp_v, zi, ALU.add)
                if t < TC - 1:
                    link(last)
            last.then_inc(S["bp"], 1)

            dve.wait_ge(S["laml"], 1)
            dve.wait_ge(s_dskip, 32)
            link(dve.tensor_tensor(st[:, 45:46], st[:, 44:45], st[:, 43:44], ALU.subtract))
            link(dve.tensor_scalar(st[:, 45:46], st[:, 45:46], LAMBDA_INIT, None, ALU.subtract))
            link(dve.tensor_scalar(st[:, 33:34], st[:, 32:33], 1.0 - LAMBDA_INIT, None, ALU.mult))

            def row_max(h):
                dve.wait_ge(S["scp"], h + 1)
                link(dve.tensor_reduce(sm[:, 4:8], pt[PD][:, :].rearrange("p (i l) -> p i l", i=4), AX.X, ALU.max))
                dve.tensor_scalar(sm[:, 0:4], sm[:, 4:8], -DH ** -0.5, None, ALU.mult).then_inc(S["smx"], 1)

            def weigh(h):
                dve.wait_ge(S["pex"], 4 * (h + 1))
                link(dve.reciprocal(sm[:, 16:20], sm[:, 8:12]))
                link(dve.tensor_scalar(sm[:, 20:22], sm[:, 18:20], st[:, 45:46], None, ALU.mult))
                for t in range(NT):
                    link(dve.tensor_scalar(prob[:, 1, t], prob[:, 1, t], sm[:, 20 + t:21 + t], None, ALU.mult))
                for t in range(NT):
                    last = dve.scalar_tensor_tensor(prob[:, 0, t], prob[:, 0, t], sm[:, 16 + t:17 + t], prob[:, 1, t],
                                                    ALU.mult, ALU.add)
                last.then_inc(S["pwv"], 1)

            for h in range(HEADS):
                row_max(h)
                weigh(h)
            for r in range(1, 8, 2):
                dve.wait_ge(S["ltp"], r + 1)
                dve.tensor_copy(ring[:, 8192 + 1024 * r:8192 + 1024 * (r + 1)], pt[PD][:, :]).then_inc(S["ltv"], 1)
            dve.wait_ge(S["pvp"], HEADS)
            dve.wait_ge(S["wtp"], HEADS)
            dve.wait_ge(S["qkp"], 2)
            dve.tensor_copy(t1[:, 1024:2048], pt[PA][:, :]).then_inc(S["on"], 1)
            dve.wait_ge(S["on"], 1)
            link(dve.tensor_tensor(t1[:, 0:1024], t1[:, 1024:2048], t1[:, 1024:2048], ALU.mult))
            dve.tensor_reduce(st[:, 20:28], t1[:, 0:1024].rearrange("p (i e) -> p i e", i=8), AX.X, ALU.add).then_inc(S["ssq"], 1)
            dve.wait_ge(S["root"], 2)
            link(dve.reciprocal(st[:, 46:54], st[:, 46:54]))
            dve.tensor_tensor(on, on, st[:, 46:54].rearrange("p (t h) -> p t h", t=NT).unsqueeze(3)
                              .to_broadcast([P, NT, HEADS, P]), ALU.mult).then_inc(S["on"], 1)
            dve.wait_ge(S["k0p"], 1)
            k0 = t1[:, 0:512].rearrange("p (j a h) -> p j a h", j=4, a=8)
            bm = con[:, C_BLK:C_BLK + P].rearrange("p (a h) -> p a h", a=8).unsqueeze(1).to_broadcast([P, 4, 8, HG])
            link(dve.tensor_tensor(k0, pt[PC][:, 0:512].rearrange("p (j a h) -> p j a h", j=4, a=8), bm, ALU.mult))
            k0s = t1[:, 512:576].rearrange("p (j h) -> p j h", j=4)
            link(dve.tensor_reduce(k0s, k0.rearrange("p j a h -> p j h a"), AX.X, ALU.add))
            for j in range(4):
                last = dve.scalar_tensor_tensor(ksr[:, j, 128:144], con[:, C_M16:C_M16 + HG], st[:, 36 + j:37 + j],
                                                k0s[:, j], ALU.mult, ALU.add)
            last.then_inc(S["kse"], 1)
            for c, u in enumerate((PB, PD)):
                dve.wait_ge(S["zp"], c + 1)
                src = pt[u][NS:P, :].rearrange("p (g k) -> p k g", g=G)
                dve.tensor_copy(zst[NS:P, :, c, :], src[:, ::-1, :]).then_inc(S["zvv"], 1)
            normed(1, mn, mn)
            gained(1, (PA, PB), memT)
            dve.wait_ge(S["zva"], 2)
            dve.wait_ge(S["zvv"], 2)
            dve.wait_ge(S["ktr"], 1)
            dve.wait_ge(S["k0p"], 1)
            link(dve.tensor_copy(xst[:, 0], zst[:, 0]))
            prod = lam8[:, 128:256].rearrange("p (f c g) -> p f c g", f=2, c=2)
            for k in range(1, NC):
                link(dve.tensor_tensor(prod, l8, xst[:, k - 1].unsqueeze(2).to_broadcast([P, 2, 2, G]), ALU.mult))
                link(dve.tensor_tensor(prod[:, 0], prod[:, 0], prod[:, 1], ALU.add))
                last = dve.tensor_tensor(xst[:, k], prod[:, 0], zst[:, k], ALU.add)
                if k < NC - 1:
                    link(last)
            last.then_inc(S["scan"], 1)
            dve.wait_ge(S["scan"], 1)
            dve.memset(enter[0:NS, :, :, 0:1], 0.0)
            dve.memset(enter[NS:P, :, :, NC - 1:NC], 0.0)
            for c in range(2):
                last = dve.tensor_copy(enter[NS:P, c, :, 0:NC - 1],
                                       xst[NS:P, NC - 2::-1, c, :].rearrange("p k g -> p g k"))
            last.then_inc(S["entv"], 1)
            dve.wait_ge(S["sgm"], 1)
            for i, u in enumerate((PC, PD)):
                slab_done(dve, f"ba{i}")
                dve.tensor_tensor(a1[:, 1024 * i:1024 * (i + 1)], a1[:, 1024 * i:1024 * (i + 1)], pt[u][:, :],
                                  ALU.mult).then_inc(S["bav"], 1)
            dve.wait_ge(S["gls"], 1)
            dve.tensor_tensor(uT_[:, :], glu_flat, pt[PC][:, :], ALU.mult).then_inc(S["osv"], 1)
            for i, u in enumerate((PA, PB)):
                slab_done(dve, f"bs{i}")
                dve.wait_ge(S["bav"], i + 1)
                dve.tensor_tensor(a2[:, 1024 * i:1024 * (i + 1)], a2[:, 1024 * i:1024 * (i + 1)], pt[u][:, :],
                                  ALU.mult).then_inc(S["bsv"], 1)
                dve.wait_ge(S["bsv"], 2 * i + 1)
                dve.tensor_tensor(a1[:, 1024 * i:1024 * (i + 1)], a1[:, 1024 * i:1024 * (i + 1)],
                                  a2[:, 1024 * i:1024 * (i + 1)], ALU.add).then_inc(S["bsv"], 1)

            def residual(prefix, units, done):
                for i, u in enumerate(units):
                    slab_done(dve, f"{prefix}{i}")
                    hs = h3[:, :, 512 * i:512 * (i + 1)]
                    dve.tensor_tensor(hs, hs, pt[u][:, :].rearrange("p (t n) -> p t n", t=NT), ALU.add).then_inc(S[done], 1)
                dve.wait_ge(S[done], 2)

            residual("mx", (PC, PD), "mh")
            normed(2, h3, xn)
            gained(2, (PA, PB), hnT)
            for i, u in enumerate((PA, PB)):
                dve.wait_ge(S["xsp"], i + 1)
                link(dve.tensor_reduce(sm[:, 24:28], pt[u][:, :].rearrange("p (i l) -> p i l", i=4), AX.X, ALU.max))
                dve.tensor_scalar(sm[:, 4 * i:4 * i + 4], sm[:, 24:28], -(D // HEADS) ** -0.5, None, ALU.mult).then_inc(S["xmx"], 1)
                dve.wait_ge(S["xmx"], i + 1)
            for i in range(2):
                dve.wait_ge(S["xex"], 4 * (i + 1))
                link(dve.reciprocal(sm[:, 16 + 4 * i:20 + 4 * i], sm[:, 8 + 4 * i:12 + 4 * i]))
                for n in range(4):
                    x = p2[:, 2 * i + n // 2, n % 2]
                    last = dve.tensor_scalar(x, x, sm[:, 16 + 4 * i + n:17 + 4 * i + n], None, ALU.mult)
                last.then_inc(S["xpn"], 1)
            residual("xo", (PC, PD), "xh")
            normed(3, h3, xn)
            gained(3, (PA, PB), hnT)

            dve.wait_ge(S["lgp"], 1)
            dve.tensor_tensor(lg, pt[PD][:, 0:NT * NE].rearrange("p (t e) -> p t e", t=NT),
                              brt.unsqueeze(1).to_broadcast([P, NT, NE]), ALU.add).then_inc(S["lgv"], 1)
            dve.wait_ge(S["lgv"], 1)
            for t in range(NT):
                link(dve.max(top8[:, t], lg[:, t]))
                link(dve.tensor_scalar(pse[:, 0, t:t + 1], top8[:, t, 0:1], -1.0, None, ALU.mult))
                link(dve.memset(top8[:, t, TOPK:8], 3.0e38))
                link(dve.match_replace(rep[:, t], top8[:, t], lg[:, t], -3.0e38))
                dve.tensor_tensor(msk[:, t], lg[:, t], rep[:, t], ALU.not_equal).then_inc(S["msk"], 1)
                dve.wait_ge(S["msk"], t + 1)
            for t in range(NT):
                dve.wait_ge(S["lex"], t + 1)
                link(dve.tensor_tensor(gate[:, t], gate[:, t], msk[:, t], ALU.mult))
                link(dve.tensor_reduce(pse[:, 1, t:t + 1], gate[:, t], AX.X, ALU.add))
                link(dve.reciprocal(pse[:, 1, t:t + 1], pse[:, 1, t:t + 1]))
                dve.tensor_scalar(gate[:, t], gate[:, t], pse[:, 1, t:t + 1], None, ALU.mult).then_inc(S["gdv"], 1)
            dve.wait_ge(S["rkp"], 1)
            cnt = pt[PD][0:NE, 512:513]
            link(dve.tensor_scalar(nbx[:, 0:1], cnt, float(SLOTS), None, ALU.is_gt))
            for b in range(2, MAXB):
                link(dve.scalar_tensor_tensor(nbx[:, 0:1], cnt, float(SLOTS * b), nbx[:, 0:1], ALU.is_gt, ALU.add))
            link(dve.scalar_tensor_tensor(posn, pt[PD][:, 0:NT * NE].rearrange("p (t e) -> p t e", t=NT), 1.0, msk,
                                          ALU.add, ALU.mult))
            dve.tensor_scalar(posn, posn, 1.0, None, ALU.subtract).then_inc(S["rkv"], 1)
            dve.wait_ge(S["rkv"], 1)
            dve.wait_ge(S["cup"], 1)
            link(dve.tensor_copy(nbx[:, 1:2], pt[PD][0:NE, 0:1]))
            link(dve.tensor_scalar(blk[:, 0:EXTRA], con[0:NE, C_IOTA:C_IOTA + EXTRA], nbx[:, 1:2], None, ALU.is_ge))
            link(dve.tensor_scalar(blk[:, EXTRA:2 * EXTRA], blk[:, 0:EXTRA], nbx[:, 0:1], None, ALU.mult))
            dve.tensor_copy(blk[:, 2 * EXTRA:2 * EXTRA + 1], nbx[:, 0:1]).then_inc(S["cuv"], 1)
            dve.wait_ge(S["ovp"], 1)
            link(dve.memset(offs, 0.0))
            tab = pt[PD][:, 512:512 + 2 * EXTRA + 1]
            link(dve.tensor_tensor(offs[:, NE:], con[:, C_IOTA:C_IOTA + EXTRA], tab[:, EXTRA:2 * EXTRA], ALU.subtract))
            link(dve.tensor_scalar(offs[:, NE:], offs[:, NE:], 1.0, float(SLOTS), ALU.add, ALU.mult))
            link(dve.tensor_scalar(ovf[:, 0:EXTRA], tab[:, 0:EXTRA], float(NE - 1), None, ALU.min))
            dve.tensor_copy(idx[:, 0:EXTRA], ovf[:, 0:EXTRA])
            dve.tensor_copy(idx[:, EXTRA:], tab[:, 2 * EXTRA:]).then_inc(S["ovi"], 1)
            dve.wait_ge(S["ovi"], 1)
            dve.wait_ge(S["b1a"], 1)
            gb = gains[:, 3 * KD:4 * KD].unsqueeze(2).to_broadcast([P, KD, SLOTS])

            STEPS = 6

            def block_of(it, e):
                n = [0]

                def chain(ins):
                    n[0] += 1
                    ins.then_inc(m_v, 1)
                    dve.wait_ge(m_v, it * STEPS + n[0])

                dve.wait_ge(m_st, it)
                chain(dve.tensor_tensor(pse[:, 0, :], posn[:, :, bass.ds(e, 1)].rearrange("p t e -> p (t e)"),
                                        offs[:, bass.ds(it, 1)].to_broadcast([P, NT]), ALU.subtract))
                chain(dve.tensor_copy(pse[:, 1, :], gate[:, :, bass.ds(e, 1)].rearrange("p t e -> p (t e)")))
                io = con[:, C_IOTA:C_IOTA + SLOTS]
                for t in range(NT):
                    dve.tensor_scalar(sel[:, t], io, pse[:, 0, t:t + 1], None, ALU.is_equal)
                for t in range(NT):
                    last = dve.tensor_scalar(selw[:, t], io, pse[:, 0, t:t + 1], pse[:, 1, t:t + 1], ALU.is_equal, ALU.mult)
                last.then_inc(m_sel, 1)
                dve.wait_ge(m_x, it + 1)
                dve.tensor_tensor(xg, pt[PD][:, 0:512].rearrange("p (k s) -> p k s", k=KD), gb, ALU.mult).then_inc(m_xev, 1)
                dve.wait_ge(m_w1u, KD * (it + 1))
                for i, dst in ((0, sg1), (1, sl1)):
                    b = b1T[:, KD * i:KD * (i + 1), bass.ds(e, 1)].to_broadcast([P, KD, SLOTS])
                    chain(dve.tensor_tensor(dst, pt[PC][:, 512 * i:512 * (i + 1)].rearrange("p (k s) -> p k s", k=KD), b,
                                            ALU.add))
                    if i == 0:
                        dve.tensor_scalar(sg2, sg1, GATE_MAX, None, ALU.min).then_inc(m_g2, 1)
                        dve.wait_ge(m_g2, it + 1)
                chain(dve.tensor_scalar(sl2, sl1, GATE_MAX, -GATE_MAX, ALU.min, ALU.max))
                chain(dve.scalar_tensor_tensor(sl1, sl2, 1.0, sg2, ALU.add, ALU.mult))
                dve.wait_ge(m_sig, it + 1)
                dve.tensor_tensor(hact, sl1, ssg, ALU.mult).then_inc(m_act, 1)
                assert n[0] == STEPS

            with dve.Fori(0, NE) as e:
                block_of(e, e)
            n_extra = dve.value_load(idx[0:1, EXTRA:EXTRA + 1], min_val=0, max_val=EXTRA)
            with dve.Fori(0, EXTRA) as j:
                with dve.If(n_extra > j):
                    block_of(NE + j, dve.value_load(idx[0:1, bass.ds(j, 1)], min_val=0, max_val=NE - 1))

            dve.wait_ge(s_gf, 16)
            dve.wait_ge(S["root"], 6)
            link(dve.reciprocal(st[:, 18:18 + NT], st[:, 18:18 + NT]))
            for t in range(NT):
                dve.scalar_tensor_tensor(h3[:, t], pt[(PA, PB)[t]][:, :], st[:, 18 + t:19 + t], gfin, ALU.mult,
                                         ALU.mult).then_inc(S["gfin"], 1)


_INS = ["x", "mem", "norm_mix_g", "w_in", "lambda_q1", "lambda_k1", "lambda_q2", "lambda_k2", "subln_g",
        "ssm_a_re", "ssm_a_im", "ssm_log_dt", "ssm_b_re", "ssm_b_im", "ssm_c_re", "ssm_c_im", "ssm_d", "w_glu",
        "w_branch_attn", "w_branch_ssm", "w_mix_out", "norm_cross_g", "norm_mem_g", "w_xq", "w_xkv", "w_xo",
        "norm_ffn_g", "w_router", "b_router", "w_e1", "b_e1", "w_e2", "b_e2", "norm_final_g"]


def kernel(**inputs):
    import numpy as _np
    import concourse.bacc as _bacc
    from concourse import mybir as _mybir
    from concourse.bass_utils import run_bass_kernel_spmd as _run

    nc = _bacc.Bacc("TRN2", target_bir_lowering=False, num_devices=1)
    arrays, T = {}, {}
    for name in _INS:
        a = _np.ascontiguousarray(inputs[name])
        arrays[f"in_{name}"] = a
        T[name] = nc.dram_tensor(f"in_{name}", a.shape, _mybir.dt.from_np(a.dtype), kind="ExternalInput").ap()
    arrays["consts"] = constants()
    T["consts"] = nc.dram_tensor("consts", (P, C_END), F32, kind="ExternalInput").ap()
    out = nc.dram_tensor("out_dram", (1, L, D), F32, kind="ExternalOutput").ap()
    build(nc, T, out)
    r = _run(nc, [arrays], core_ids=[0])
    return r.results[0]["out_dram"]
```

```python
from contextlib import ExitStack

import concourse.bass as bass
from concourse import mybir

F32 = mybir.dt.float32
I32 = mybir.dt.int32
ALU = mybir.AluOpType
ACT = mybir.ActivationFunctionType
AX = mybir.AxisListType

P = 128
D = 1024
L = 256
KD = D // P
NT = L // P
HEADS = 4
DH = 64
WA = 512
G, NS, HG = 32, 64, 16
TC = 8
NC = L // TC
NE, TOPK = 32, 4
SLOTS = 64
EXTRA = (L * TOPK - 1) // SLOTS
MAXB = (L + SLOTS - 1) // SLOTS
EPS = 1e-6
LAMBDA_INIT = 0.2
TWO_PI = 6.283185307179586
PI_A, PI_B, PI_C = 6.28125, 0.0019350051879882812, 3.0199159819567e-07
ROUND = 12582912.0
GATE_MAX = 7.0
GATE_ALPHA = 1.702
STAGE = 4

C_ID = 0
C_UP = C_ID + P
C_ONE = C_UP + P
C_BLK = C_ONE + P
C_M16 = C_BLK + P
C_IOTA = C_M16 + HG
C_COS = C_IOTA + 64
C_SIN = C_COS + NT * 32
C_TRI = C_SIN + NT * 32
C_END = C_TRI + NE


def constants():
    import numpy as np

    c = np.zeros((P, C_END), np.float32)
    r = np.arange(P)
    c[:, C_ID:C_ID + P] = np.eye(P)
    c[:, C_UP:C_UP + P] = r[:, None] < r[None, :]
    c[:, C_ONE:C_ONE + P] = 1
    c[:, C_BLK:C_BLK + P] = r[:, None] // HG == r[None, :] // HG
    c[:, C_M16:C_M16 + HG] = r[:, None] % HG == np.arange(HG)[None, :]
    c[:, C_IOTA:C_IOTA + 64] = np.arange(64)[None, :]
    inv = (np.float32(10000.0) ** (-np.arange(32, dtype=np.float32) * np.float32(2.0 / DH))).astype(np.float32)
    for t in range(NT):
        ang = ((t * P + r).astype(np.float32)[:, None] * inv[None, :]).astype(np.float32)
        c[:, C_COS + 32 * t:C_COS + 32 * t + 32] = np.cos(ang)
        c[:, C_SIN + 32 * t:C_SIN + 32 * t + 32] = np.sin(ang)
    c[:, C_TRI:C_TRI + NE] = (r[:, None] <= np.arange(NE)[None, :]) & (r[:, None] < NE)
    return c


def build(nc, T, out):
    ctx = ExitStack()
    with ctx:
        def sb(name, cols, parts=P, dt=F32):
            return ctx.enter_context(nc.sbuf_tensor(name, [parts, cols], dt))

        def sem(name):
            return ctx.enter_context(nc.semaphore(name))

        ring = sb("ring", 8 * 2048 + 8 * 1024)
        w1 = ring[:, 0:16384].rearrange("p (k n) -> p k n", k=KD)
        w2 = ring[:, 16384:24576].rearrange("p (k n) -> p k n", k=KD)
        s5w = ring[:, 0:8192].rearrange("p (c g t h) -> p c g t h", c=2, g=G, t=TC)
        s5b = ring[:, 8192:16384].rearrange("p (g c t h) -> p g c t h", g=G, c=2, t=TC)
        lin = ring[:, 8192:16384].rearrange("p (g c m) -> p g c m", g=G, c=2)
        toep = ring[:, 16384:20480].rearrange("p (g m) -> p g m", g=G)
        bsplit = ring[:, 20480:22528].rearrange("p (c g d h) -> p c g d h", c=2, g=G, d=2)
        zst = ring[:, 20480:22528].rearrange("p (k c g) -> p k c g", k=NC, c=2)
        bbar = ring[:, 22528:23552].rearrange("p (c g h) -> p c g h", c=2, g=G)
        tmp_v = ring[:, 23552:24064].rearrange("p (g h) -> p g h", g=G)
        tmp_p = ring[:, 24064:24576].rearrange("p (g h) -> p g h", g=G)
        zk = ring[:, 22528:24576].rearrange("p (a n) -> p a n", a=8)
        xst = ring[:, 22528:24576].rearrange("p (k c g) -> p k c g", k=NC, c=2)
        enter = ring[:, 8192:10240].rearrange("p (c g k) -> p c g k", c=2, g=G)
        craw = ring[:, 16384:17408].rearrange("p (c j m) -> p c j m", c=2, j=4)
        braw = ring[:, 17408:18432].rearrange("p (c g h) -> p c g h", c=2, g=G)
        y4 = ring[:, 11264:12288].rearrange("p (t a h) -> p t a h", t=TC, a=8)
        prep = ring[0:G, 8192:16384]

        stage = sb("stage", STAGE * 2048)
        slot = [stage[:, i * 2048:(i + 1) * 2048].rearrange("p (k n) -> p k n", k=4) for i in range(STAGE)]
        con = sb("con", C_END)
        ident = con[:, C_ID:C_ID + P]
        ones = con[:, C_ONE:C_ONE + P]
        hres = sb("hres", NT * D)
        h3 = hres[:, :].rearrange("p (t n) -> p t n", t=NT)
        hnt = sb("hnt", KD * L)
        hnT = hnt[:, :].rearrange("p (k l) -> p k l", k=KD)
        a1 = sb("a1", 2048)
        a2 = sb("a2", 2048)
        t1, t2, t3 = sb("t1", 2048), sb("t2", 2048), sb("t3", 2048)
        gaT = a1[:, :].rearrange("p (k l) -> p k l", k=KD)
        gsT = a2[:, :].rearrange("p (k l) -> p k l", k=KD)
        pw = a1[0:G, :].rearrange("p (c t m) -> p c t m", c=2, t=TC)
        xn = a2[:, :].rearrange("p (t n) -> p t n", t=NT)
        usb = a2[:, 0:1024].rearrange("p (t n) -> p t n", t=NT)
        u4 = a2[:, 1024:2048].rearrange("p (t n) -> p t n", t=TC)
        u5 = a2[:, 0:1024].rearrange("p (a t h) -> p a t h", a=8, t=TC)
        qn = t1[:, 0:1024].rearrange("p (t n) -> p t n", t=NT)
        kn = t1[:, 1024:2048].rearrange("p (t n) -> p t n", t=NT)
        vn = t2[:, 0:1024].rearrange("p (t n) -> p t n", t=NT)
        qT = t2[:, 1024:2048].rearrange("p (h l) -> p h l", h=HEADS)
        kT0 = t3[:, 0:1024].rearrange("p (h l) -> p h l", h=HEADS)
        wT = t3[:, 1024:2048].rearrange("p (b k l) -> p b k l", b=2, k=NT)
        prob = t1[:, 0:1024].rearrange("p (c t l) -> p c t l", c=2, t=NT)
        on = t1[:, 1024:2048].rearrange("p (t h e) -> p t h e", t=NT, h=HEADS)
        memT = t1[:, :].rearrange("p (k l) -> p k l", k=KD)
        mkT = t2[:, :].rearrange("p (k l) -> p k l", k=KD)
        mn = t3[:, :].rearrange("p (t n) -> p t n", t=NT)
        big = sb("big", 1024 + 4 * HG)
        kT1 = big[:, 0:1024].rearrange("p (h l) -> p h l", h=HEADS)
        tap0 = big[:, 1024:].rearrange("p (j h) -> p j h", j=4)
        taps = t1[:, 1024:2048].rearrange("p (a n) -> p a n", a=8)
        uT_ = sb("uT_", 1024)
        uT = uT_[:, :].rearrange("p (a n) -> p a n", a=8)
        ct_ = sb("ct_", 1024)
        ct = ct_[:, :].rearrange("p (c j n) -> p c j n", c=2, j=4)
        wi_ = sb("wi_", 1024)
        wpow = wi_[:, 0:512].rearrange("p (c t g) -> p c t g", c=2, t=TC)
        ipow = wi_[:, 512:1024].rearrange("p (c t g) -> p c t g", c=2, t=TC)
        oT = wi_[:, :].rearrange("p (h l) -> p h l", h=HEADS)
        yT = ct_[:, :].rearrange("p (j l) -> p j l", j=4)
        osT = uT_[:, :].rearrange("p (j l) -> p j l", j=4)
        graw = ring[0:4 * KD, 16384:16384 + P]
        gains = sb("gains", 4 * KD)
        st = sb("st", 64)
        lamb = sb("lamb", 4 * DH)
        lam8 = sb("lam8", 2 * 2 * 2 * G)
        sm = sb("sm", 3 * NT * 4 + 8)
        idx = sb("idx", NE + EXTRA + 2, dt=I32)

        pt = [ctx.enter_context(nc.psum_tensor(f"pt{i}", [P, 1024], F32)) for i in range(4)]
        PA, PB, PC, PD = range(4)

        taps_dram = nc.dram_tensor("taps_dram", [G, HG, 272], F32, kind="Internal").ap()

        s_con = sem("const_loaded"); s_x = sem("x_loaded"); s_gain = sem("gains_loaded"); s_small = sem("s5_small_loaded")
        s_braw = sem("b_loaded"); s_craw = sem("c_loaded"); s_lamb = sem("lambda_loaded"); s_mem = sem("mem_loaded")
        s_u4 = sem("u4_regrouped"); s_tapw = sem("taps_written"); s_tap0 = sem("lag0_taps_written"); s_toep = sem("toeplitz_loaded")
        s_rt = sem("router_loaded"); s_b1 = sem("expert_bias_loaded"); s_gf = sem("final_gain_loaded")
        s_out = sem("out_written"); s_dskip = sem("d_loaded")
        s_slot = [sem(f"slot{i}_loaded") for i in range(STAGE)]
        s_used = sem("slots_used")
        s_v = sem("dve_step"); s_a = sem("act_step"); s_p = sem("pool_step")
        names = """root epsv ssq u4r usb dtl mag red trig tabsrc tabp taba bspl vev utp uta ctp cta scp smx pex pwv wtp wta pvp on
            otp ota lamx laml bp s5wd kp kta k0p kse kz ltp lta ltv zp zka zkv ztp zva zvv scan enta entv mka mva
            sgm bav yp ygel ytp graw yta gls osv bsv mh xqa xsp xmx xex xpn xtp xta xop xoa xh lgp lgv lex msk
            rkp rkv gdv gdp gda cup cuv ovp ovi acci hn3 gfin accd rope gates qkp qka sumsq normed tokp
            tokv""".split()
        S = {n: sem(n) for n in names}
        s_w1 = [sem(f"w1_chunk{k}_loaded") for k in range(KD)]
        s_w2 = [sem(f"w2_pair{k}_loaded") for k in range(KD // 2)]
        m_sel = sem("block_selected"); m_selw = sem("block_weighted"); m_x = sem("block_gathered")
        m_xn = sem("block_tokens_copied"); m_xt = sem("block_tokens_turned"); m_xT = sem("block_tokens_ready")
        m_w1u = sem("w1_chunks_consumed"); m_w2u = sem("w2_pairs_consumed"); m_st = sem("scatter_transposed")
        m_gs = sem("scatter_ready"); m_g2 = sem("gate_clamped"); m_sig = sem("gate_sigmoid"); m_act = sem("hidden_ready")
        m_at = sem("hidden_turned"); m_hT = sem("hidden_turned_ready"); m_y = sem("y_ready"); m_v = sem("block_dve_step")
        m_sc = sem("scattered")

        cols = {"u": ("w_in", 3 * WA), "q": ("w_in", 0), "k": ("w_in", WA), "v": ("w_in", 2 * WA)}
        SLABS = [(n, *cols[n], D) for n in "uqkv"]
        for n, w, c0, rows, count in (("ga", "w_in", 4 * WA, D, 2), ("gs", "w_in", 6 * WA, D, 2), ("mk", "w_xkv", 0, D, 2),
                                      ("mv", "w_xkv", D, D, 2), ("ba", "w_branch_attn", 0, WA, 2), ("gl", "w_glu", 0, WA, 2),
                                      ("bs", "w_branch_ssm", 0, WA, 2), ("mx", "w_mix_out", 0, D, 2),
                                      ("xq", "w_xq", 0, D, 2), ("xo", "w_xo", 0, D, 2)):
            SLABS += [(f"{n}{i}", w, c0 + WA * i, rows) for i in range(count)]
        SLABS.insert([s[0] for s in SLABS].index("gl1"), SLABS.pop([s[0] for s in SLABS].index("ba1")))
        SLAB_NO = {s[0]: i for i, s in enumerate(SLABS)}
        SLOT_USES = [(i, w, r, c) for i, (_, w, c, rows) in enumerate(SLABS) for r in range(0, rows, WA)]

        SLAB_END = {n: sum(u[0] <= i for u in SLOT_USES) for n, i in SLAB_NO.items()}

        def slab_done(eng, name):
            eng.wait_ge(s_used, SLAB_END[name])

        w1_dram = T["w_e1"].rearrange("a e (k p) n -> (a e) k p n", p=P)
        w2_dram = T["w_e2"].rearrange("a e (k p) n -> (a e) p k n", p=P)

        def load_w1(eng, e, k):
            src = w1_dram[0, k] if e is None else w1_dram[bass.ds(e, 1), k].rearrange("a p n -> p (a n)")
            eng.dma_start(w1[:, k, :], src).then_inc(s_w1[k], 16)

        def load_w2(eng, e, kk):
            if e is None:
                src = w2_dram[0, :, 2 * kk:2 * kk + 2, :]
            else:
                src = w2_dram[bass.ds(e, 1), :, 2 * kk:2 * kk + 2, :].rearrange("a p k n -> p (a k) n")
            eng.dma_start(w2[:, 2 * kk:2 * kk + 2, :], src).then_inc(s_w2[kk], 16)

        block = ctx.enter_context(nc.Block())

        def part(a, n):
            return stage[:, a:a + n]
        xgn = part(0, 512)
        xT = part(512, 512).rearrange("p (c n s) -> p c n s", c=4, n=2)
        hg = part(1024, 512)
        hl = part(1536, 512)
        hgl = part(2048, 512)
        hsg = part(2560, 512)
        hact = part(3072, 512)
        hT = part(3584, 512).rearrange("p (c g s) -> p c g s", c=4, g=2)
        ysb = part(4096, 512)
        gsc = part(4608, 512).rearrange("p (n t l) -> p n t l", n=2, t=NT)
        ecol = part(5120, SLOTS)
        selw = part(5200, NT * 3 * SLOTS).rearrange("p (t s) -> p t s", t=NT)
        sel = part(5888, NT * SLOTS).rearrange("p (t s) -> p t s", t=NT)
        posn = part(6144, NT * NE).rearrange("p (t e) -> p t e", t=NT)
        gate = part(6208, NT * NE).rearrange("p (t e) -> p t e", t=NT)
        lg = part(6272, NT * NE).rearrange("p (t e) -> p t e", t=NT)
        msk = part(6336, NT * NE).rearrange("p (t e) -> p t e", t=NT)
        offs = part(6400, NE + EXTRA + 1)
        pse = part(6464, 2 * NT).rearrange("p (a t) -> p a t", a=2)
        top8 = part(6472, NT * 8).rearrange("p (t e) -> p t e", t=NT)
        rep = part(6488, NT * NE).rearrange("p (t e) -> p t e", t=NT)
        ovf = part(6552, 2 * EXTRA + 1)
        gT = stage[0:NE, 6656:6656 + L]
        wr = uT_[:, 0:KD * NE].rearrange("p (k e) -> p k e", k=KD)
        nbx = part(7168, 2)[0:NE]
        blk = part(7176, 2 * EXTRA + 1)[0:NE]
        p2 = a1[:, :].rearrange("p (h t l) -> p h t l", h=HEADS, t=NT)
        p2T = t1[:, :].rearrange("p (h k l) -> p h k l", h=HEADS, k=NT)
        glu_flat = big[:, 0:1024]
        hnT_flat = hnt[:, :]
        gfin = t1[:, 0:D]
        be1 = t3
        gffn = wi_[:, :]
        be2 = t2[0:NE, 0:D]
        brt = t1[:, 1024:1024 + NE]

        @block.sync
        def _(sp):
            sp.dma_start(h3, T["x"].rearrange("a (t p) n -> p (a t) n", p=P)).then_inc(s_x, 16)
            sp.dma_start(con[:, :], T["consts"]).then_inc(s_con, 16)
            for i, n in enumerate(("norm_mix_g", "norm_mem_g", "norm_cross_g", "norm_ffn_g")):
                sp.dma_start(graw[i * KD:(i + 1) * KD], T[n].rearrange("a (k p) -> (a k) p", p=P)).then_inc(s_gain, 16)
            pre = [(load_w1, k) for k in range(KD)] + [(load_w2, k) for k in range(KD // 2)]
            for i, (slab, w, r, c) in enumerate(SLOT_USES):
                if i >= STAGE:
                    sp.wait_ge(s_used, i - STAGE + 1)
                src = T[w][0, r:r + WA, c:c + WA].rearrange("(k p) n -> p k n", p=P)
                sp.dma_start(slot[i % STAGE], src).then_inc(s_slot[i % STAGE], 16)
                if slab >= SLAB_NO["mx0"] and pre:
                    if len(pre) == KD + KD // 2:
                        sp.wait_ge(S["ytp"], 1)
                    load, k = pre.pop(0)
                    load(sp, None, k)
            for load, k in pre:
                load(sp, None, k)

            def refill(it, e):
                for k in range(KD):
                    sp.wait_ge(m_w1u, KD * (it - 1) + k + 1)
                    load_w1(sp, e, k)
                for kk in range(KD // 2):
                    sp.wait_ge(m_w2u, (KD // 2) * (it - 1) + kk + 1)
                    load_w2(sp, e, kk)

            with sp.Fori(1, NE) as e:
                refill(e, e)
            sp.wait_ge(S["ovi"], 1)
            n_extra = sp.value_load(idx[0:1, NE + EXTRA + 1:NE + EXTRA + 2], min_val=0, max_val=EXTRA)
            with sp.Fori(0, EXTRA) as j:
                with sp.If(n_extra > j):
                    refill(NE + j, sp.value_load(idx[0:1, bass.ds(NE + j, 1)], min_val=0, max_val=NE - 1))
            sp.wait_ge(S["gfin"], NT)
            sp.dma_start(out.rearrange("a (t p) n -> p (a t) n", p=P), h3).then_inc(s_out, 16)
            sp.wait_ge(s_out, 16)

        @block.gpsimd
        def _(pool):
            steps = [0]

            def link(ins):
                steps[0] += 1
                ins.then_inc(s_p, 1)
                pool.wait_ge(s_p, steps[0])

            are = prep[:, 0:128].rearrange("p (d m) -> p d m", d=2)
            aim = prep[:, 128:256].rearrange("p (d m) -> p d m", d=2)
            ldt = prep[:, 256:258]
            pool.dma_start(are, T["ssm_a_re"].rearrange("a d g p -> g (a d) p")).then_inc(s_small, 16)
            pool.dma_start(aim, T["ssm_a_im"].rearrange("a d g p -> g (a d) p")).then_inc(s_small, 16)
            pool.dma_start(ldt, T["ssm_log_dt"].rearrange("a d g -> g (a d)"),
                           allow_slow_non_contiguous=True).then_inc(s_small, 16)
            pool.wait_ge(S["graw"], 1)
            for c, n in enumerate(("ssm_c_re", "ssm_c_im")):
                for d in range(2):
                    dst = craw[:, c, :, d * NS:(d + 1) * NS]
                    src = T[n][0, d].rearrange("(j a) h p -> (a h) j p", j=4)
                    pool.dma_start(dst, src).then_inc(s_craw, 16)
            for c, n in enumerate(("ssm_b_re", "ssm_b_im")):
                for d in range(2):
                    pool.dma_start(braw[d * NS:(d + 1) * NS, c], T[n][0, d].rearrange("g p h -> p g h")).then_inc(s_braw, 16)
            for i, n in enumerate(("lambda_q1", "lambda_k1", "lambda_q2", "lambda_k2")):
                pool.dma_start(lamb[:, i * DH:(i + 1) * DH], T[n].broadcast_to([P, DH])).then_inc(s_lamb, 16)
            pool.dma_start(st[:, 32:33], T["subln_g"].rearrange("a p -> p a"), allow_slow_non_contiguous=True).then_inc(s_dskip, 16)
            pool.dma_start(st[:, 36:40], T["ssm_d"].rearrange("a (j p) -> p (a j)", p=P),
                           allow_slow_non_contiguous=True).then_inc(s_dskip, 16)

            pool.wait_ge(S["taba"], 1)
            pool.wait_ge(S["cta"], 1)
            cr = ct[:, 0].rearrange("p j (a h) -> p (j a) h", h=HG)
            cn = ct[:, 1].rearrange("p j (a h) -> p (j a) h", h=HG)
            for t in range(TC):
                lr = wpow[:, 0, t, :].unsqueeze(2).to_broadcast([P, G, HG])
                li = wpow[:, 1, t, :].unsqueeze(2).to_broadcast([P, G, HG])
                link(pool.tensor_tensor(tmp_p, cr, lr, ALU.mult))
                link(pool.tensor_tensor(s5w[:, 0, :, t, :], cn, li, ALU.mult))
                link(pool.tensor_tensor(s5w[:, 0, :, t, :], tmp_p, s5w[:, 0, :, t, :], ALU.add))
                link(pool.tensor_tensor(tmp_p, cr, li, ALU.mult))
                link(pool.tensor_tensor(s5w[:, 1, :, t, :], cn, lr, ALU.mult))
                last = pool.tensor_tensor(s5w[:, 1, :, t, :], s5w[:, 1, :, t, :], tmp_p, ALU.subtract)
                if t < TC - 1:
                    link(last)
            last.then_inc(S["s5wd"], 1)

            pool.wait_ge(S["kse"], 1)
            pool.dma_start(taps_dram[:, :, 128:144].rearrange("(j a) h n -> (a h) j n", j=4), tap0).then_inc(s_tap0, 16)
            pool.wait_ge(s_tap0, 16)
            pool.wait_ge(s_tapw, 8 * 16)
            for t in range(TC):
                pool.dma_start(toep[HG * t:HG * (t + 1)],
                               taps_dram[:, :, HG * (TC - t):HG * (TC - t) + P].rearrange("g h n -> h g n")).then_inc(s_toep, 16)
            pool.wait_ge(S["pvp"], HEADS)
            pool.dma_start(mn, T["mem"].rearrange("a (t p) n -> p (a t) n", p=P)).then_inc(s_mem, 16)
            slab_done(pool, "bs1")
            pool.dma_start(gffn, T["norm_ffn_g"].broadcast_to([P, D])).then_inc(s_gf, 16)
            pool.dma_start(wr, T["w_router"].rearrange("a (k p) e -> p (a k) e", p=P)).then_inc(s_rt, 16)
            pool.wait_ge(S["xop"], 2)
            pool.dma_start(brt, T["b_router"].broadcast_to([P, NE])).then_inc(s_rt, 16)
            link(pool.memset(t3[:, :], 0.0))
            pool.dma_start(t3[0:NE, :], T["b_e1"].rearrange("a e n -> (a e) n")).then_inc(s_b1, 16)
            pool.dma_start(be2, T["b_e2"].rearrange("a e n -> (a e) n")).then_inc(s_b1, 16)
            pool.dma_start(gfin, T["norm_final_g"].rearrange("(a n) -> a n", a=1).broadcast_to([P, D])).then_inc(s_gf, 16)
            pool.wait_ge(s_gf, 32)
            pool.wait_ge(S["tokp"], 8)
            for t in range(NT):
                pool.tensor_tensor(xn[:, t], xn[:, t], gffn, ALU.mult).then_inc(S["hn3"], 1)

        @block.tensor
        def _(pe):
            readers = [[], [], [], []]
            slots_used = [0]

            def take(u, *who):
                for name, n in readers[u]:
                    pe.wait_ge(S[name], n)
                readers[u] = list(who)

            def turn(dst, src):
                n = src.shape[0]
                return pe.transpose(dst, src, ident[0:n, 0:n])

            def weights(slab):
                got = []
                while slots_used[0] < len(SLOT_USES) and SLOT_USES[slots_used[0]][0] == SLAB_NO[slab]:
                    i = slots_used[0]
                    pe.wait_ge(s_slot[i % STAGE], 16 * (i // STAGE + 1))
                    got.append(slot[i % STAGE])
                    slots_used[0] += 1
                return got

            def natural(slab, u, xT, *who):
                ws = weights(slab)
                take(u, *who)
                for t in range(NT):
                    for k in range(4 * len(ws)):
                        last = pe.matmul(pt[u][:, 512 * t:512 * t + 512], xT[:, k, t * P:(t + 1) * P],
                                         ws[k // 4][:, k % 4, :], start=(k == 0), stop=(k == 4 * len(ws) - 1))
                        if t == NT - 1 and k % 4 == 3:
                            last.then_inc(s_used, 1)

            def flipped(slab, u, xT, *who):
                ws = weights(slab)
                take(u, *who)
                for m in range(4):
                    for k in range(4 * len(ws)):
                        last = pe.matmul(pt[u][:, L * m:L * m + L], ws[k // 4][:, k % 4, m * P:(m + 1) * P], xT[:, k, :],
                                         start=(k == 0), stop=(k == 4 * len(ws) - 1))
                        if m == 3 and k % 4 == 3:
                            last.then_inc(s_used, 1)

            def turn_tokens(src, units, norm):
                pe.wait_ge(S["normed"], NT * (norm + 1))
                for i, u in enumerate(units):
                    take(u, ("tokv", 2 * norm + i + 1))
                    for k in range(4):
                        for t in range(NT):
                            last = turn(pt[u][:, L * k + P * t:L * k + P * (t + 1)],
                                        src[:, t, P * (4 * i + k):P * (4 * i + k + 1)])
                    last.then_inc(S["tokp"], 1)

            pe.wait_ge(s_con, 16)
            pe.wait_ge(s_gain, 64)
            turn(pt[PA][:, 0:4 * KD], graw).then_inc(S["graw"], 1)
            readers[PA] = [("tokv", 1)]
            turn_tokens(xn, (PC, PD), 0)
            pe.wait_ge(S["tokv"], 2)
            natural("u", PA, hnT, ("usb", 1))
            natural("q", PB, hnT, ("rope", 1))

            pe.wait_ge(S["tabsrc"], 1)
            take(PC, ("taba", 1))
            for c in range(2):
                for t in range(TC):
                    turn(pt[PC][:, (c * TC + t) * G:(c * TC + t + 1) * G], pw[:, c, t, :])
            for c in range(2):
                last = turn(pt[PC][:, 512 + c * G:512 + (c + 1) * G], prep[:, 4096 + c * P:4096 + (c + 1) * P])
            last.then_inc(S["tabp"], 1)
            pe.wait_ge(s_craw, 64)
            take(PD, ("cta", 1))
            for c in range(2):
                for j in range(4):
                    last = turn(pt[PD][:, (4 * c + j) * P:(4 * c + j + 1) * P], craw[:, c, j, :])
            last.then_inc(S["ctp"], 1)

            natural("k", PA, hnT, ("rope", 2))
            natural("v", PB, hnT, ("vev", 1))

            pe.wait_ge(S["u4r"], 1)
            take(PC, ("uta", 1))
            for a in range(8):
                last = turn(pt[PC][:, P * a:P * (a + 1)], u5[:, a])
            last.then_inc(S["utp"], 1)
            flipped("ga0", PA, hnT, ("gates", 1))

            for n, src, u in ((1, qn, PD), (2, kn, PC)):
                pe.wait_ge(S["rope"], n)
                take(u, ("qka", n))
                for h in range(HEADS):
                    for t in range(NT):
                        last = turn(pt[u][:, L * h + P * t:L * h + P * (t + 1)], src[:, t, P * h:P * (h + 1)])
                last.then_inc(S["qkp"], 1)

            def scores(h):
                take(PD, ("smx", h + 1), ("pex", 4 * (h + 1)))
                for t in range(NT):
                    for c in range(2):
                        last = pe.matmul(pt[PD][:, 512 * c + L * t:512 * c + L * (t + 1)],
                                         qT[:, h, P * t:P * (t + 1)], (kT0, kT1)[c][:, h, :],
                                         start=True, stop=True)
                last.then_inc(S["scp"], 1)

            def turn_probs(h):
                pe.wait_ge(S["pwv"], h + 1)
                take(PC, ("wta", h + 1))
                for k in range(NT):
                    for t in range(NT):
                        last = turn(pt[PC][:, L * k + P * t:L * k + P * (t + 1)], prob[:, 0, t, P * k:P * (k + 1)])
                last.then_inc(S["wtp"], 1)

            def values(h):
                pe.wait_ge(S["wta"], h + 1)
                if h == 0:
                    take(PA, ("on", 1))
                for t in range(NT):
                    for k in range(NT):
                        last = pe.matmul(pt[PA][:, 512 * t + P * h:512 * t + P * (h + 1)], wT[:, h % 2, k, P * t:P * (t + 1)],
                                         vn[:, k, P * h:P * (h + 1)], start=(k == 0), stop=(k == NT - 1))
                last.then_inc(S["pvp"], 1)

            pe.wait_ge(S["qka"], 2)
            pe.wait_ge(S["vev"], 1)
            scores(0)
            flipped("ga1", PB, hnT, ("gates", 2))
            turn_probs(0)
            scores(1)
            flipped("gs0", PB, hnT, ("gates", 3))
            values(0)
            turn_probs(1)
            scores(2)
            flipped("gs1", PB, hnT, ("gates", 4))
            values(1)
            turn_probs(2)
            scores(3)

            pe.wait_ge(S["s5wd"], 1)
            pe.wait_ge(S["bspl"], 1)
            take(PB, ("kta", 1))
            for a in range(8):
                for c in range(2):
                    for j in range(4):
                        last = pe.matmul(pt[PB][32 * j:32 * (j + 1), P * a:P * (a + 1)], bsplit[:, c, 8 * j + a],
                                         s5w[:, c, 8 * j + a], start=(c == 0), stop=(c == 1))
            last.then_inc(S["kp"], 1)
            take(PC, ("kse", 1))
            for j in range(4):
                for c in range(2):
                    last = pe.matmul(pt[PC][:, P * j:P * (j + 1)], bbar[:, c, 8 * j:8 * j + 8], ct[:, c, j],
                                     start=(c == 0), stop=(c == 1))
            last.then_inc(S["k0p"], 1)
            values(2)
            turn_probs(3)

            pe.wait_ge(S["bp"], 1)
            for r in range(8):
                u, read = ((PB, "lta"), (PD, "ltv"))[r % 2]
                take(u, (read, r // 2 + 1))
                for i in range(8):
                    last = turn(pt[u][:, P * i:P * (i + 1)], s5b[:, 4 * r + i // 2, i % 2])
                last.then_inc(S["ltp"], 1)
            values(3)

            pe.wait_ge(S["lta"], 4)
            pe.wait_ge(S["ltv"], 4)
            for i, (u, read) in enumerate(((PB, "zka"), (PD, "zkv"))):
                take(u, (read, 1))
                for a in range(4 * i, 4 * i + 4):
                    for j in range(4):
                        last = pe.matmul(pt[u][32 * j:32 * (j + 1), L * (a % 4):L * (a % 4 + 1)], uT[:, a, NC * j:NC * (j + 1)],
                                         lin[:, 8 * j + a].rearrange("p c m -> p (c m)"), start=True, stop=True)
                last.then_inc(S["zp"], 1)

            pe.wait_ge(S["on"], 2)
            take(PC, ("ota", 1))
            for h in range(HEADS):
                for t in range(NT):
                    last = turn(pt[PC][:, L * h + P * t:L * h + P * (t + 1)], on[:, t, h])
            last.then_inc(S["otp"], 1)

            for i, (u, read) in enumerate(((PB, "zka"), (PD, "zkv"))):
                pe.wait_ge(S[read], 1)
                take(u, ("zva", 2 * i + 2), ("zvv", 2 * i + 2))
                for a in range(4 * i, 4 * i + 4):
                    for c in range(2):
                        n = 2 * (a % 4) + c
                        last = turn(pt[u][:, P * n:P * (n + 1)], zk[:, a, P * c:P * (c + 1)])
                last.then_inc(S["ztp"], 1)

            turn_tokens(mn, (PA, PB), 1)
            pe.wait_ge(S["tokv"], 4)
            flipped("mk0", PC, memT, ("mka", 1))
            flipped("mk1", PD, memT, ("mka", 2))
            natural("mv0", PA, memT, ("mva", 1))

            pe.wait_ge(s_toep, TC * 16)
            pe.wait_ge(S["enta"], 2)
            pe.wait_ge(S["entv"], 1)
            take(PB, ("ygel", 1))
            for a in range(8):
                for i in range(3):
                    for j in range(4):
                        g = 8 * j + a
                        lhsT = uT[:, a, NC * j:NC * (j + 1)] if i == 0 else enter[:, i - 1, g]
                        rhs = toep[:, g] if i == 0 else s5w[:, i - 1, g].rearrange("p t h -> p (t h)")
                        last = pe.matmul(pt[PB][32 * j:32 * (j + 1), P * a:P * (a + 1)], lhsT, rhs, start=(i == 0), stop=(i == 2))
            last.then_inc(S["yp"], 1)
            natural("mv1", PC, memT, ("mva", 2))
            pe.wait_ge(S["ygel"], 1)
            take(PD, ("yta", 1))
            for t in range(TC):
                last = turn(pt[PD][:, P * t:P * (t + 1)], y4[:, t])
            last.then_inc(S["ytp"], 1)
            pe.wait_ge(S["ota"], 1)
            flipped("ba0", PA, oT, ("bav", 1))
            pe.wait_ge(S["yta"], 1)
            flipped("gl0", PC, yT, ("osv", 1))
            flipped("gl1", PD, yT, ("gls", 1))
            flipped("ba1", PB, oT, ("bav", 2))
            pe.wait_ge(S["osv"], 1)
            flipped("bs0", PA, osT, ("bsv", 2))
            flipped("bs1", PC, osT, ("bsv", 4))
            pe.wait_ge(S["bsv"], 4)
            natural("mx0", PB, gaT, ("mh", 1))
            natural("mx1", PD, gaT, ("mh", 2))

            turn_tokens(xn, (PA, PB), 2)
            pe.wait_ge(S["tokv"], 6)
            flipped("xq0", PC, hnT, ("xqa", 1))
            flipped("xq1", PD, hnT, ("xqa", 2))
            pe.wait_ge(S["mka"], 2)
            for i, u in enumerate((PA, PB)):
                pe.wait_ge(S["xqa"], i + 1)
                take(u, ("xmx", i + 1), ("xex", 4 * (i + 1)))
                for hh in range(2):
                    for t in range(NT):
                        for m in range(2):
                            k = 4 * i + 2 * hh + m
                            last = pe.matmul(pt[u][:, 512 * hh + L * t:512 * hh + L * (t + 1)], gsT[:, k, P * t:P * (t + 1)],
                                             mkT[:, k, :], start=(m == 0), stop=(m == 1))
                last.then_inc(S["xsp"], 1)
            for i, u in enumerate((PC, PD)):
                pe.wait_ge(S["xpn"], i + 1)
                take(u, ("xta", i + 1))
                for hh in range(2):
                    for k in range(NT):
                        for t in range(NT):
                            last = turn(pt[u][:, 512 * hh + L * k + P * t:512 * hh + L * k + P * (t + 1)],
                                        p2[:, 2 * i + hh, t, P * k:P * (k + 1)])
                last.then_inc(S["xtp"], 1)
            pe.wait_ge(S["mva"], 2)
            for i, u in enumerate((PA, PB)):
                pe.wait_ge(S["xta"], i + 1)
                take(u, ("xoa", i + 1))
                for hh in range(2):
                    h = 2 * i + hh
                    for m in range(2):
                        for k in range(NT):
                            last = pe.matmul(pt[u][:, 512 * hh + L * m:512 * hh + L * (m + 1)],
                                             mn[:, k, L * h + P * m:L * h + P * (m + 1)], p2T[:, h, k],
                                             start=(k == 0), stop=(k == NT - 1))
                last.then_inc(S["xop"], 1)
            pe.wait_ge(S["xoa"], 2)
            natural("xo0", PC, hnT, ("xh", 1))
            natural("xo1", PD, hnT, ("xh", 2))

            turn_tokens(xn, (PA, PB), 3)
            pe.wait_ge(S["tokv"], 8)
            pe.wait_ge(s_rt, 32)
            take(PD, ("lgv", 1))
            for t in range(NT):
                for k in range(KD):
                    last = pe.matmul(pt[PD][:, NE * t:NE * (t + 1)], hnT[:, k, P * t:P * (t + 1)], wr[:, k, :],
                                     start=(k == 0), stop=(k == KD - 1))
            last.then_inc(S["lgp"], 1)
            pe.wait_ge(S["msk"], NT)
            take(PD, ("rkv", 1))
            up = con[:, C_UP:C_UP + P]
            pe.matmul(pt[PD][:, 0:NE], up, msk[:, 0, :], start=True, stop=True)
            pe.matmul(pt[PD][:, NE:2 * NE], ones, msk[:, 0, :], start=True, stop=False)
            pe.matmul(pt[PD][:, NE:2 * NE], up, msk[:, 1, :], start=False, stop=True)
            for t in range(NT):
                last = pe.matmul(pt[PD][0:NE, 512:513], msk[:, t, :], ones[:, 0:1], start=(t == 0), stop=(t == NT - 1))
            last.then_inc(S["rkp"], 1)
            pe.wait_ge(S["gdv"], NT)
            take(PC, ("gda", 1))
            for t in range(NT):
                last = turn(pt[PC][0:NE, P * t:P * (t + 1)], gate[:, t, :])
            last.then_inc(S["gdp"], 1)
            pe.wait_ge(S["rkv"], 1)
            pe.matmul(pt[PD][0:NE, 0:1], con[0:NE, C_TRI:C_TRI + NE], nbx[:, 0:1], start=True, stop=True).then_inc(S["cup"], 1)
            pe.wait_ge(S["cuv"], 1)
            pe.matmul(pt[PD][:, 512:512 + 2 * EXTRA + 1], ones[0:NE, :], blk[:, :], start=True, stop=True).then_inc(S["ovp"], 1)
            take(PA)
            take(PB)
            pe.wait_ge(s_b1, 32)
            pe.wait_ge(S["gda"], 1)
            for t in range(NT):
                for n in range(2):
                    acc = pt[(PA, PB)[t]][:, 512 * n:512 * (n + 1)]
                    pe.matmul(acc, ident, h3[:, t, 512 * n:512 * (n + 1)], start=True, stop=False)
                    last = pe.matmul(acc, gT[:, P * t:P * (t + 1)], be2[:, 512 * n:512 * (n + 1)], start=False, stop=False)
            last.then_inc(S["acci"], 1)
            take(PC)
            take(PD)
            pe.wait_ge(S["ovi"], 1)

            def gather():
                for t in range(NT):
                    for n in range(2):
                        last = pe.matmul(pt[PD][SLOTS * n:SLOTS * (n + 1), 0:512], sel[:, t, :],
                                         xn[:, t, 512 * n:512 * (n + 1)], start=(t == 0), stop=(t == NT - 1))
                last.then_inc(m_x, 1)

            def turn_block():
                for c in range(4):
                    last = turn(pt[PD][:, P * c:P * (c + 1)], xgn[:, P * c:P * (c + 1)])
                last.then_inc(m_xt, 1)

            def scatter(stop):
                for t in range(NT):
                    for n in range(2):
                        last = pe.matmul(pt[(PA, PB)[t]][:, 512 * n:512 * (n + 1)], gsc[:, n, t], ysb, start=False, stop=stop)
                return last

            pe.wait_ge(S["hn3"], NT)
            pe.wait_ge(m_sel, 1)
            gather()
            pe.wait_ge(m_xn, 1)
            turn_block()

            def block_of(it):
                pe.wait_ge(m_xT, it + 1)
                for b in range(2):
                    for g in range(2):
                        pe.matmul(pt[PC][SLOTS * g:SLOTS * (g + 1), 512 * b:512 * (b + 1)], ecol,
                                  be1[:, D * b + 512 * g:D * b + 512 * (g + 1)], start=True, stop=False)
                for k in range(KD):
                    pe.wait_ge(s_w1[k], 16 * (it + 1))
                    for b in range(2):
                        for g in range(2):
                            last = pe.matmul(pt[PC][SLOTS * g:SLOTS * (g + 1), 512 * b:512 * (b + 1)], xT[:, k % 4, k // 4],
                                             w1[:, k, D * b + 512 * g:D * b + 512 * (g + 1)], start=False, stop=(k == KD - 1))
                    last.then_inc(m_w1u, 1)
                pe.wait_ge(m_sel, it + 2)
                gather()
                pe.wait_ge(m_selw, it + 1)
                pe.wait_ge(m_y, it + 1)
                for n in range(2):
                    for t in range(NT):
                        last = turn(pt[PD][:, 512 + P * (NT * n + t):512 + P * (NT * n + t + 1)],
                                    selw[:, t, SLOTS * (1 - n):SLOTS * (3 - n)])
                last.then_inc(m_st, 1)
                pe.wait_ge(m_gs, it + 1)
                scatter(False).then_inc(m_sc, 1)
                pe.wait_ge(m_act, it + 1)
                for c in range(4):
                    last = turn(pt[PC][:, P * c:P * (c + 1)], hact[:, P * c:P * (c + 1)])
                last.then_inc(m_at, 1)
                pe.wait_ge(m_xn, it + 2)
                turn_block()
                pe.wait_ge(m_hT, it + 1)
                pe.wait_ge(m_gs, it + 2)
                for k in range(KD):
                    if k % 2 == 0:
                        pe.wait_ge(s_w2[k // 2], 16 * (it + 1))
                    for n in range(2):
                        last = pe.matmul(pt[PD][SLOTS * n:SLOTS * (n + 1), 512:1024], hT[:, k % 4, k // 4],
                                         w2[:, k, 512 * n:512 * (n + 1)], start=(k == 0), stop=(k == KD - 1))
                    if k % 2:
                        last.then_inc(m_w2u, 1)

            with pe.Fori(0, NE) as e:
                block_of(e)
            n_extra = pe.value_load(idx[0:1, NE + EXTRA + 1:NE + EXTRA + 2], min_val=0, max_val=EXTRA)
            with pe.Fori(0, EXTRA) as j:
                with pe.If(n_extra > j):
                    block_of(NE + j)
            pe.wait_ge(m_y, NE + 1 + n_extra)
            pe.wait_ge(m_gs, NE + 1 + n_extra)
            scatter(True).then_inc(S["accd"], 1)

        @block.scalar
        def _(act):
            def square(src, scratch, col):
                act.activation(scratch, src, ACT.Square, accum_out=st[:, col:col + 1]).then_inc(S["sumsq"], 1)

            def root(src, dst, n, width, count=None):
                if count is not None:
                    act.wait_ge(S["sumsq"], count)
                act.activation(st[:, dst:dst + n], st[:, src:src + n], ACT.Sqrt, scale=1.0 / width,
                               bias=st[:, 60:61]).then_inc(S["root"], 1)

            def copy(dst, src):
                return act.activation(dst, src, ACT.Copy)

            def unit(u, pat=None, **kw):
                return pt[u][:, :] if pat is None else pt[u][:, :].rearrange(pat, **kw)

            act.wait_ge(s_x, 16)
            for t in range(NT):
                square(h3[:, t], hnT_flat[:, t * D:(t + 1) * D], t)
            act.wait_ge(S["epsv"], 1)
            root(0, 2, NT, D, NT)
            act.wait_ge(s_small, 48)
            act.activation(prep[:, 258:260], prep[:, 256:258], ACT.Exp).then_inc(S["dtl"], 1)
            act.wait_ge(S["lamx"], 1)
            act.activation(st[:, 43:45], st[:, 41:43], ACT.Exp).then_inc(S["laml"], 1)
            act.wait_ge(S["mag"], 1)
            act.activation(prep[:, 640:768], prep[:, 384:512], ACT.Exp)
            act.wait_ge(S["red"], 1)
            act.activation(prep[:, 1024:1152], prep[:, 896:1024], ACT.Sin)
            act.activation(prep[:, 1280:1408], prep[:, 1152:1280], ACT.Sin).then_inc(S["trig"], 1)

            slab_done(act, "u")
            copy(usb, unit(PA, "p (t n) -> p t n", t=NT)).then_inc(S["usb"], 1)
            act.wait_ge(S["usb"], 1)
            for t in range(NT):
                for j in range(4):
                    act.dma_start(u4[32 * j + 16 * t:32 * j + 16 * t + 16], usb[:, t, P * j:P * (j + 1)]).then_inc(s_u4, 16)
            act.wait_ge(S["tabp"], 1)
            copy(wi_[:, 0:512], pt[PC][:, 0:512])
            copy(lam8[:, 0:2 * G], pt[PC][:, 512:512 + 2 * G]).then_inc(S["taba"], 1)
            act.wait_ge(S["ctp"], 1)
            copy(ct_[:, 0:512], pt[PD][:, 0:512])
            act.activation(ct_[:, 512:1024], pt[PD][:, 512:1024], ACT.Copy, scale=-1.0).then_inc(S["cta"], 1)
            act.wait_ge(s_u4, 8 * 16)
            copy(u5, u4.rearrange("p t (a h) -> p a t h", a=8)).then_inc(S["u4r"], 1)
            slab_done(act, "v")
            copy(vn, unit(PB, "p (t n) -> p t n", t=NT)).then_inc(S["vev"], 1)
            act.wait_ge(S["utp"], 1)
            copy(uT_[:, :], unit(PC)).then_inc(S["uta"], 1)
            slab_done(act, "ga0")
            act.wait_ge(S["tabp"], 1)
            copy(a1[:, 0:1024], unit(PA)).then_inc(S["gates"], 1)
            act.wait_ge(S["qkp"], 1)
            copy(t2[:, 1024:2048], unit(PD)).then_inc(S["qka"], 1)
            act.wait_ge(S["qkp"], 2)
            act.wait_ge(S["kz"], 1)
            copy(t3[0:DH, 0:1024], pt[PC][0:DH, :])
            copy(big[DH:P, 0:1024], pt[PC][DH:P, :]).then_inc(S["qka"], 1)

            def exps(h):
                act.wait_ge(S["smx"], h + 1)
                if h:
                    act.wait_ge(S["wtp"], h)
                for c in range(2):
                    for t in range(NT):
                        i = 2 * c + t
                        act.activation(prob[:, c, t], pt[PD][:, 512 * c + L * t:512 * c + L * (t + 1)], ACT.Exp,
                                       bias=sm[:, i:i + 1], scale=DH ** -0.5, accum_out=sm[:, 8 + i:9 + i]).then_inc(S["pex"], 1)

            def copy_probs(h):
                act.wait_ge(S["wtp"], h + 1)
                if h >= 2:
                    act.wait_ge(S["pvp"], h - 1)
                copy(wT[:, h % 2], pt[PC][:, 0:512].rearrange("p (k l) -> p k l", k=NT)).then_inc(S["wta"], 1)

            exps(0)
            slab_done(act, "ga1")
            copy(a1[:, 1024:2048], unit(PB)).then_inc(S["gates"], 1)
            copy_probs(0)
            exps(1)
            slab_done(act, "gs0")
            copy(a2[:, 0:1024], unit(PB)).then_inc(S["gates"], 1)
            copy_probs(1)
            exps(2)
            slab_done(act, "gs1")
            copy(a2[:, 1024:2048], unit(PB)).then_inc(S["gates"], 1)
            copy_probs(2)
            exps(3)
            act.wait_ge(S["kp"], 1)
            copy(t1[:, 1024:2048], unit(PB)).then_inc(S["kta"], 1)
            act.wait_ge(S["kta"], 1)
            for j in range(4):
                for d in range(2):
                    act.dma_start(taps_dram[8 * j:8 * j + 8, :, 144 * d:144 * d + P].rearrange("a h n -> h a n"),
                                  taps[32 * j + HG * d:32 * j + HG * (d + 1)]).then_inc(s_tapw, 16)
            copy_probs(3)
            for r in range(0, 8, 2):
                act.wait_ge(S["ltp"], r + 1)
                copy(ring[:, 8192 + 1024 * r:8192 + 1024 * (r + 1)], unit(PB)).then_inc(S["lta"], 1)
            act.wait_ge(S["ssq"], 1)
            root(20, 46, 8, 2 * DH)
            act.wait_ge(S["zp"], 1)
            act.wait_ge(S["k0p"], 1)
            act.wait_ge(S["kse"], 1)
            copy(ring[:, 22528:23552], unit(PB)).then_inc(S["zka"], 1)
            for i, u in enumerate((PB, PD)):
                act.wait_ge(S["ztp"], i + 1)
                for c in range(2):
                    src = pt[u][0:NS, :].rearrange("p (a c j k) -> p c k j a", a=4, c=2, j=4)[:, c]
                    dst = zst[0:NS, :, c, :].rearrange("p k (j a) -> p k j a", j=4)[:, :, :, 4 * i:4 * i + 4]
                    copy(dst, src).then_inc(S["zva"], 1)
            act.wait_ge(S["otp"], 1)
            act.activation(wi_[:, :], unit(PC), ACT.Copy, scale=st[:, 33:34]).then_inc(S["ota"], 1)
            act.wait_ge(s_mem, 16)
            for t in range(NT):
                square(mn[:, t], t2[:, t * D:(t + 1) * D], 4 + t)
            root(4, 6, NT, D, 2 * NT)
            act.activation(a1[:, :], a1[:, :], ACT.Sigmoid)
            act.activation(a2[:, :], a2[:, :], ACT.Sigmoid).then_inc(S["sgm"], 1)
            for i, u in enumerate((PC, PD)):
                slab_done(act, f"mk{i}")
                copy(t2[:, 1024 * i:1024 * (i + 1)], unit(u)).then_inc(S["mka"], 1)
            slab_done(act, "mv0")
            copy(mn[:, :, 0:512], unit(PA, "p (t n) -> p t n", t=NT)).then_inc(S["mva"], 1)
            act.wait_ge(S["scan"], 1)
            for c in range(2):
                copy(enter[0:NS, c, :, 1:NC], xst[0:NS, 0:NC - 1, c, :].rearrange("p k g -> p g k")).then_inc(S["enta"], 1)
            act.wait_ge(S["yp"], 1)
            act.activation(y4, unit(PB, "p (a t h) -> p t a h", a=8, t=TC), ACT.Gelu_apprx_tanh).then_inc(S["ygel"], 1)
            slab_done(act, "mv1")
            copy(mn[:, :, 512:1024], unit(PC, "p (t n) -> p t n", t=NT)).then_inc(S["mva"], 1)
            act.wait_ge(S["ytp"], 1)
            for j in range(4):
                last = copy(yT[:, j].rearrange("p (k t) -> p t k", t=TC),
                            unit(PD, "p (t j k) -> p j t k", t=TC, j=4)[:, j])
            last.then_inc(S["yta"], 1)
            slab_done(act, "gl1")
            act.activation(glu_flat, unit(PD), ACT.Sigmoid).then_inc(S["gls"], 1)
            act.wait_ge(S["mh"], 2)
            for t in range(NT):
                square(h3[:, t], hnT_flat[:, t * D:(t + 1) * D], 8 + t)
            root(8, 10, NT, D, 3 * NT)
            for i, u in enumerate((PC, PD)):
                slab_done(act, f"xq{i}")
                copy(a2[:, 1024 * i:1024 * (i + 1)], unit(u)).then_inc(S["xqa"], 1)
            for i, u in enumerate((PA, PB)):
                act.wait_ge(S["xmx"], i + 1)
                for hh in range(2):
                    for t in range(NT):
                        n = 2 * hh + t
                        act.activation(p2[:, 2 * i + hh, t], pt[u][:, 512 * hh + L * t:512 * hh + L * (t + 1)], ACT.Exp,
                                       bias=sm[:, 4 * i + n:4 * i + n + 1], scale=(D // HEADS) ** -0.5,
                                       accum_out=sm[:, 8 + 4 * i + n:9 + 4 * i + n]).then_inc(S["xex"], 1)
            for i, u in enumerate((PC, PD)):
                act.wait_ge(S["xtp"], i + 1)
                copy(t1[:, 1024 * i:1024 * (i + 1)], unit(u)).then_inc(S["xta"], 1)
            for i, u in enumerate((PA, PB)):
                act.wait_ge(S["xop"], i + 1)
                copy(hnt[:, 1024 * i:1024 * (i + 1)], unit(u)).then_inc(S["xoa"], 1)
            act.wait_ge(S["xh"], 2)
            for t in range(NT):
                square(h3[:, t], a1[:, 0:D], 12 + t)
                act.wait_ge(S["sumsq"], 3 * NT + t + 1)
            root(12, 14, NT, D)
            for t in range(NT):
                act.wait_ge(S["msk"], t + 1)
                act.activation(gate[:, t, :], lg[:, t, :], ACT.Exp, bias=pse[:, 0, t:t + 1]).then_inc(S["lex"], 1)
            act.wait_ge(S["gdp"], 1)
            copy(gT, pt[PC][0:NE, 0:L]).then_inc(S["gda"], 1)
            act.wait_ge(S["ovi"], 1)
            act.activation(ysb, con[:, 0:1].to_broadcast([P, 512]), ACT.Copy, scale=0.0).then_inc(m_y, 1)
            act.activation(part(4608, 512), con[:, 0:1].to_broadcast([P, 512]), ACT.Copy, scale=0.0).then_inc(m_gs, 1)

            def block_of(it):
                act.wait_ge(m_g2, it + 1)
                act.activation(hsg, hg, ACT.Sigmoid, scale=GATE_ALPHA).then_inc(m_sig, 1)
                act.wait_ge(m_st, it + 1)
                act.wait_ge(m_sc, it + 1)
                copy(part(4608, 512), pt[PD][:, 512:1024]).then_inc(m_gs, 1)
                act.wait_ge(m_at, it + 1)
                copy(part(3584, 512), pt[PC][:, 0:512]).then_inc(m_hT, 1)
                act.wait_ge(m_w2u, (KD // 2) * (it + 1))
                copy(ysb, pt[PD][:, 512:1024]).then_inc(m_y, 1)

            with act.Fori(0, NE) as e:
                block_of(e)
            n_extra = act.value_load(idx[0:1, NE + EXTRA + 1:NE + EXTRA + 2], min_val=0, max_val=EXTRA)
            with act.Fori(0, EXTRA) as j:
                with act.If(n_extra > j):
                    block_of(NE + j)
            act.wait_ge(S["accd"], 1)
            for t in range(NT):
                square(pt[(PA, PB)[t]][:, :], a1[:, 0:D], 16 + t)
                act.wait_ge(S["sumsq"], 4 * NT + t + 1)
            root(16, 18, NT, D)

        @block.vector
        def _(dve):
            steps = [0]

            def link(ins):
                steps[0] += 1
                ins.then_inc(s_v, 1)
                dve.wait_ge(s_v, steps[0])

            def bc(x, shape):
                return x.to_broadcast(shape)

            def normed(norm, src, dst):
                col = 4 * norm
                dve.wait_ge(S["root"], (1, 3, 4, 5)[norm])
                link(dve.reciprocal(st[:, col + 2:col + 2 + NT], st[:, col + 2:col + 2 + NT]))
                for t in range(NT):
                    dve.tensor_scalar(dst[:, t], src[:, t], st[:, col + 2 + t:col + 3 + t], None, ALU.mult).then_inc(S["normed"], 1)

            def gained(norm, units, dst):
                for i, u in enumerate(units):
                    dve.wait_ge(S["tokp"], 2 * norm + i + 1)
                    g = gains[:, norm * KD + 4 * i:norm * KD + 4 * i + 4].unsqueeze(2).to_broadcast([P, 4, L])
                    dve.tensor_tensor(dst[:, 4 * i:4 * i + 4], pt[u][:, :].rearrange("p (k l) -> p k l", k=4), g,
                                      ALU.mult).then_inc(S["tokv"], 1)

            dve.memset(st[:, 60:61], EPS).then_inc(S["epsv"], 1)
            normed(0, h3, xn)
            dve.wait_ge(S["graw"], 1)
            link(dve.tensor_copy(gains[:, :], pt[PA][:, 0:4 * KD]))
            gained(0, (PC, PD), hnT)

            dve.wait_ge(s_lamb, 64)
            for i in range(2):
                last = dve.tensor_tensor_reduce(lamb[:, 2 * i * DH:(2 * i + 1) * DH], lamb[:, 2 * i * DH:(2 * i + 1) * DH],
                                                lamb[:, (2 * i + 1) * DH:(2 * i + 2) * DH], 1.0, 0.0, ALU.mult, ALU.add,
                                                st[:, 41 + i:42 + i])
            last.then_inc(S["lamx"], 1)

            are, aim, dt = prep[:, 0:128], prep[:, 128:256], prep[:, 258:260]
            ad, th, mag, kk, red, sn, ab, cs = (prep[:, 384 + 128 * i:512 + 128 * i] for i in range(8))
            d2 = lambda x: x.rearrange("p (d m) -> p d m", d=2)
            dve.wait_ge(s_small, 48)
            dve.wait_ge(S["dtl"], 1)
            dtb = dt.unsqueeze(2).to_broadcast([G, 2, NS])
            dve.tensor_tensor(d2(ad), d2(are), dtb, ALU.mult).then_inc(S["mag"], 1)
            link(dve.tensor_tensor(d2(th), d2(aim), dtb, ALU.mult))
            link(dve.tensor_scalar(kk, th, 1.0 / TWO_PI, ROUND, ALU.mult, ALU.add))
            link(dve.tensor_scalar(kk, kk, ROUND, None, ALU.subtract))
            link(dve.scalar_tensor_tensor(red, kk, -PI_A, th, ALU.mult, ALU.add))
            link(dve.scalar_tensor_tensor(red, kk, -PI_B, red, ALU.mult, ALU.add))
            link(dve.scalar_tensor_tensor(red, kk, -PI_C, red, ALU.mult, ALU.add))
            link(dve.tensor_scalar(red, red, 3.1415925, -3.1415925, ALU.min, ALU.max))
            link(dve.scalar_tensor_tensor(ab, red, -1.0, red, ALU.mult, ALU.min))
            dve.tensor_scalar(ab, ab, TWO_PI / 4, None, ALU.add).then_inc(S["red"], 1)
            dve.wait_ge(S["trig"], 1)
            pwn = prep[:, 2048:4096].rearrange("p (c t m) -> p c t m", c=2, t=TC)
            link(dve.tensor_tensor(pwn[:, 0, 0], mag, cs, ALU.mult))
            link(dve.tensor_tensor(pwn[:, 1, 0], mag, sn, ALU.mult))

            def powers(a, b, n):
                tm = prep[:, 4608:4608 + n * P].rearrange("p (t m) -> p t m", t=n)
                pr, pi = (pwn[:, c, b - 1:b].to_broadcast([G, n, P]) for c in range(2))
                xr, xi = pwn[:, 0, 0:n], pwn[:, 1, 0:n]
                zr, zi = pwn[:, 0, a:a + n], pwn[:, 1, a:a + n]
                link(dve.tensor_tensor(tm, xr, pr, ALU.mult))
                link(dve.tensor_tensor(zr, xi, pi, ALU.mult))
                link(dve.tensor_tensor(zr, tm, zr, ALU.subtract))
                link(dve.tensor_tensor(tm, xr, pi, ALU.mult))
                link(dve.tensor_tensor(zi, xi, pr, ALU.mult))
                link(dve.tensor_tensor(zi, tm, zi, ALU.add))

            powers(1, 1, 1)
            powers(2, 2, 2)
            powers(4, 4, 4)
            nr, den, t0 = prep[:, 5632:5760], prep[:, 5760:5888], prep[:, 5888:6016]
            cf = prep[:, 4096:4352].rearrange("p (c m) -> p c m", c=2)
            link(dve.tensor_scalar(nr, pwn[:, 0, 0], 1.0, None, ALU.subtract))
            link(dve.tensor_tensor(den, are, are, ALU.mult))
            link(dve.tensor_tensor(t0, aim, aim, ALU.mult))
            link(dve.tensor_tensor(den, den, t0, ALU.add))
            link(dve.reciprocal(den, den))
            for c, (x, y, op) in enumerate(((nr, pwn[:, 1, 0], ALU.add), (pwn[:, 1, 0], nr, ALU.subtract))):
                link(dve.tensor_tensor(cf[:, c], x, are, ALU.mult))
                link(dve.tensor_tensor(t0, y, aim, ALU.mult))
                link(dve.tensor_tensor(cf[:, c], cf[:, c], t0, op))
                link(dve.tensor_tensor(cf[:, c], cf[:, c], den, ALU.mult))
            dve.tensor_copy(pw[:, :, :, 0:NS], pwn[:, :, :, 0:NS])
            for c in range(2):
                last = dve.tensor_copy(pw[:, c, :, NS:P], pwn[:, c, ::-1, NS:P])
            last.then_inc(S["tabsrc"], 1)

            cos = con[:, C_COS:C_COS + NT * 32].rearrange("p (t i) -> p t i", t=NT)
            sin = con[:, C_SIN:C_SIN + NT * 32].rearrange("p (t i) -> p t i", t=NT)
            dve.wait_ge(s_con, 16)
            rt1 = t3[:, 0:512].rearrange("p (c f i) -> p c f i", c=8, f=2)
            rt2 = t3[:, 512:1024].rearrange("p (c f i) -> p c f i", c=8, f=2)
            for n, slab, u, dst in ((1, "q", PB, qn), (2, "k", PA, kn)):
                slab_done(dve, slab)
                for t in range(NT):
                    x = pt[u][:, 512 * t:512 * (t + 1)].rearrange("p (c f i) -> p c f i", c=8, f=2)
                    y = dst[:, t].rearrange("p (c f i) -> p c f i", c=8, f=2)
                    cb = cos[:, t].unsqueeze(1).unsqueeze(1).to_broadcast([P, 8, 2, 32])
                    sb_ = sin[:, t].unsqueeze(1).unsqueeze(1).to_broadcast([P, 8, 2, 32])
                    dve.tensor_tensor(rt1, x, cb, ALU.mult)
                    link(dve.tensor_tensor(rt2, x, sb_, ALU.mult))
                    dve.tensor_tensor(y[:, :, 0], rt1[:, :, 0], rt2[:, :, 1], ALU.subtract)
                    last = dve.tensor_tensor(y[:, :, 1], rt1[:, :, 1], rt2[:, :, 0], ALU.add)
                    if t < NT - 1:
                        link(last)
                last.then_inc(S["rope"], 1)
                dve.wait_ge(S["rope"], n)
            dve.memset(big[0:DH, 0:1024], 0.0)
            dve.memset(t3[DH:P, 0:1024], 0.0).then_inc(S["kz"], 1)

            dve.wait_ge(S["taba"], 1)
            for c in range(2):
                dve.tensor_copy(ipow[0:NS, c, 0:7], wpow[0:NS, c, 6::-1])
                dve.tensor_copy(ipow[NS:P, c, 1:8], wpow[NS:P, c, 7:0:-1])
                dve.memset(ipow[0:NS, c, 7], 1.0 - c)
                link(dve.memset(ipow[NS:P, c, 0], 1.0 - c))
            dve.wait_ge(s_braw, 64)
            cfr, cfi = (lam8[:, c * G:(c + 1) * G].unsqueeze(2).to_broadcast([P, G, HG]) for c in range(2))
            link(dve.tensor_tensor(tmp_v, braw[:, 0], cfr, ALU.mult))
            link(dve.tensor_tensor(bbar[:, 0], braw[:, 1], cfi, ALU.mult))
            link(dve.tensor_tensor(bbar[:, 0], tmp_v, bbar[:, 0], ALU.subtract))
            link(dve.tensor_tensor(tmp_v, braw[:, 1], cfr, ALU.mult))
            link(dve.tensor_tensor(bbar[:, 1], braw[:, 0], cfi, ALU.mult))
            link(dve.tensor_tensor(bbar[:, 1], tmp_v, bbar[:, 1], ALU.add))
            link(dve.memset(ring[:, 20480:22528], 0.0))
            for c in range(2):
                dve.tensor_copy(bsplit[0:NS, c, :, 1], bbar[0:NS, c])
                last = dve.tensor_copy(bsplit[NS:P, c, :, 0], bbar[NS:P, c])
            last.then_inc(S["bspl"], 1)
            l8 = lam8[:, 0:128].rearrange("p (f c g) -> p f c g", f=2, c=2)
            for lo, hi, t in ((0, NS, TC - 1), (NS, P, 0)):
                dve.tensor_copy(l8[lo:hi, 0, 0], wpow[lo:hi, 0, t])
                dve.tensor_copy(l8[lo:hi, 1, 1], wpow[lo:hi, 0, t])
                dve.tensor_copy(l8[lo:hi, 0, 1], wpow[lo:hi, 1, t])
                link(dve.tensor_scalar(l8[lo:hi, 1, 0], wpow[lo:hi, 1, t], -1.0, None, ALU.mult))
            dve.wait_ge(S["laml"], 1)
            dve.wait_ge(s_dskip, 32)
            link(dve.tensor_tensor(st[:, 45:46], st[:, 44:45], st[:, 43:44], ALU.subtract))
            link(dve.tensor_scalar(st[:, 45:46], st[:, 45:46], LAMBDA_INIT, None, ALU.subtract))
            link(dve.tensor_scalar(st[:, 33:34], st[:, 32:33], 1.0 - LAMBDA_INIT, None, ALU.mult))

            def row_max(h):
                dve.wait_ge(S["scp"], h + 1)
                link(dve.tensor_reduce(sm[:, 4:8], pt[PD][:, :].rearrange("p (i l) -> p i l", i=4), AX.X, ALU.max))
                dve.tensor_scalar(sm[:, 0:4], sm[:, 4:8], -DH ** -0.5, None, ALU.mult).then_inc(S["smx"], 1)

            def weigh(h):
                dve.wait_ge(S["pex"], 4 * (h + 1))
                link(dve.reciprocal(sm[:, 16:20], sm[:, 8:12]))
                link(dve.tensor_scalar(sm[:, 20:22], sm[:, 18:20], st[:, 45:46], None, ALU.mult))
                for t in range(NT):
                    link(dve.tensor_scalar(prob[:, 1, t], prob[:, 1, t], sm[:, 20 + t:21 + t], None, ALU.mult))
                for t in range(NT):
                    last = dve.scalar_tensor_tensor(prob[:, 0, t], prob[:, 0, t], sm[:, 16 + t:17 + t], prob[:, 1, t],
                                                    ALU.mult, ALU.add)
                last.then_inc(S["pwv"], 1)

            def way_in(times):
                for t in times:
                    ir, ii = (ipow[:, c, t, :].unsqueeze(2).to_broadcast([P, G, HG]) for c in range(2))
                    zr, zi = s5b[:, :, 0, t], s5b[:, :, 1, t]
                    link(dve.tensor_tensor(tmp_v, bbar[:, 0], ir, ALU.mult))
                    link(dve.tensor_tensor(zr, bbar[:, 1], ii, ALU.mult))
                    link(dve.tensor_tensor(zr, tmp_v, zr, ALU.subtract))
                    link(dve.tensor_tensor(tmp_v, bbar[:, 1], ir, ALU.mult))
                    link(dve.tensor_tensor(zi, bbar[:, 0], ii, ALU.mult))
                    last = dve.tensor_tensor(zi, tmp_v, zi, ALU.add)
                    if t < TC - 1:
                        link(last)
                    else:
                        last.then_inc(S["bp"], 1)
                        dve.wait_ge(S["bp"], 1)

            dve.wait_ge(S["tabp"], 1)
            for h, times in enumerate((range(0, 3), range(3, 6), range(6, TC), ())):
                row_max(h)
                weigh(h)
                way_in(times)
            dve.wait_ge(S["k0p"], 1)
            k0 = tmp_v.rearrange("p (j a) h -> p j a h", j=4)
            bm = con[:, C_BLK:C_BLK + P].rearrange("p (a h) -> p a h", a=8).unsqueeze(1).to_broadcast([P, 4, 8, HG])
            link(dve.tensor_tensor(k0, pt[PC][:, 0:512].rearrange("p (j a h) -> p j a h", j=4, a=8), bm, ALU.mult))
            k0s = lamb[:, 0:64].rearrange("p (j h) -> p j h", j=4)
            link(dve.tensor_reduce(k0s, k0.rearrange("p j a h -> p j h a"), AX.X, ALU.add))
            for j in range(4):
                last = dve.scalar_tensor_tensor(tap0[:, j], con[:, C_M16:C_M16 + HG], st[:, 36 + j:37 + j],
                                                k0s[:, j], ALU.mult, ALU.add)
            last.then_inc(S["kse"], 1)
            for r in range(1, 8, 2):
                dve.wait_ge(S["ltp"], r + 1)
                dve.tensor_copy(ring[:, 8192 + 1024 * r:8192 + 1024 * (r + 1)], pt[PD][:, :]).then_inc(S["ltv"], 1)
            dve.wait_ge(S["zp"], 2)
            dve.tensor_copy(ring[:, 23552:24576], pt[PD][:, :]).then_inc(S["zkv"], 1)
            dve.wait_ge(S["pvp"], HEADS)
            dve.wait_ge(S["wtp"], HEADS)
            dve.wait_ge(s_tapw, 8 * 16)
            dve.tensor_copy(t1[:, 1024:2048], pt[PA][:, :]).then_inc(S["on"], 1)
            dve.wait_ge(S["on"], 1)
            link(dve.tensor_tensor(t1[:, 0:1024], t1[:, 1024:2048], t1[:, 1024:2048], ALU.mult))
            dve.tensor_reduce(st[:, 20:28], t1[:, 0:1024].rearrange("p (i e) -> p i e", i=8), AX.X, ALU.add).then_inc(S["ssq"], 1)
            dve.wait_ge(S["root"], 2)
            link(dve.reciprocal(st[:, 46:54], st[:, 46:54]))
            dve.tensor_tensor(on, on, st[:, 46:54].rearrange("p (t h) -> p t h", t=NT).unsqueeze(3)
                              .to_broadcast([P, NT, HEADS, P]), ALU.mult).then_inc(S["on"], 1)
            for i, u in enumerate((PB, PD)):
                dve.wait_ge(S["ztp"], i + 1)
                for c in range(2):
                    src = pt[u][NS:P, :].rearrange("p (a c j k) -> p c k j a", a=4, c=2, j=4)[:, c]
                    dst = zst[NS:P, :, c, :].rearrange("p k (j a) -> p k j a", j=4)[:, :, :, 4 * i:4 * i + 4]
                    dve.tensor_copy(dst, src[:, ::-1]).then_inc(S["zvv"], 1)
            normed(1, mn, mn)
            gained(1, (PA, PB), memT)
            dve.wait_ge(S["zva"], 4)
            dve.wait_ge(S["zvv"], 4)
            link(dve.tensor_copy(xst[:, 0], zst[:, 0]))
            prod = lam8[:, 128:256].rearrange("p (f c g) -> p f c g", f=2, c=2)
            for k in range(1, NC):
                link(dve.tensor_tensor(prod, l8, xst[:, k - 1].unsqueeze(2).to_broadcast([P, 2, 2, G]), ALU.mult))
                link(dve.tensor_tensor(prod[:, 0], prod[:, 0], prod[:, 1], ALU.add))
                last = dve.tensor_tensor(xst[:, k], prod[:, 0], zst[:, k], ALU.add)
                if k < NC - 1:
                    link(last)
            last.then_inc(S["scan"], 1)
            dve.wait_ge(S["scan"], 1)
            dve.memset(enter[0:NS, :, :, 0:1], 0.0)
            dve.memset(enter[NS:P, :, :, NC - 1:NC], 0.0)
            for c in range(2):
                last = dve.tensor_copy(enter[NS:P, c, :, 0:NC - 1],
                                       xst[NS:P, NC - 2::-1, c, :].rearrange("p k g -> p g k"))
            last.then_inc(S["entv"], 1)
            dve.wait_ge(S["sgm"], 1)

            def gate_attention(i, u):
                slab_done(dve, f"ba{i}")
                dve.tensor_tensor(a1[:, 1024 * i:1024 * (i + 1)], a1[:, 1024 * i:1024 * (i + 1)], pt[u][:, :],
                                  ALU.mult).then_inc(S["bav"], 1)

            gate_attention(0, PA)
            dve.wait_ge(S["gls"], 1)
            dve.tensor_tensor(uT_[:, :], glu_flat, pt[PC][:, :], ALU.mult).then_inc(S["osv"], 1)
            gate_attention(1, PB)
            for i, u in enumerate((PA, PC)):
                slab_done(dve, f"bs{i}")
                dve.wait_ge(S["bav"], i + 1)
                dve.tensor_tensor(a2[:, 1024 * i:1024 * (i + 1)], a2[:, 1024 * i:1024 * (i + 1)], pt[u][:, :],
                                  ALU.mult).then_inc(S["bsv"], 1)
                dve.wait_ge(S["bsv"], 2 * i + 1)
                dve.tensor_tensor(a1[:, 1024 * i:1024 * (i + 1)], a1[:, 1024 * i:1024 * (i + 1)],
                                  a2[:, 1024 * i:1024 * (i + 1)], ALU.add).then_inc(S["bsv"], 1)

            def residual(prefix, units, done):
                for i, u in enumerate(units):
                    slab_done(dve, f"{prefix}{i}")
                    hs = h3[:, :, 512 * i:512 * (i + 1)]
                    dve.tensor_tensor(hs, hs, pt[u][:, :].rearrange("p (t n) -> p t n", t=NT), ALU.add).then_inc(S[done], 1)
                dve.wait_ge(S[done], 2)

            residual("mx", (PB, PD), "mh")
            normed(2, h3, xn)
            gained(2, (PA, PB), hnT)
            for i, u in enumerate((PA, PB)):
                dve.wait_ge(S["xsp"], i + 1)
                link(dve.tensor_reduce(sm[:, 24:28], pt[u][:, :].rearrange("p (i l) -> p i l", i=4), AX.X, ALU.max))
                dve.tensor_scalar(sm[:, 4 * i:4 * i + 4], sm[:, 24:28], -(D // HEADS) ** -0.5, None, ALU.mult).then_inc(S["xmx"], 1)
                dve.wait_ge(S["xmx"], i + 1)
            for i in range(2):
                dve.wait_ge(S["xex"], 4 * (i + 1))
                link(dve.reciprocal(sm[:, 16 + 4 * i:20 + 4 * i], sm[:, 8 + 4 * i:12 + 4 * i]))
                for n in range(4):
                    x = p2[:, 2 * i + n // 2, n % 2]
                    last = dve.tensor_scalar(x, x, sm[:, 16 + 4 * i + n:17 + 4 * i + n], None, ALU.mult)
                last.then_inc(S["xpn"], 1)
            residual("xo", (PC, PD), "xh")
            normed(3, h3, xn)
            gained(3, (PA, PB), hnT)

            dve.wait_ge(S["lgp"], 1)
            dve.tensor_tensor(lg, pt[PD][:, 0:NT * NE].rearrange("p (t e) -> p t e", t=NT),
                              brt.unsqueeze(1).to_broadcast([P, NT, NE]), ALU.add).then_inc(S["lgv"], 1)
            dve.wait_ge(S["lgv"], 1)
            for t in range(NT):
                link(dve.max(top8[:, t], lg[:, t]))
                link(dve.tensor_scalar(pse[:, 0, t:t + 1], top8[:, t, 0:1], -1.0, None, ALU.mult))
                link(dve.memset(top8[:, t, TOPK:8], 3.0e38))
                link(dve.match_replace(rep[:, t], top8[:, t], lg[:, t], -3.0e38))
                dve.tensor_tensor(msk[:, t], lg[:, t], rep[:, t], ALU.not_equal).then_inc(S["msk"], 1)
                dve.wait_ge(S["msk"], t + 1)
            for t in range(NT):
                dve.wait_ge(S["lex"], t + 1)
                link(dve.tensor_tensor(gate[:, t], gate[:, t], msk[:, t], ALU.mult))
                link(dve.tensor_reduce(pse[:, 1, t:t + 1], gate[:, t], AX.X, ALU.add))
                link(dve.reciprocal(pse[:, 1, t:t + 1], pse[:, 1, t:t + 1]))
                dve.tensor_scalar(gate[:, t], gate[:, t], pse[:, 1, t:t + 1], None, ALU.mult).then_inc(S["gdv"], 1)
            dve.wait_ge(S["rkp"], 1)
            cnt = pt[PD][0:NE, 512:513]
            link(dve.tensor_scalar(nbx[:, 0:1], cnt, float(SLOTS), None, ALU.is_gt))
            for b in range(2, MAXB):
                link(dve.scalar_tensor_tensor(nbx[:, 0:1], cnt, float(SLOTS * b), nbx[:, 0:1], ALU.is_gt, ALU.add))
            link(dve.scalar_tensor_tensor(posn, pt[PD][:, 0:NT * NE].rearrange("p (t e) -> p t e", t=NT), 1.0, msk,
                                          ALU.add, ALU.mult))
            dve.tensor_scalar(posn, posn, 1.0, None, ALU.subtract).then_inc(S["rkv"], 1)
            dve.wait_ge(S["rkv"], 1)
            dve.wait_ge(S["cup"], 1)
            link(dve.tensor_copy(nbx[:, 1:2], pt[PD][0:NE, 0:1]))
            link(dve.tensor_scalar(blk[:, 0:EXTRA], con[0:NE, C_IOTA:C_IOTA + EXTRA], nbx[:, 1:2], None, ALU.is_ge))
            link(dve.tensor_scalar(blk[:, EXTRA:2 * EXTRA], blk[:, 0:EXTRA], nbx[:, 0:1], None, ALU.mult))
            dve.tensor_copy(blk[:, 2 * EXTRA:2 * EXTRA + 1], nbx[:, 0:1]).then_inc(S["cuv"], 1)
            dve.wait_ge(S["ovp"], 1)
            link(dve.memset(offs, 0.0))
            link(dve.memset(idx[:, :], 0))
            tab = pt[PD][:, 512:512 + 2 * EXTRA + 1]
            link(dve.tensor_tensor(offs[:, NE:NE + EXTRA], con[:, C_IOTA:C_IOTA + EXTRA], tab[:, EXTRA:2 * EXTRA], ALU.subtract))
            link(dve.tensor_scalar(offs[:, NE:NE + EXTRA], offs[:, NE:NE + EXTRA], 1.0, float(SLOTS), ALU.add, ALU.mult))
            link(dve.tensor_scalar(ovf[:, 0:EXTRA], tab[:, 0:EXTRA], float(NE - 1), None, ALU.min))
            dve.tensor_copy(idx[:, 0:NE], con[:, C_IOTA:C_IOTA + NE])
            dve.tensor_copy(idx[:, NE:NE + EXTRA], ovf[:, 0:EXTRA])
            dve.tensor_copy(idx[:, NE + EXTRA + 1:], tab[:, 2 * EXTRA:]).then_inc(S["ovi"], 1)
            dve.wait_ge(S["ovi"], 1)
            link(dve.memset(part(5200, NT * 3 * SLOTS), 0.0))
            io = con[:, C_IOTA:C_IOTA + SLOTS]

            def place(it, e, chain):
                dve.tensor_copy(pse[:, 1, :], gate[:, :, bass.ds(e, 1)].rearrange("p t e -> p (t e)"))
                chain(dve.tensor_tensor(pse[:, 0, :], posn[:, :, bass.ds(e, 1)].rearrange("p t e -> p (t e)"),
                                        offs[:, bass.ds(it, 1)].to_broadcast([P, NT]), ALU.subtract))
                for t in range(NT):
                    dve.tensor_scalar(sel[:, t], io, pse[:, 0, t:t + 1], None, ALU.is_equal)
                dve.tensor_copy(ecol, con[:, bass.ds(e, 1)].to_broadcast([P, SLOTS])).then_inc(m_sel, 1)

            place(0, 0, link)
            dve.wait_ge(m_x, 1)
            dve.tensor_copy(xgn, pt[PD][:, 0:512]).then_inc(m_xn, 1)
            dve.wait_ge(m_xt, 1)
            dve.tensor_copy(part(512, 512), pt[PD][:, 0:512]).then_inc(m_xT, 1)

            STEPS = 3

            def block_of(it):
                n = [0]

                def chain(ins):
                    n[0] += 1
                    ins.then_inc(m_v, 1)
                    dve.wait_ge(m_v, it * STEPS + n[0])

                for t in range(NT):
                    last = dve.tensor_scalar(selw[:, t, SLOTS:2 * SLOTS], io, pse[:, 0, t:t + 1], pse[:, 1, t:t + 1],
                                             ALU.is_equal, ALU.mult)
                last.then_inc(m_selw, 1)
                dve.wait_ge(m_selw, it + 1)
                dve.wait_ge(m_w1u, KD * it + 1)
                place(it + 1, dve.value_load(idx[0:1, bass.ds(it + 1, 1)], min_val=0, max_val=NE - 1), chain)
                dve.wait_ge(m_w1u, KD * (it + 1))
                dve.tensor_scalar(hg, pt[PC][:, 0:512], GATE_MAX, None, ALU.min).then_inc(m_g2, 1)
                chain(dve.tensor_scalar(hl, pt[PC][:, 512:1024], GATE_MAX, -GATE_MAX, ALU.min, ALU.max))
                chain(dve.scalar_tensor_tensor(hgl, hl, 1.0, hg, ALU.add, ALU.mult))
                dve.wait_ge(m_sig, it + 1)
                dve.tensor_tensor(hact, hgl, hsg, ALU.mult).then_inc(m_act, 1)
                dve.wait_ge(m_x, it + 2)
                dve.tensor_copy(xgn, pt[PD][:, 0:512]).then_inc(m_xn, 1)
                dve.wait_ge(m_xt, it + 2)
                dve.tensor_copy(part(512, 512), pt[PD][:, 0:512]).then_inc(m_xT, 1)
                assert n[0] == STEPS

            with dve.Fori(0, NE) as e:
                block_of(e)
            n_extra = dve.value_load(idx[0:1, NE + EXTRA + 1:NE + EXTRA + 2], min_val=0, max_val=EXTRA)
            with dve.Fori(0, EXTRA) as j:
                with dve.If(n_extra > j):
                    block_of(NE + j)

            dve.wait_ge(s_gf, 32)
            dve.wait_ge(S["root"], 6)
            link(dve.reciprocal(st[:, 18:18 + NT], st[:, 18:18 + NT]))
            for t in range(NT):
                dve.scalar_tensor_tensor(h3[:, t], pt[(PA, PB)[t]][:, :], st[:, 18 + t:19 + t], gfin, ALU.mult,
                                         ALU.mult).then_inc(S["gfin"], 1)


_INS = ["x", "mem", "norm_mix_g", "w_in", "lambda_q1", "lambda_k1", "lambda_q2", "lambda_k2", "subln_g",
        "ssm_a_re", "ssm_a_im", "ssm_log_dt", "ssm_b_re", "ssm_b_im", "ssm_c_re", "ssm_c_im", "ssm_d", "w_glu",
        "w_branch_attn", "w_branch_ssm", "w_mix_out", "norm_cross_g", "norm_mem_g", "w_xq", "w_xkv", "w_xo",
        "norm_ffn_g", "w_router", "b_router", "w_e1", "b_e1", "w_e2", "b_e2", "norm_final_g"]


def kernel(**inputs):
    import numpy as _np
    import concourse.bacc as _bacc
    from concourse import mybir as _mybir
    from concourse.bass_utils import run_bass_kernel_spmd as _run

    nc = _bacc.Bacc("TRN2", target_bir_lowering=False, num_devices=1)
    arrays, T = {}, {}
    for name in _INS:
        a = _np.ascontiguousarray(inputs[name])
        arrays[f"in_{name}"] = a
        T[name] = nc.dram_tensor(f"in_{name}", a.shape, _mybir.dt.from_np(a.dtype), kind="ExternalInput").ap()
    arrays["consts"] = constants()
    T["consts"] = nc.dram_tensor("consts", (P, C_END), F32, kind="ExternalInput").ap()
    out = nc.dram_tensor("out_dram", (1, L, D), F32, kind="ExternalOutput").ap()
    build(nc, T, out)
    r = _run(nc, [arrays], core_ids=[0])
    return r.results[0]["out_dram"]
```

```python
from contextlib import ExitStack

import concourse.bass as bass
from concourse import mybir

F32 = mybir.dt.float32
I32 = mybir.dt.int32
ALU = mybir.AluOpType
ACT = mybir.ActivationFunctionType
AX = mybir.AxisListType

P = 128
D = 1024
L = 256
KD = D // P
NT = L // P
HEADS = 4
DH = 64
WA = 512
G, NS, HG = 32, 64, 16
TC = 8
NC = L // TC
NE, TOPK = 32, 4
SLOTS = 64
EXTRA = (L * TOPK - 1) // SLOTS
MAXB = (L + SLOTS - 1) // SLOTS
EPS = 1e-6
LAMBDA_INIT = 0.2
TWO_PI = 6.283185307179586
PI_A, PI_B, PI_C = 6.28125, 0.0019350051879882812, 3.0199159819567e-07
ROUND = 12582912.0
GATE_MAX = 7.0
GATE_ALPHA = 1.702
WAY_IN_SPLIT = 5
WARM_UP = 4
STAGE = 4
LAST = 3
AHEAD = 5

C_ID = 0
C_UP = C_ID + P
C_ONE = C_UP + P
C_BLK = C_ONE + P
C_M16 = C_BLK + P
C_IOTA = C_M16 + HG
C_COS = C_IOTA + 64
C_SIN = C_COS + NT * 32
C_TRI = C_SIN + NT * 32
C_END = C_TRI + NE


def constants():
    import numpy as np

    c = np.zeros((P, C_END), np.float32)
    r = np.arange(P)
    c[:, C_ID:C_ID + P] = np.eye(P)
    c[:, C_UP:C_UP + P] = r[:, None] < r[None, :]
    c[:, C_ONE:C_ONE + P] = 1
    c[:, C_BLK:C_BLK + P] = r[:, None] // HG == r[None, :] // HG
    c[:, C_M16:C_M16 + HG] = r[:, None] % HG == np.arange(HG)[None, :]
    c[:, C_IOTA:C_IOTA + 64] = np.arange(64)[None, :]
    inv = (np.float32(10000.0) ** (-np.arange(32, dtype=np.float32) * np.float32(2.0 / DH))).astype(np.float32)
    for t in range(NT):
        ang = ((t * P + r).astype(np.float32)[:, None] * inv[None, :]).astype(np.float32)
        c[:, C_COS + 32 * t:C_COS + 32 * t + 32] = np.cos(ang)
        c[:, C_SIN + 32 * t:C_SIN + 32 * t + 32] = np.sin(ang)
    c[:, C_TRI:C_TRI + NE] = (r[:, None] <= np.arange(NE)[None, :]) & (r[:, None] < NE)
    return c


def build(nc, T, out):
    ctx = ExitStack()
    with ctx:
        def sb(name, cols, parts=P, dt=F32):
            return ctx.enter_context(nc.sbuf_tensor(name, [parts, cols], dt))

        def sem(name):
            return ctx.enter_context(nc.semaphore(name))

        ring = sb("ring", 8 * 2048 + 8 * 1024)
        w1 = ring[:, 0:16384].rearrange("p (k n) -> p k n", k=KD)
        w2 = ring[:, 16384:24576].rearrange("p (k n) -> p k n", k=KD)
        s5w = ring[:, 0:8192].rearrange("p (c g t h) -> p c g t h", c=2, g=G, t=TC)
        s5b = ring[:, 8192:16384].rearrange("p (g c t h) -> p g c t h", g=G, c=2, t=TC)
        lin = ring[:, 8192:16384].rearrange("p (g c m) -> p g c m", g=G, c=2)
        toep = ring[:, 16384:20480].rearrange("p (g m) -> p g m", g=G)
        bsplit = ring[:, 20480:22528].rearrange("p (c g d h) -> p c g d h", c=2, g=G, d=2)
        zst = ring[:, 20480:22528].rearrange("p (k c g) -> p k c g", k=NC, c=2)
        bbar = ring[:, 22528:23552].rearrange("p (c g h) -> p c g h", c=2, g=G)
        tmp_v = ring[:, 23552:24064].rearrange("p (g h) -> p g h", g=G)
        tmp_p = ring[:, 24064:24576].rearrange("p (g h) -> p g h", g=G)
        zk = ring[:, 22528:24576].rearrange("p (a n) -> p a n", a=8)
        xst = ring[:, 22528:24576].rearrange("p (k c g) -> p k c g", k=NC, c=2)
        enter = ring[:, 8192:10240].rearrange("p (c g k) -> p c g k", c=2, g=G)
        craw = ring[:, 16384:17408].rearrange("p (c j m) -> p c j m", c=2, j=4)
        braw = ring[:, 17408:18432].rearrange("p (c g h) -> p c g h", c=2, g=G)
        y4 = ring[:, 11264:12288].rearrange("p (t a h) -> p t a h", t=TC, a=8)
        prep = ring[0:G, 8192:16384]

        stage = sb("stage", STAGE * 2048)
        slot = [stage[:, i * 2048:(i + 1) * 2048].rearrange("p (k n) -> p k n", k=4) for i in range(STAGE)]
        con = sb("con", C_END)
        ident = con[:, C_ID:C_ID + P]
        ones = con[:, C_ONE:C_ONE + P]
        hres = sb("hres", NT * D)
        h3 = hres[:, :].rearrange("p (t n) -> p t n", t=NT)
        hnt = sb("hnt", KD * L)
        hnT = hnt[:, :].rearrange("p (k l) -> p k l", k=KD)
        a1 = sb("a1", 2048)
        a2 = sb("a2", 2048)
        t1, t2, t3 = sb("t1", 2048), sb("t2", 2048), sb("t3", 2048)
        gaT = a1[:, :].rearrange("p (k l) -> p k l", k=KD)
        gsT = a2[:, :].rearrange("p (k l) -> p k l", k=KD)
        pw = a1[0:G, :].rearrange("p (c t m) -> p c t m", c=2, t=TC)
        xn = a2[:, :].rearrange("p (t n) -> p t n", t=NT)
        usb = a2[:, 0:1024].rearrange("p (t n) -> p t n", t=NT)
        u4 = a2[:, 1024:2048].rearrange("p (t n) -> p t n", t=TC)
        u5 = a2[:, 0:1024].rearrange("p (a t h) -> p a t h", a=8, t=TC)
        qn = t1[:, 0:1024].rearrange("p (t n) -> p t n", t=NT)
        kn = t1[:, 1024:2048].rearrange("p (t n) -> p t n", t=NT)
        vn = t2[:, 0:1024].rearrange("p (t n) -> p t n", t=NT)
        qT = t2[:, 1024:2048].rearrange("p (h l) -> p h l", h=HEADS)
        kT0 = t3[:, 0:1024].rearrange("p (h l) -> p h l", h=HEADS)
        wT = t3[:, 1024:2048].rearrange("p (b k l) -> p b k l", b=2, k=NT)
        prob = t1[:, 0:1024].rearrange("p (c t l) -> p c t l", c=2, t=NT)
        on = t1[:, 1024:2048].rearrange("p (t h e) -> p t h e", t=NT, h=HEADS)
        memT = t3[:, :].rearrange("p (k l) -> p k l", k=KD)
        mkT = t2[:, :].rearrange("p (k l) -> p k l", k=KD)
        mn = hnt[:, :].rearrange("p (t n) -> p t n", t=NT)
        mvn = t1[:, :].rearrange("p (t n) -> p t n", t=NT)
        big = sb("big", 1024 + 4 * HG)
        kT1 = big[:, 0:1024].rearrange("p (h l) -> p h l", h=HEADS)
        tap0 = big[:, 1024:].rearrange("p (j h) -> p j h", j=4)
        taps = t1[:, 1024:2048].rearrange("p (a n) -> p a n", a=8)
        uT_ = sb("uT_", 1024)
        uT = uT_[:, :].rearrange("p (a n) -> p a n", a=8)
        ct_ = sb("ct_", 1024)
        ct = ct_[:, :].rearrange("p (c j n) -> p c j n", c=2, j=4)
        wi_ = sb("wi_", 1024)
        wpow = wi_[:, 0:512].rearrange("p (c t g) -> p c t g", c=2, t=TC)
        ipow = wi_[:, 512:1024].rearrange("p (c t g) -> p c t g", c=2, t=TC)
        oT = wi_[:, :].rearrange("p (h l) -> p h l", h=HEADS)
        yT = ct_[:, :].rearrange("p (j l) -> p j l", j=4)
        osT = uT_[:, :].rearrange("p (j l) -> p j l", j=4)
        graw = ring[0:4 * KD, 16384:16384 + P]
        gains = sb("gains", 4 * KD)
        st = sb("st", 64)
        lamb = sb("lamb", 4 * DH)
        lam8 = sb("lam8", 2 * 2 * 2 * G)
        sm = sb("sm", 3 * NT * 4 + 8)
        idx = sb("idx", NE + EXTRA + 2, dt=I32)

        pt = [ctx.enter_context(nc.psum_tensor(f"pt{i}", [P, 1024], F32)) for i in range(4)]
        PA, PB, PC, PD = range(4)

        taps_dram = nc.dram_tensor("taps_dram", [G, HG, 272], F32, kind="Internal").ap()

        s_con = sem("const_loaded"); s_x = [sem(f"x_tile{t}_loaded") for t in range(NT)]; s_gain = sem("gains_loaded"); s_small = sem("s5_small_loaded")
        s_bc = sem("b_and_c_loaded"); s_par = sem("small_parameters_loaded"); s_mem = sem("mem_loaded")
        s_u4 = sem("u4_regrouped"); s_tapw = sem("taps_written"); s_tap0 = sem("lag0_taps_written"); s_toep = sem("toeplitz_loaded")
        s_rt = sem("router_and_biases_loaded"); s_gf = sem("final_gain_loaded")
        s_out = sem("out_written")
        s_slot = [sem(f"slot{i}_loaded") for i in range(STAGE)]
        s_used = sem("slots_used")
        s_v = sem("dve_step"); s_p = sem("pool_step")
        names = """root tile0 epsv ssq u4r usb dtl mag red trig tabsrc tabp taba bspl vev utp uta cta scp smx pex pwv wtp wta pvp on
            otp ota lamx laml bp s5wd kp kta k0p kse kz ltp lta ltv zp zka zkv ztp zva zvv scan enta entv mka mva
            sgm bav yp ygel ytp graw yta gls osv bsv mh xqa xsp xmx xex xpn xtp xta xop xoa xh lgp lgv lex msk
            rkp rkv gdv gdp gda cup cuv ovp ovi hn3 gfin accd rope gates qkp qka sumsq normed tokp
            tokv""".split()
        S = {n: sem(n) for n in names}
        s_w1 = [[sem(f"w1_chunk{k}_loaded") for k in range(KD)], [sem(f"w1_chunk{k}_loaded_odd") for k in range(AHEAD)]]
        s_w2 = [sem(f"w2_pair{k}_loaded") for k in range(KD // 2)]
        m_sel = sem("block_selected"); m_selw = sem("block_weighted"); m_x = sem("block_gathered")
        m_xn = sem("block_tokens_copied"); m_xt = sem("block_tokens_turned"); m_xT = sem("block_tokens_ready")
        m_w1u = sem("w1_chunks_consumed"); m_w2u = sem("w2_pairs_consumed"); m_st = sem("scatter_transposed")
        m_gs = sem("scatter_ready"); m_g2 = sem("gate_clamped"); m_sig = sem("gate_sigmoid"); m_act = sem("hidden_ready")
        m_at = sem("hidden_turned"); m_hT = sem("hidden_turned_ready"); m_y = sem("y_ready"); m_v = sem("block_dve_step")
        m_sc = sem("scattered")

        cols = {"u": ("w_in", 3 * WA), "q": ("w_in", 0), "k": ("w_in", WA), "v": ("w_in", 2 * WA)}
        SLABS = [(n, *cols[n], D) for n in "uqkv"]
        for n, w, c0, rows, count in (("ga", "w_in", 4 * WA, D, 2), ("gs", "w_in", 6 * WA, D, 2), ("mk", "w_xkv", 0, D, 2),
                                      ("mv", "w_xkv", D, D, 2), ("ba", "w_branch_attn", 0, WA, 2), ("gl", "w_glu", 0, WA, 2),
                                      ("bs", "w_branch_ssm", 0, WA, 2), ("mx", "w_mix_out", 0, D, 2),
                                      ("xq", "w_xq", 0, D, 2), ("xo", "w_xo", 0, D, 2)):
            SLABS += [(f"{n}{i}", w, c0 + WA * i, rows) for i in range(count)]
        SLABS.insert([s[0] for s in SLABS].index("gl1"), SLABS.pop([s[0] for s in SLABS].index("ba1")))
        SLAB_NO = {s[0]: i for i, s in enumerate(SLABS)}
        SLOT_USES = [(i, w, r, c) for i, (_, w, c, rows) in enumerate(SLABS) for r in range(0, rows, WA)]

        SLAB_END = {n: sum(u[0] <= i for u in SLOT_USES) for n, i in SLAB_NO.items()}

        def slab_done(eng, name):
            eng.wait_ge(s_used, SLAB_END[name])

        def way_in_step(eng, t, tmp, link):
            ir, ii = (ipow[:, c, t, :].unsqueeze(2).to_broadcast([P, G, HG]) for c in range(2))
            zr, zi = s5b[:, :, 0, t], s5b[:, :, 1, t]
            link(eng.tensor_tensor(tmp, bbar[:, 0], ir, ALU.mult))
            link(eng.tensor_tensor(zr, bbar[:, 1], ii, ALU.mult))
            link(eng.tensor_tensor(zr, tmp, zr, ALU.subtract))
            link(eng.tensor_tensor(tmp, bbar[:, 1], ir, ALU.mult))
            link(eng.tensor_tensor(zi, bbar[:, 0], ii, ALU.mult))
            return eng.tensor_tensor(zi, tmp, zi, ALU.add)

        w1_dram = T["w_e1"].rearrange("a e (k p) n -> (a e) k p n", p=P)
        w2_dram = T["w_e2"].rearrange("a e (k p) n -> (a e) p k n", p=P)

        odd = [(a1[:, 0:1024], a1[:, 1024:2048]), (t2[:, 1024:2048], ct_[:, :]), (big[:, 0:1024], t1[:, 1024:2048]),
               (stage[:, 4096:5120], stage[:, 5120:6144]), (stage[:, 6144:7168], stage[:, 7168:8192])]

        def w1_cols(par, k, c):
            if par and k < AHEAD:
                return odd[k][c // D][:, c % D:c % D + 512]
            return w1[:, k, c:c + 512]

        def w1_loaded(par, k, it):
            if k >= AHEAD:
                return s_w1[0][k], 16 * (it + 1)
            return (s_w1[1][k], 16 * (it + 1)) if par else (s_w1[0][k], 8 * it + 16)

        def load_w1(eng, e, k, par=0):
            src = w1_dram[0, k] if e is None else w1_dram[bass.ds(e, 1), k].rearrange("a p n -> p (a n)")
            if par and k < AHEAD:
                for c in range(2):
                    eng.dma_start(odd[k][c], src[:, D * c:D * (c + 1)]).then_inc(s_w1[1][k], 16)
            else:
                eng.dma_start(w1[:, k, :], src).then_inc(s_w1[0][k], 16)

        def load_w2(eng, e, kk):
            if e is None:
                src = w2_dram[0, :, 2 * kk:2 * kk + 2, :]
            else:
                src = w2_dram[bass.ds(e, 1), :, 2 * kk:2 * kk + 2, :].rearrange("a p k n -> p (a k) n")
            eng.dma_start(w2[:, 2 * kk:2 * kk + 2, :], src).then_inc(s_w2[kk], 16)

        block = ctx.enter_context(nc.Block())

        def part(a, n):
            return stage[:, a:a + n]
        xgn = part(0, 512)
        xT_flat = part(512, 512)
        xT = xT_flat.rearrange("p (c n s) -> p c n s", c=4, n=2)
        hg, hl, hgl, hsg = (hnt[:, 512 * i:512 * (i + 1)] for i in range(4))
        hact = wi_[:, 0:512]
        hT_flat = wi_[:, 512:1024]
        hT = hT_flat.rearrange("p (c g s) -> p c g s", c=4, g=2)
        ysb = part(3584, 512)
        gsc_flat = uT_[:, 512:1024]
        gsc = gsc_flat.rearrange("p (n t l) -> p n t l", n=2, t=NT)
        ecol = part(1024, SLOTS)
        selw = part(1104, NT * 3 * SLOTS).rearrange("p (t s) -> p t s", t=NT)
        sel = part(1792, NT * SLOTS).rearrange("p (t s) -> p t s", t=NT)
        posn = part(2048, NT * NE).rearrange("p (t e) -> p t e", t=NT)
        gate = part(2112, NT * NE).rearrange("p (t e) -> p t e", t=NT)
        lg = part(2176, NT * NE).rearrange("p (t e) -> p t e", t=NT)
        msk = part(2240, NT * NE).rearrange("p (t e) -> p t e", t=NT)
        offs = part(2304, NE + EXTRA + 1)
        pse = part(2368, 2 * NT).rearrange("p (a t) -> p a t", a=2)
        top8 = part(2376, NT * 8).rearrange("p (t e) -> p t e", t=NT)
        rep = part(2392, NT * NE).rearrange("p (t e) -> p t e", t=NT)
        ovf = part(2456, 2 * EXTRA + 1)
        gT = part(2560, L)
        wr = uT_[:, 0:KD * NE].rearrange("p (k e) -> p k e", k=KD)
        nbx = part(3072, 2)[0:NE]
        blk = part(3080, 2 * EXTRA + 1)[0:NE]
        p2 = a1[:, :].rearrange("p (h t l) -> p h t l", h=HEADS, t=NT)
        p2T = t3[:, :].rearrange("p (h k l) -> p h k l", h=HEADS, k=NT)
        glu_flat = big[:, 0:1024]
        hnT_flat = hnt[:, :]
        gfin = t1[:, 0:D]
        be1 = t3
        gffn = wi_[:, :]
        be2 = t2[:, 0:D]
        brt = uT_[:, KD * NE:(KD + 1) * NE]

        @block.sync
        def _(sp):
            for t in range(NT):
                sp.dma_start(h3[:, t], T["x"][0, P * t:P * (t + 1)]).then_inc(s_x[t], 16)
            sp.dma_start(con[:, :], T["consts"]).then_inc(s_con, 16)
            for i, n in enumerate(("norm_mix_g", "norm_mem_g", "norm_cross_g", "norm_ffn_g")):
                sp.dma_start(graw[i * KD:(i + 1) * KD], T[n].rearrange("a (k p) -> (a k) p", p=P)).then_inc(s_gain, 16)
            for i, (slab, w, r, c) in enumerate(SLOT_USES):
                if i == SLAB_END["gs1"] + STAGE:
                    sp.wait_ge(S["kta"], 1)
                    for j in range(4):
                        for d in range(2):
                            sp.dma_start(taps_dram[8 * j:8 * j + 8, :, 144 * d:144 * d + P].rearrange("a h n -> h a n"),
                                         taps[32 * j + HG * d:32 * j + HG * (d + 1)]).then_inc(s_tapw, 16)
                if i >= STAGE:
                    sp.wait_ge(s_used, i - STAGE + 1)
                src = T[w][0, r:r + WA, c:c + WA].rearrange("(k p) n -> p k n", p=P)
                sp.dma_start(slot[i % STAGE], src).then_inc(s_slot[i % STAGE], 16)
                if i + 1 == SLAB_END["xq1"]:
                    sp.wait_ge(S["ytp"], 1)
                    for k in range(KD):
                        load_w1(sp, None, k)
                    for k in range(KD // 2):
                        load_w2(sp, None, k)

            def load_ahead(it, e, par, used=True):
                for k in range(AHEAD):
                    if used:
                        sp.wait_ge(m_w1u, KD * (it - 2) + k + 1)
                    load_w1(sp, e, k, par)
                    if not used and k == 2:
                        sp.wait_ge(s_used, len(SLOT_USES) - 2)

            def load_rest(it, e):
                for k in range(AHEAD, KD):
                    sp.wait_ge(m_w1u, KD * (it - 1) + k + 1)
                    load_w1(sp, e, k)
                for kk in range(KD // 2):
                    sp.wait_ge(m_w2u, (KD // 2) * (it - 1) + kk + 1)
                    load_w2(sp, e, kk)

            sp.wait_ge(S["xtp"], 2)
            sp.wait_ge(S["xop"], 2)
            load_ahead(1, 1, 1, used=False)
            with sp.Fori(0, NE // 2 - 1 - LAST) as pair:
                load_ahead(pair * 2 + 2, pair * 2 + 2, 0)
                load_rest(pair * 2 + 1, pair * 2 + 1)
                load_ahead(pair * 2 + 3, pair * 2 + 3, 1)
                load_rest(pair * 2 + 2, pair * 2 + 2)
            load_rest(NE - 2 * LAST - 1, NE - 2 * LAST - 1)
            with sp.Fori(NE // 2 - LAST, NE // 2) as pair:
                for par in range(2):
                    load_ahead(pair * 2 + par, pair * 2 + par, par)
                    load_rest(pair * 2 + par, pair * 2 + par)
            sp.wait_ge(S["ovi"], 1)
            n_extra = sp.value_load(idx[0:1, NE + EXTRA + 1:NE + EXTRA + 2], min_val=0, max_val=EXTRA)
            with sp.If(n_extra > 0):
                with sp.Fori(0, (EXTRA + 1) // 2) as pair:
                    for par in range(2):
                        with sp.If(n_extra > pair * 2 + par):
                            e = sp.value_load(idx[0:1, bass.ds(pair * 2 + NE + par, 1)], min_val=0, max_val=NE - 1)
                            load_ahead(pair * 2 + NE + par, e, par)
                            load_rest(pair * 2 + NE + par, e)
            for t in range(NT):
                sp.wait_ge(S["gfin"], t + 1)
                sp.dma_start(out[0, P * t:P * (t + 1)], h3[:, t]).then_inc(s_out, 16)
            sp.wait_ge(s_out, 16 * NT)

        @block.gpsimd
        def _(pool):
            steps = [0]

            def link(ins):
                steps[0] += 1
                ins.then_inc(s_p, 1)
                pool.wait_ge(s_p, steps[0])

            are = prep[:, 0:128].rearrange("p (d m) -> p d m", d=2)
            aim = prep[:, 128:256].rearrange("p (d m) -> p d m", d=2)
            ldt = prep[:, 256:258]
            pool.dma_start(are, T["ssm_a_re"].rearrange("a d g p -> g (a d) p")).then_inc(s_small, 16)
            pool.dma_start(aim, T["ssm_a_im"].rearrange("a d g p -> g (a d) p")).then_inc(s_small, 16)
            pool.dma_start(ldt, T["ssm_log_dt"].rearrange("a d g -> g (a d)"),
                           allow_slow_non_contiguous=True).then_inc(s_small, 16)
            for i, n in enumerate(("lambda_q1", "lambda_k1", "lambda_q2", "lambda_k2")):
                pool.dma_start(lamb[:, i * DH:(i + 1) * DH], T[n].broadcast_to([P, DH])).then_inc(s_par, 16)
            pool.dma_start(st[:, 32:33], T["subln_g"].rearrange("a p -> p a"), allow_slow_non_contiguous=True).then_inc(s_par, 16)
            pool.dma_start(st[:, 36:40], T["ssm_d"].rearrange("a (j p) -> p (a j)", p=P),
                           allow_slow_non_contiguous=True).then_inc(s_par, 16)
            pool.wait_ge(S["graw"], 1)
            for c, n in enumerate(("ssm_c_re", "ssm_c_im")):
                for d in range(2):
                    dst = craw[:, c, :, d * NS:(d + 1) * NS]
                    src = T[n][0, d].rearrange("(j a) h p -> (a h) j p", j=4)
                    pool.dma_start(dst, src).then_inc(s_bc, 16)
            for c, n in enumerate(("ssm_b_re", "ssm_b_im")):
                for d in range(2):
                    pool.dma_start(braw[d * NS:(d + 1) * NS, c], T[n][0, d].rearrange("g p h -> p g h")).then_inc(s_bc, 16)
            pool.wait_ge(S["taba"], 1)
            pool.wait_ge(S["cta"], 1)
            cr = ct[:, 0].rearrange("p j (a h) -> p (j a) h", h=HG)
            cn = ct[:, 1].rearrange("p j (a h) -> p (j a) h", h=HG)
            for t in range(TC):
                lr = wpow[:, 0, t, :].unsqueeze(2).to_broadcast([P, G, HG])
                li = wpow[:, 1, t, :].unsqueeze(2).to_broadcast([P, G, HG])
                link(pool.tensor_tensor(tmp_p, cr, lr, ALU.mult))
                link(pool.tensor_tensor(s5w[:, 0, :, t, :], cn, li, ALU.mult))
                link(pool.tensor_tensor(s5w[:, 0, :, t, :], tmp_p, s5w[:, 0, :, t, :], ALU.add))
                link(pool.tensor_tensor(tmp_p, cr, li, ALU.mult))
                link(pool.tensor_tensor(s5w[:, 1, :, t, :], cn, lr, ALU.mult))
                last = pool.tensor_tensor(s5w[:, 1, :, t, :], s5w[:, 1, :, t, :], tmp_p, ALU.subtract)
                if t < TC - 1:
                    link(last)
            last.then_inc(S["s5wd"], 1)
            pool.wait_ge(S["s5wd"], 1)
            pool.wait_ge(S["bspl"], 1)
            for t in range(WAY_IN_SPLIT, TC):
                last = way_in_step(pool, t, tmp_p, link)
                if t < TC - 1:
                    link(last)
            last.then_inc(S["bp"], 1)

            slab_done(pool, "gs1")
            pool.dma_start(mn, T["mem"].rearrange("a (t p) n -> p (a t) n", p=P)).then_inc(s_mem, 16)
            pool.wait_ge(S["kse"], 1)
            pool.dma_start(taps_dram[:, :, 128:144].rearrange("(j a) h n -> (a h) j n", j=4), tap0).then_inc(s_tap0, 16)
            pool.wait_ge(s_tap0, 16)
            pool.wait_ge(s_tapw, 8 * 16)
            for t in range(TC):
                pool.dma_start(toep[HG * t:HG * (t + 1)],
                               taps_dram[:, :, HG * (TC - t):HG * (TC - t) + P].rearrange("g h n -> h g n")).then_inc(s_toep, 16)
            slab_done(pool, "bs1")
            pool.dma_start(gffn, T["norm_ffn_g"].broadcast_to([P, D])).then_inc(s_gf, 16)
            pool.dma_start(wr, T["w_router"].rearrange("a (k p) e -> p (a k) e", p=P)).then_inc(s_rt, 16)
            pool.wait_ge(S["xop"], 2)
            pool.dma_start(brt, T["b_router"].broadcast_to([P, NE])).then_inc(s_rt, 16)
            pool.memset(t2[:, 0:D], 0.0)
            link(pool.memset(t3[:, :], 0.0))
            pool.dma_start(t3[0:NE, :], T["b_e1"].rearrange("a e n -> (a e) n")).then_inc(s_rt, 16)
            pool.dma_start(t2[0:NE, 0:D], T["b_e2"].rearrange("a e n -> (a e) n")).then_inc(s_rt, 16)
            pool.dma_start(gfin, T["norm_final_g"].rearrange("(a n) -> a n", a=1).broadcast_to([P, D])).then_inc(s_gf, 16)
            pool.wait_ge(s_gf, 32)
            pool.wait_ge(S["tokp"], 8)
            for t in range(NT):
                pool.tensor_tensor(xn[:, t], xn[:, t], gffn, ALU.mult).then_inc(S["hn3"], 1)

        @block.tensor
        def _(pe):
            readers = [[], [], [], []]
            slots_used = [0]

            def take(u, *who):
                for name, n in readers[u]:
                    pe.wait_ge(S[name], n)
                readers[u] = list(who)

            def turn(dst, src):
                n = src.shape[0]
                return pe.transpose(dst, src, ident[0:n, 0:n])

            def weights(slab):
                got = []
                while slots_used[0] < len(SLOT_USES) and SLOT_USES[slots_used[0]][0] == SLAB_NO[slab]:
                    i = slots_used[0]
                    got.append((slot[i % STAGE], s_slot[i % STAGE], 16 * (i // STAGE + 1)))
                    slots_used[0] += 1
                return got

            def natural(slab, u, xT, *who):
                ws = weights(slab)
                take(u, *who)
                for t in range(NT):
                    for k in range(4 * len(ws)):
                        w, loaded, n_loaded = ws[k // 4]
                        if t == 0 and k % 4 == 0:
                            pe.wait_ge(loaded, n_loaded)
                        last = pe.matmul(pt[u][:, 512 * t:512 * t + 512], xT[:, k, t * P:(t + 1) * P], w[:, k % 4, :], start=(k == 0), stop=(k == 4 * len(ws) - 1))
                        if t == NT - 1 and k % 4 == 3:
                            last.then_inc(s_used, 1)

            def flipped(slab, u, xT, *who):
                ws = weights(slab)
                take(u, *who)
                for m in range(4):
                    for k in range(4 * len(ws)):
                        w, loaded, n_loaded = ws[k // 4]
                        if m == 0 and k % 4 == 0:
                            pe.wait_ge(loaded, n_loaded)
                        last = pe.matmul(pt[u][:, L * m:L * m + L], w[:, k % 4, m * P:(m + 1) * P], xT[:, k, :],
                                         start=(k == 0), stop=(k == 4 * len(ws) - 1))
                        if m == 3 and k % 4 == 3:
                            last.then_inc(s_used, 1)

            def turn_some(src, i, u, norm):
                pe.wait_ge(S["normed"], NT * (norm + 1))
                take(u, ("tokv", 2 * norm + i + 1))
                for k in range(4):
                    for t in range(NT):
                        last = turn(pt[u][:, L * k + P * t:L * k + P * (t + 1)],
                                    src[:, t, P * (4 * i + k):P * (4 * i + k + 1)])
                last.then_inc(S["tokp"], 1)

            def turn_tile(src, t, u, norm):
                pe.wait_ge(S["normed"], NT * norm + t + 1)
                take(u, ("tokv", 2 * norm + t + 1))
                for k in range(KD):
                    last = turn(pt[u][:, P * k:P * (k + 1)], src[:, t, P * k:P * (k + 1)])
                last.then_inc(S["tokp"], 1)

            def natural_tile(ws, t, u, xT, done, halfway=None, between=None):
                take(u, (done, t + 1))
                for n in range(2):
                    if n == 1 and between:
                        between()
                    for k in range(KD):
                        if k == 4 and n == 0 and halfway:
                            pe.wait_ge(S[halfway[0]], halfway[1])
                        w, loaded, n_loaded = ws[2 * n + k // 4]
                        if t == 0 and k % 4 == 0:
                            pe.wait_ge(loaded, n_loaded)
                        last = pe.matmul(pt[u][:, 512 * n:512 * (n + 1)], xT[:, k, P * t:P * (t + 1)], w[:, k % 4, :], start=(k == 0), stop=(k == KD - 1))
                        if t == NT - 1 and k % 4 == 3:
                            last.then_inc(s_used, 1)
                        elif k == KD - 1 and n == 1:
                            last.then_inc(S["tile0"], 1)

            def flipped_tile(ws, t, u, m0, xT):
                for m in range(4):
                    for k in range(KD):
                        w, loaded, n_loaded = ws[m0 + k // 4]
                        if t == 0 and m == 0 and k % 4 == 0:
                            pe.wait_ge(loaded, n_loaded)
                        last = pe.matmul(pt[u][:, L * m + P * t:L * m + P * (t + 1)], w[:, k % 4, m * P:(m + 1) * P],
                                         xT[:, k, P * t:P * (t + 1)], start=(k == 0), stop=(k == KD - 1))
                        if t == NT - 1 and m == 3 and k % 4 == 3:
                            last.then_inc(s_used, 1)

            pe.wait_ge(S["epsv"], 1)
            for _ in range(WARM_UP):
                pe.matmul(pt[PB][:, 0:512], t3[:, 0:P], t3[:, 0:512], start=True, stop=True)
            pe.wait_ge(s_con, 16)
            pe.wait_ge(s_gain, 64)
            turn(pt[PA][:, 0:4 * KD], graw).then_inc(S["graw"], 1)
            readers[PA] = [("tokv", 1)]
            turn_some(xn, 0, PC, 0)
            turn_some(xn, 1, PD, 0)
            pe.wait_ge(S["tokv"], 2)
            natural("u", PA, hnT, ("usb", 1))
            natural("q", PB, hnT, ("rope", 1))

            pe.wait_ge(S["tabsrc"], 1)
            take(PC, ("taba", 1))
            for c in range(2):
                for t in range(TC):
                    turn(pt[PC][:, (c * TC + t) * G:(c * TC + t + 1) * G], pw[:, c, t, :])
            for c in range(2):
                last = turn(pt[PC][:, 512 + c * G:512 + (c + 1) * G], prep[:, 4096 + c * P:4096 + (c + 1) * P])
            last.then_inc(S["tabp"], 1)
            pe.wait_ge(s_bc, 128)
            take(PD, ("cta", 1))
            for c in range(2):
                for j in range(4):
                    last = turn(pt[PD][:, (4 * c + j) * P:(4 * c + j + 1) * P], craw[:, c, j, :])
            last.then_inc(S["tabp"], 1)

            natural("k", PA, hnT, ("rope", 2))
            natural("v", PB, hnT, ("vev", 1))

            pe.wait_ge(S["u4r"], 1)
            take(PC, ("uta", 1))
            for a in range(8):
                last = turn(pt[PC][:, P * a:P * (a + 1)], u5[:, a])
            last.then_inc(S["utp"], 1)
            flipped("ga0", PA, hnT, ("gates", 1))

            for n, src, u in ((1, qn, PD), (2, kn, PC)):
                pe.wait_ge(S["rope"], n)
                take(u, ("qka", n))
                for h in range(HEADS):
                    for t in range(NT):
                        last = turn(pt[u][:, L * h + P * t:L * h + P * (t + 1)], src[:, t, P * h:P * (h + 1)])
                last.then_inc(S["qkp"], 1)

            def scores(h):
                take(PD, ("smx", h + 1), ("pex", 4 * (h + 1)))
                for t in range(NT):
                    for c in range(2):
                        last = pe.matmul(pt[PD][:, 512 * c + L * t:512 * c + L * (t + 1)],
                                         qT[:, h, P * t:P * (t + 1)], (kT0, kT1)[c][:, h, :],
                                         start=True, stop=True)
                last.then_inc(S["scp"], 1)

            def turn_probs(h):
                pe.wait_ge(S["pwv"], h + 1)
                take(PC, ("wta", h + 1))
                for k in range(NT):
                    for t in range(NT):
                        last = turn(pt[PC][:, L * k + P * t:L * k + P * (t + 1)], prob[:, 0, t, P * k:P * (k + 1)])
                last.then_inc(S["wtp"], 1)

            def values(h):
                pe.wait_ge(S["wta"], h + 1)
                if h == 0:
                    take(PA, ("on", 1))
                for t in range(NT):
                    for k in range(NT):
                        last = pe.matmul(pt[PA][:, 512 * t + P * h:512 * t + P * (h + 1)], wT[:, h % 2, k, P * t:P * (t + 1)],
                                         vn[:, k, P * h:P * (h + 1)], start=(k == 0), stop=(k == NT - 1))
                last.then_inc(S["pvp"], 1)

            pe.wait_ge(S["bspl"], 1)
            take(PA, ("kse", 1))
            for j in range(4):
                for c in range(2):
                    last = pe.matmul(pt[PA][:, P * j:P * (j + 1)], bbar[:, c, 8 * j:8 * j + 8], ct[:, c, j],
                                     start=(c == 0), stop=(c == 1))
            last.then_inc(S["k0p"], 1)
            pe.wait_ge(S["qka"], 2)
            pe.wait_ge(S["vev"], 1)
            scores(0)
            flipped("ga1", PB, hnT, ("gates", 2))
            turn_probs(0)
            scores(1)
            flipped("gs0", PB, hnT, ("gates", 3))
            values(0)
            turn_probs(1)
            scores(2)
            flipped("gs1", PB, hnT, ("gates", 4))
            values(1)
            turn_probs(2)
            scores(3)

            pe.wait_ge(S["s5wd"], 1)
            pe.wait_ge(S["bspl"], 1)
            take(PB, ("kta", 1))
            for a in range(8):
                for c in range(2):
                    for j in range(4):
                        last = pe.matmul(pt[PB][32 * j:32 * (j + 1), P * a:P * (a + 1)], bsplit[:, c, 8 * j + a],
                                         s5w[:, c, 8 * j + a], start=(c == 0), stop=(c == 1))
            last.then_inc(S["kp"], 1)
            values(2)
            turn_probs(3)

            pe.wait_ge(S["bp"], 2)
            for r in range(8):
                u, read = ((PB, "lta"), (PD, "ltv"))[r % 2]
                take(u, (read, r // 2 + 1))
                for i in range(8):
                    last = turn(pt[u][:, P * i:P * (i + 1)], s5b[:, 4 * r + i // 2, i % 2])
                last.then_inc(S["ltp"], 1)
            values(3)

            pe.wait_ge(S["lta"], 4)
            pe.wait_ge(S["ltv"], 4)
            for i, (u, read) in enumerate(((PB, "zka"), (PD, "zkv"))):
                take(u, (read, 1))
                for a in range(4 * i, 4 * i + 4):
                    for j in range(4):
                        last = pe.matmul(pt[u][32 * j:32 * (j + 1), L * (a % 4):L * (a % 4 + 1)], uT[:, a, NC * j:NC * (j + 1)],
                                         lin[:, 8 * j + a].rearrange("p c m -> p (c m)"), start=True, stop=True)
                last.then_inc(S["zp"], 1)

            turn_some(mn, 0, PC, 1)
            for i, (u, read) in enumerate(((PB, "zka"), (PD, "zkv"))):
                pe.wait_ge(S[read], 1)
                take(u, ("zva", 2 * i + 2), ("zvv", 2 * i + 2))
                for a in range(4 * i, 4 * i + 4):
                    for c in range(2):
                        n = 2 * (a % 4) + c
                        last = turn(pt[u][:, P * n:P * (n + 1)], zk[:, a, P * c:P * (c + 1)])
                last.then_inc(S["ztp"], 1)

            pe.wait_ge(S["on"], 1)
            turn_some(mn, 1, PA, 1)
            pe.wait_ge(S["tokv"], 4)
            flipped("mk0", PC, memT, ("mka", 1))
            flipped("mk1", PD, memT, ("mka", 2))
            pe.wait_ge(S["on"], 2)
            take(PA, ("ota", 1))
            for h in range(HEADS):
                for t in range(NT):
                    last = turn(pt[PA][:, L * h + P * t:L * h + P * (t + 1)], on[:, t, h])
            last.then_inc(S["otp"], 1)

            natural("mv0", PB, memT, ("mva", 1))

            pe.wait_ge(s_toep, TC * 16)
            pe.wait_ge(S["enta"], 2)
            pe.wait_ge(S["entv"], 1)
            take(PD, ("ygel", 1))
            for a in range(8):
                for i in range(3):
                    for j in range(4):
                        g = 8 * j + a
                        lhsT = uT[:, a, NC * j:NC * (j + 1)] if i == 0 else enter[:, i - 1, g]
                        rhs = toep[:, g] if i == 0 else s5w[:, i - 1, g].rearrange("p t h -> p (t h)")
                        last = pe.matmul(pt[PD][32 * j:32 * (j + 1), P * a:P * (a + 1)], lhsT, rhs, start=(i == 0), stop=(i == 2))
            last.then_inc(S["yp"], 1)
            natural("mv1", PC, memT, ("mva", 2))
            pe.wait_ge(S["ygel"], 1)
            take(PA, ("yta", 1))
            for t in range(TC):
                last = turn(pt[PA][:, P * t:P * (t + 1)], y4[:, t])
            last.then_inc(S["ytp"], 1)
            pe.wait_ge(S["ota"], 1)
            flipped("ba0", PB, oT, ("bav", 1))
            pe.wait_ge(S["yta"], 1)
            flipped("gl0", PC, yT, ("osv", 1))
            flipped("gl1", PD, yT, ("gls", 1))
            flipped("ba1", PA, oT, ("bav", 2))
            pe.wait_ge(S["osv"], 1)
            flipped("bs0", PB, osT, ("bsv", 2))
            flipped("bs1", PC, osT, ("bsv", 4))
            pe.wait_ge(S["bsv"], 2)
            ws = weights("mx0") + weights("mx1")
            natural_tile(ws, 0, PD, gaT, "mh", ("bsv", 4))
            natural_tile(ws, 1, PA, gaT, "mh", between=lambda: turn_tile(xn, 0, PB, 2))

            pe.wait_ge(S["tokv"], 5)
            ws = weights("xq0") + weights("xq1")
            take(PC, ("xqa", 1))
            take(PD, ("xqa", 2))
            flipped_tile(ws, 0, PC, 0, hnT)
            turn_tile(xn, 1, PA, 2)
            flipped_tile(ws, 0, PD, 2, hnT)
            pe.wait_ge(S["tokv"], 6)
            flipped_tile(ws, 1, PC, 0, hnT)
            flipped_tile(ws, 1, PD, 2, hnT)
            pe.wait_ge(S["mka"], 2)
            for i, u in enumerate((PA, PB)):
                pe.wait_ge(S["xqa"], i + 1)
                take(u, ("xmx", i + 1), ("xex", 4 * (i + 1)))
                for hh in range(2):
                    for t in range(NT):
                        for m in range(2):
                            k = 4 * i + 2 * hh + m
                            last = pe.matmul(pt[u][:, 512 * hh + L * t:512 * hh + L * (t + 1)], gsT[:, k, P * t:P * (t + 1)],
                                             mkT[:, k, :], start=(m == 0), stop=(m == 1))
                last.then_inc(S["xsp"], 1)
            for i, u in enumerate((PC, PD)):
                take(u, ("xta", i + 1))
                for hh in range(2):
                    pe.wait_ge(S["xpn"], 2 * i + hh + 1)
                    for k in range(NT):
                        for t in range(NT):
                            last = turn(pt[u][:, 512 * hh + L * k + P * t:512 * hh + L * k + P * (t + 1)],
                                        p2[:, 2 * i + hh, t, P * k:P * (k + 1)])
                last.then_inc(S["xtp"], 1)
            pe.wait_ge(S["mva"], 2)
            for i, u in enumerate((PA, PB)):
                pe.wait_ge(S["xta"], i + 1)
                take(u, ("xoa", i + 1))
                for hh in range(2):
                    h = 2 * i + hh
                    for m in range(2):
                        for k in range(NT):
                            last = pe.matmul(pt[u][:, 512 * hh + L * m:512 * hh + L * (m + 1)],
                                             mvn[:, k, L * h + P * m:L * h + P * (m + 1)], p2T[:, h, k],
                                             start=(k == 0), stop=(k == NT - 1))
                last.then_inc(S["xop"], 1)
            pe.wait_ge(S["xoa"], 2)
            ws = weights("xo0") + weights("xo1")
            natural_tile(ws, 0, PC, hnT, "xh")
            natural_tile(ws, 1, PD, hnT, "xh", between=lambda: turn_tile(xn, 0, PA, 3))

            def route(t):
                pe.wait_ge(S["tokv"], 7 + t)
                take(PB, ("lgv", t + 1))
                for k in range(KD):
                    last = pe.matmul(pt[PB][:, 512 * t:512 * t + NE], hnT[:, k, P * t:P * (t + 1)], wr[:, k, :],
                                     start=(k == 0), stop=(k == KD - 1))
                last.then_inc(S["lgp"], 1)

            pe.wait_ge(s_rt, 64)
            def start_output(t):
                take((PA, PB)[t])
                for n in range(2):
                    pe.matmul(pt[(PA, PB)[t]][:, 512 * n:512 * (n + 1)], ident, h3[:, t, 512 * n:512 * (n + 1)],
                              start=True, stop=False)

            route(0)
            start_output(0)
            turn_tile(xn, 1, PC, 3)
            route(1)
            pe.wait_ge(S["msk"], NT)
            take(PD, ("rkv", 1))
            up = con[:, C_UP:C_UP + P]
            pe.matmul(pt[PD][:, 0:NE], up, msk[:, 0, :], start=True, stop=True)
            pe.matmul(pt[PD][:, NE:2 * NE], ones, msk[:, 0, :], start=True, stop=False)
            pe.matmul(pt[PD][:, NE:2 * NE], up, msk[:, 1, :], start=False, stop=True)
            for t in range(NT):
                last = pe.matmul(pt[PD][0:NE, 512:513], msk[:, t, :], ones[:, 0:1], start=(t == 0), stop=(t == NT - 1))
            last.then_inc(S["rkp"], 1)
            start_output(1)
            pe.wait_ge(S["gdv"], NT)
            take(PC, ("gda", 1))
            for t in range(NT):
                last = turn(pt[PC][0:NE, P * t:P * (t + 1)], gate[:, t, :])
            last.then_inc(S["gdp"], 1)

            def gather():
                for t in range(NT):
                    for n in range(2):
                        last = pe.matmul(pt[PD][SLOTS * n:SLOTS * (n + 1), 0:512], sel[:, t, :],
                                         xn[:, t, 512 * n:512 * (n + 1)], start=(t == 0), stop=(t == NT - 1))
                last.then_inc(m_x, 1)

            def turn_block():
                for c in range(4):
                    last = turn(pt[PD][:, P * c:P * (c + 1)], xgn[:, P * c:P * (c + 1)])
                last.then_inc(m_xt, 1)

            def scatter(stop, tiles=range(NT)):
                for t in tiles:
                    for n in range(2):
                        last = pe.matmul(pt[(PA, PB)[t]][:, 512 * n:512 * (n + 1)], gsc[:, n, t], ysb, start=False, stop=stop)
                return last

            def add_bias():
                for t in range(NT):
                    for n in range(2):
                        last = pe.matmul(pt[(PA, PB)[t]][:, 512 * n:512 * (n + 1)], gT[:, P * t:P * (t + 1)],
                                         be2[:, 512 * n:512 * (n + 1)], start=False, stop=False)
                return last

            pe.wait_ge(S["hn3"], NT)
            pe.wait_ge(m_sel, 1)
            gather()
            pe.wait_ge(S["rkv"], 1)
            pe.matmul(pt[PD][0:NE, 513:514], con[0:NE, C_TRI:C_TRI + NE], nbx[:, 0:1], start=True, stop=True).then_inc(S["cup"], 1)
            pe.wait_ge(m_xn, 1)
            turn_block()
            pe.wait_ge(S["cuv"], 1)
            pe.matmul(pt[PD][:, 512:512 + 2 * EXTRA + 1], ones[0:NE, :], blk[:, :], start=True, stop=True).then_inc(S["ovp"], 1)
            take(PC)

            def block_of(it, par, first=False):
                pe.wait_ge(m_xT, it + 1)
                for k in range(KD):
                    pe.wait_ge(*w1_loaded(par, k, it))
                    for b in range(2):
                        for g in range(2):
                            last = pe.matmul(pt[PC][SLOTS * g:SLOTS * (g + 1), 512 * b:512 * (b + 1)], xT[:, k % 4, k // 4],
                                             w1_cols(par, k, D * b + 512 * g), start=(k == 0), stop=(k == KD - 1))
                    last.then_inc(m_w1u, 1)
                    if k == 0:
                        for b in range(2):
                            for g in range(2):
                                pe.matmul(pt[PC][SLOTS * g:SLOTS * (g + 1), 512 * b:512 * (b + 1)], ecol,
                                          be1[:, D * b + 512 * g:D * b + 512 * (g + 1)], start=False, stop=False)
                pe.wait_ge(m_sel, it + 2)
                gather()
                pe.wait_ge(m_selw, it + 1)
                if not first:
                    pe.wait_ge(m_y, it)
                for n in range(2):
                    for t in range(NT):
                        last = turn(pt[PD][:, 512 + P * (NT * n + t):512 + P * (NT * n + t + 1)],
                                    selw[:, t, SLOTS * (1 - n):SLOTS * (3 - n)])
                last.then_inc(m_st, 1)
                if first:
                    add_bias().then_inc(m_sc, 1)
                else:
                    pe.wait_ge(m_gs, it)
                    scatter(False).then_inc(m_sc, 1)
                pe.wait_ge(m_act, it + 1)
                for c in range(4):
                    last = turn(pt[PC][:, P * c:P * (c + 1)], hact[:, P * c:P * (c + 1)])
                last.then_inc(m_at, 1)
                pe.wait_ge(m_xn, it + 2)
                turn_block()
                pe.wait_ge(m_hT, it + 1)
                pe.wait_ge(m_gs, it + 1)
                for k in range(KD):
                    if k % 2 == 0:
                        pe.wait_ge(s_w2[k // 2], 16 * (it + 1))
                    for n in range(2):
                        last = pe.matmul(pt[PD][SLOTS * n:SLOTS * (n + 1), 512:1024], hT[:, k % 4, k // 4],
                                         w2[:, k, 512 * n:512 * (n + 1)], start=(k == 0), stop=(k == KD - 1))
                    if k % 2:
                        last.then_inc(m_w2u, 1)

            block_of(0, 0, first=True)
            block_of(1, 1)
            with pe.Fori(1, NE // 2) as pair:
                block_of(pair * 2, 0)
                block_of(pair * 2 + 1, 1)
            pe.wait_ge(S["ovi"], 1)
            n_extra = pe.value_load(idx[0:1, NE + EXTRA + 1:NE + EXTRA + 2], min_val=0, max_val=EXTRA)
            with pe.If(n_extra > 0):
                with pe.Fori(0, (EXTRA + 1) // 2) as pair:
                    for par in range(2):
                        with pe.If(n_extra > pair * 2 + par):
                            block_of(pair * 2 + NE + par, par)
            pe.wait_ge(m_y, NE + n_extra)
            pe.wait_ge(m_gs, NE + n_extra)
            for t in range(NT):
                scatter(True, (t,)).then_inc(S["accd"], 1)

        @block.scalar
        def _(act):
            def square(src, scratch, col):
                act.activation(scratch, src, ACT.Square, accum_out=st[:, col:col + 1]).then_inc(S["sumsq"], 1)

            def root(src, dst, n, width, count=None):
                if count is not None:
                    act.wait_ge(S["sumsq"], count)
                act.activation(st[:, dst:dst + n], st[:, src:src + n], ACT.Sqrt, scale=1.0 / width,
                               bias=st[:, 60:61]).then_inc(S["root"], 1)

            def copy(dst, src):
                return act.activation(dst, src, ACT.Copy)

            def unit(u, pat=None, **kw):
                return pt[u][:, :] if pat is None else pt[u][:, :].rearrange(pat, **kw)

            act.wait_ge(S["epsv"], 1)
            act.activation(st[:, 61:62], st[:, 60:61], ACT.Sqrt)
            for t in range(NT):
                act.wait_ge(s_x[t], 16)
                square(h3[:, t], hnT_flat[:, t * D:(t + 1) * D], t)
            root(0, 2, NT, D, NT)
            act.wait_ge(s_small, 48)
            act.activation(prep[:, 258:260], prep[:, 256:258], ACT.Exp).then_inc(S["dtl"], 1)
            act.wait_ge(S["lamx"], 1)
            act.activation(st[:, 43:45], st[:, 41:43], ACT.Exp).then_inc(S["laml"], 1)
            act.wait_ge(S["mag"], 1)
            act.activation(prep[:, 640:768], prep[:, 384:512], ACT.Exp)
            act.wait_ge(S["red"], 1)
            act.activation(prep[:, 1024:1152], prep[:, 896:1024], ACT.Sin)
            act.activation(prep[:, 1280:1408], prep[:, 1152:1280], ACT.Sin).then_inc(S["trig"], 1)

            slab_done(act, "u")
            copy(usb, unit(PA, "p (t n) -> p t n", t=NT)).then_inc(S["usb"], 1)
            act.wait_ge(S["usb"], 1)
            for t in range(NT):
                for j in range(4):
                    act.dma_start(u4[32 * j + 16 * t:32 * j + 16 * t + 16], usb[:, t, P * j:P * (j + 1)]).then_inc(s_u4, 16)
            act.wait_ge(S["tabp"], 1)
            copy(wi_[:, 0:512], pt[PC][:, 0:512])
            copy(lam8[:, 0:2 * G], pt[PC][:, 512:512 + 2 * G]).then_inc(S["taba"], 1)
            act.wait_ge(S["tabp"], 2)
            copy(ct_[:, 0:512], pt[PD][:, 0:512])
            act.activation(ct_[:, 512:1024], pt[PD][:, 512:1024], ACT.Copy, scale=-1.0).then_inc(S["cta"], 1)
            act.wait_ge(s_u4, 8 * 16)
            copy(u5, u4.rearrange("p t (a h) -> p a t h", a=8)).then_inc(S["u4r"], 1)
            slab_done(act, "v")
            copy(vn, unit(PB, "p (t n) -> p t n", t=NT)).then_inc(S["vev"], 1)
            act.wait_ge(S["utp"], 1)
            copy(uT_[:, :], unit(PC)).then_inc(S["uta"], 1)
            slab_done(act, "ga0")
            act.wait_ge(S["tabp"], 1)
            copy(a1[:, 0:1024], unit(PA)).then_inc(S["gates"], 1)
            act.wait_ge(S["qkp"], 1)
            copy(t2[:, 1024:2048], unit(PD)).then_inc(S["qka"], 1)
            act.wait_ge(S["qkp"], 2)
            act.wait_ge(S["kz"], 1)
            copy(t3[0:DH, 0:1024], pt[PC][0:DH, :])
            copy(big[DH:P, 0:1024], pt[PC][DH:P, :]).then_inc(S["qka"], 1)

            def exps(h):
                act.wait_ge(S["smx"], h + 1)
                if h:
                    act.wait_ge(S["wtp"], h)
                for c in range(2):
                    for t in range(NT):
                        i = 2 * c + t
                        act.activation(prob[:, c, t], pt[PD][:, 512 * c + L * t:512 * c + L * (t + 1)], ACT.Exp,
                                       bias=sm[:, i:i + 1], scale=DH ** -0.5, accum_out=sm[:, 8 + i:9 + i]).then_inc(S["pex"], 1)

            def copy_probs(h):
                act.wait_ge(S["wtp"], h + 1)
                if h >= 2:
                    act.wait_ge(S["pvp"], h - 1)
                copy(wT[:, h % 2], pt[PC][:, 0:512].rearrange("p (k l) -> p k l", k=NT)).then_inc(S["wta"], 1)

            exps(0)
            slab_done(act, "ga1")
            copy(a1[:, 1024:2048], unit(PB)).then_inc(S["gates"], 1)
            copy_probs(0)
            exps(1)
            slab_done(act, "gs0")
            copy(a2[:, 0:1024], unit(PB)).then_inc(S["gates"], 1)
            copy_probs(1)
            exps(2)
            slab_done(act, "gs1")
            copy(a2[:, 1024:2048], unit(PB)).then_inc(S["gates"], 1)
            copy_probs(2)
            exps(3)
            act.wait_ge(S["kp"], 1)
            copy(t1[:, 1024:2048], unit(PB)).then_inc(S["kta"], 1)
            copy_probs(3)
            for r in range(0, 8, 2):
                act.wait_ge(S["ltp"], r + 1)
                copy(ring[:, 8192 + 1024 * r:8192 + 1024 * (r + 1)], unit(PB)).then_inc(S["lta"], 1)
                if r < 2 * NT:
                    t = r // 2
                    act.wait_ge(s_mem, 16)
                    square(mn[:, t], ring[:, 20480 + t * D:20480 + (t + 1) * D], 4 + t)
            root(4, 6, NT, D, 2 * NT)
            act.wait_ge(S["zp"], 1)
            act.wait_ge(S["k0p"], 1)
            act.wait_ge(S["kse"], 1)
            copy(ring[:, 22528:23552], unit(PB)).then_inc(S["zka"], 1)
            for i, u in enumerate((PB, PD)):
                act.wait_ge(S["ztp"], i + 1)
                for c in range(2):
                    src = pt[u][0:NS, :].rearrange("p (a c j k) -> p c k j a", a=4, c=2, j=4)[:, c]
                    dst = zst[0:NS, :, c, :].rearrange("p k (j a) -> p k j a", j=4)[:, :, :, 4 * i:4 * i + 4]
                    copy(dst, src).then_inc(S["zva"], 1)
            act.wait_ge(S["ssq"], 1)
            root(20, 46, 8, 2 * DH)
            act.activation(a1[:, :], a1[:, :], ACT.Sigmoid)
            act.activation(a2[:, :], a2[:, :], ACT.Sigmoid).then_inc(S["sgm"], 1)
            for i, u in enumerate((PC, PD)):
                slab_done(act, f"mk{i}")
                copy(t2[:, 1024 * i:1024 * (i + 1)], unit(u)).then_inc(S["mka"], 1)
            act.wait_ge(S["otp"], 1)
            act.activation(wi_[:, :], unit(PA), ACT.Copy, scale=st[:, 33:34]).then_inc(S["ota"], 1)
            act.wait_ge(S["scan"], 1)
            for c in range(2):
                copy(enter[0:NS, c, :, 1:NC], xst[0:NS, 0:NC - 1, c, :].rearrange("p k g -> p g k")).then_inc(S["enta"], 1)
            slab_done(act, "mv0")
            copy(mvn[:, :, 0:512], unit(PB, "p (t n) -> p t n", t=NT)).then_inc(S["mva"], 1)
            act.wait_ge(S["yp"], 1)
            act.activation(y4, unit(PD, "p (a t h) -> p t a h", a=8, t=TC), ACT.Gelu_apprx_tanh).then_inc(S["ygel"], 1)
            slab_done(act, "mv1")
            copy(mvn[:, :, 512:1024], unit(PC, "p (t n) -> p t n", t=NT)).then_inc(S["mva"], 1)
            act.wait_ge(S["ytp"], 1)
            for j in range(4):
                last = copy(yT[:, j].rearrange("p (k t) -> p t k", t=TC),
                            unit(PA, "p (t j k) -> p j t k", t=TC, j=4)[:, j])
            last.then_inc(S["yta"], 1)
            slab_done(act, "gl1")
            act.activation(glu_flat, unit(PD), ACT.Sigmoid).then_inc(S["gls"], 1)
            for t in range(NT):
                act.wait_ge(S["mh"], t + 1)
                square(h3[:, t], t3[:, 0:D], 8 + t)
                root(8 + t, 10 + t, 1, D, 2 * NT + t + 1)
            for i, u in enumerate((PC, PD)):
                slab_done(act, f"xq{i}")
                copy(a2[:, 1024 * i:1024 * (i + 1)], unit(u)).then_inc(S["xqa"], 1)
            for i, u in enumerate((PA, PB)):
                act.wait_ge(S["xmx"], i + 1)
                for hh in range(2):
                    for t in range(NT):
                        n = 2 * hh + t
                        act.activation(p2[:, 2 * i + hh, t], pt[u][:, 512 * hh + L * t:512 * hh + L * (t + 1)], ACT.Exp,
                                       bias=sm[:, 4 * i + n:4 * i + n + 1], scale=(D // HEADS) ** -0.5,
                                       accum_out=sm[:, 8 + 4 * i + n:9 + 4 * i + n]).then_inc(S["xex"], 1)
            for i, u in enumerate((PC, PD)):
                act.wait_ge(S["xtp"], i + 1)
                copy(t3[:, 1024 * i:1024 * (i + 1)], unit(u)).then_inc(S["xta"], 1)
            for i, u in enumerate((PA, PB)):
                act.wait_ge(S["xop"], i + 1)
                copy(hnt[:, 1024 * i:1024 * (i + 1)], unit(u)).then_inc(S["xoa"], 1)
            act.activation(st[:, 61:62], st[:, 60:61], ACT.Sqrt)
            for t in range(NT):
                act.wait_ge(S["xh"], t + 1)
                square(h3[:, t], pt[PC][:, :], 12 + t)
                root(12 + t, 14 + t, 1, D, 3 * NT + t + 1)
            for t in range(NT):
                act.wait_ge(S["msk"], t + 1)
                act.activation(gate[:, t, :], lg[:, t, :], ACT.Exp, bias=pse[:, 0, t:t + 1]).then_inc(S["lex"], 1)
            act.wait_ge(S["gdp"], 1)
            copy(gT[0:NE], pt[PC][0:NE, 0:L]).then_inc(S["gda"], 1)
            def block_of(it):
                act.wait_ge(m_g2, it + 1)
                act.activation(hsg, hg, ACT.Sigmoid, scale=GATE_ALPHA).then_inc(m_sig, 1)
                act.wait_ge(m_st, it + 1)
                act.wait_ge(m_sc, it + 1)
                copy(gsc_flat, pt[PD][:, 512:1024]).then_inc(m_gs, 1)
                act.wait_ge(m_at, it + 1)
                copy(hT_flat, pt[PC][:, 0:512]).then_inc(m_hT, 1)
                act.wait_ge(m_w2u, (KD // 2) * (it + 1))
                copy(ysb, pt[PD][:, 512:1024]).then_inc(m_y, 1)

            with act.Fori(0, NE) as e:
                block_of(e)
            act.wait_ge(S["ovi"], 1)
            n_extra = act.value_load(idx[0:1, NE + EXTRA + 1:NE + EXTRA + 2], min_val=0, max_val=EXTRA)
            with act.If(n_extra > 0):
                with act.Fori(0, EXTRA) as j:
                    with act.If(n_extra > j):
                        block_of(NE + j)
            act.activation(st[:, 61:62], st[:, 60:61], ACT.Sqrt)
            for t in range(NT):
                act.wait_ge(S["accd"], t + 1)
                square(pt[(PA, PB)[t]][:, :], hnt[:, t * D:(t + 1) * D], 16 + t)
                root(16 + t, 18 + t, 1, D, 4 * NT + t + 1)

        @block.vector
        def _(dve):
            steps = [0]

            def link(ins):
                steps[0] += 1
                ins.then_inc(s_v, 1)
                dve.wait_ge(s_v, steps[0])

            def bc(x, shape):
                return x.to_broadcast(shape)

            def normed(norm, src, dst):
                col = 4 * norm
                dve.wait_ge(S["root"], (1, 2)[norm])
                link(dve.reciprocal(st[:, col + 2:col + 2 + NT], st[:, col + 2:col + 2 + NT]))
                for t in range(NT):
                    dve.tensor_scalar(dst[:, t], src[:, t], st[:, col + 2 + t:col + 3 + t], None, ALU.mult).then_inc(S["normed"], 1)

            def gained(norm, i, u, dst):
                dve.wait_ge(S["tokp"], 2 * norm + i + 1)
                g = gains[:, norm * KD + 4 * i:norm * KD + 4 * i + 4].unsqueeze(2).to_broadcast([P, 4, L])
                dve.tensor_tensor(dst[:, 4 * i:4 * i + 4], pt[u][:, :].rearrange("p (k l) -> p k l", k=4), g,
                                  ALU.mult).then_inc(S["tokv"], 1)

            def residual_tile(t, u, done):
                if t == 0:
                    dve.wait_ge(S["tile0"], {"mh": 1, "xh": 2}[done])
                else:
                    slab_done(dve, {"mh": "mx1", "xh": "xo1"}[done])
                dve.tensor_tensor(h3[:, t], h3[:, t], pt[u][:, :], ALU.add).then_inc(S[done], 1)
                dve.wait_ge(S[done], t + 1)

            def norm_tile(norm, t):
                col = 4 * norm + 2 + t
                dve.wait_ge(S["root"], 3 + 2 * (norm - 2) + t + 1)
                link(dve.reciprocal(st[:, col:col + 1], st[:, col:col + 1]))
                dve.tensor_scalar(xn[:, t], h3[:, t], st[:, col:col + 1], None, ALU.mult).then_inc(S["normed"], 1)

            def gained_tile(norm, t, u):
                dve.wait_ge(S["tokp"], 2 * norm + t + 1)
                g = gains[:, norm * KD:(norm + 1) * KD].unsqueeze(2).to_broadcast([P, KD, P])
                dve.tensor_tensor(hnT[:, :, P * t:P * (t + 1)], pt[u][:, :].rearrange("p (k l) -> p k l", k=KD), g,
                                  ALU.mult).then_inc(S["tokv"], 1)

            dve.memset(t3[:, 0:512], 0.0)
            dve.memset(st[:, 60:61], EPS).then_inc(S["epsv"], 1)
            normed(0, h3, xn)
            dve.wait_ge(S["graw"], 1)
            link(dve.tensor_copy(gains[:, :], pt[PA][:, 0:4 * KD]))
            gained(0, 0, PC, hnT)
            gained(0, 1, PD, hnT)

            dve.wait_ge(s_par, 96)
            for i in range(2):
                last = dve.tensor_tensor_reduce(lamb[:, 2 * i * DH:(2 * i + 1) * DH], lamb[:, 2 * i * DH:(2 * i + 1) * DH],
                                                lamb[:, (2 * i + 1) * DH:(2 * i + 2) * DH], 1.0, 0.0, ALU.mult, ALU.add,
                                                st[:, 41 + i:42 + i])
            last.then_inc(S["lamx"], 1)

            are, aim, dt = prep[:, 0:128], prep[:, 128:256], prep[:, 258:260]
            ad, th, mag, kk, red, sn, ab, cs = (prep[:, 384 + 128 * i:512 + 128 * i] for i in range(8))
            d2 = lambda x: x.rearrange("p (d m) -> p d m", d=2)
            dve.wait_ge(s_small, 48)
            dve.wait_ge(S["dtl"], 1)
            dtb = dt.unsqueeze(2).to_broadcast([G, 2, NS])
            dve.tensor_tensor(d2(ad), d2(are), dtb, ALU.mult).then_inc(S["mag"], 1)
            link(dve.tensor_tensor(d2(th), d2(aim), dtb, ALU.mult))
            link(dve.tensor_scalar(kk, th, 1.0 / TWO_PI, ROUND, ALU.mult, ALU.add))
            link(dve.tensor_scalar(kk, kk, ROUND, None, ALU.subtract))
            link(dve.scalar_tensor_tensor(red, kk, -PI_A, th, ALU.mult, ALU.add))
            link(dve.scalar_tensor_tensor(red, kk, -PI_B, red, ALU.mult, ALU.add))
            link(dve.scalar_tensor_tensor(red, kk, -PI_C, red, ALU.mult, ALU.add))
            link(dve.tensor_scalar(red, red, 3.1415925, -3.1415925, ALU.min, ALU.max))
            link(dve.scalar_tensor_tensor(ab, red, -1.0, red, ALU.mult, ALU.min))
            dve.tensor_scalar(ab, ab, TWO_PI / 4, None, ALU.add).then_inc(S["red"], 1)
            dve.wait_ge(S["trig"], 1)
            pwn = prep[:, 2048:4096].rearrange("p (c t m) -> p c t m", c=2, t=TC)
            link(dve.tensor_tensor(pwn[:, 0, 0], mag, cs, ALU.mult))
            link(dve.tensor_tensor(pwn[:, 1, 0], mag, sn, ALU.mult))

            def powers(a, b, n):
                tm = prep[:, 4608:4608 + n * P].rearrange("p (t m) -> p t m", t=n)
                pr, pi = (pwn[:, c, b - 1:b].to_broadcast([G, n, P]) for c in range(2))
                xr, xi = pwn[:, 0, 0:n], pwn[:, 1, 0:n]
                zr, zi = pwn[:, 0, a:a + n], pwn[:, 1, a:a + n]
                link(dve.tensor_tensor(tm, xr, pr, ALU.mult))
                link(dve.tensor_tensor(zr, xi, pi, ALU.mult))
                link(dve.tensor_tensor(zr, tm, zr, ALU.subtract))
                link(dve.tensor_tensor(tm, xr, pi, ALU.mult))
                link(dve.tensor_tensor(zi, xi, pr, ALU.mult))
                link(dve.tensor_tensor(zi, tm, zi, ALU.add))

            powers(1, 1, 1)
            powers(2, 2, 2)
            powers(4, 4, 4)
            nr, den, t0 = prep[:, 5632:5760], prep[:, 5760:5888], prep[:, 5888:6016]
            cf = prep[:, 4096:4352].rearrange("p (c m) -> p c m", c=2)
            link(dve.tensor_scalar(nr, pwn[:, 0, 0], 1.0, None, ALU.subtract))
            link(dve.tensor_tensor(den, are, are, ALU.mult))
            link(dve.tensor_tensor(t0, aim, aim, ALU.mult))
            link(dve.tensor_tensor(den, den, t0, ALU.add))
            link(dve.reciprocal(den, den))
            for c, (x, y, op) in enumerate(((nr, pwn[:, 1, 0], ALU.add), (pwn[:, 1, 0], nr, ALU.subtract))):
                link(dve.tensor_tensor(cf[:, c], x, are, ALU.mult))
                link(dve.tensor_tensor(t0, y, aim, ALU.mult))
                link(dve.tensor_tensor(cf[:, c], cf[:, c], t0, op))
                link(dve.tensor_tensor(cf[:, c], cf[:, c], den, ALU.mult))
            dve.tensor_copy(pw[:, :, :, 0:NS], pwn[:, :, :, 0:NS])
            for c in range(2):
                last = dve.tensor_copy(pw[:, c, :, NS:P], pwn[:, c, ::-1, NS:P])
            last.then_inc(S["tabsrc"], 1)

            cos = con[:, C_COS:C_COS + NT * 32].rearrange("p (t i) -> p t i", t=NT)
            sin = con[:, C_SIN:C_SIN + NT * 32].rearrange("p (t i) -> p t i", t=NT)
            dve.wait_ge(s_con, 16)
            rt1 = t3[:, 0:512].rearrange("p (c f i) -> p c f i", c=8, f=2)
            rt2 = t3[:, 512:1024].rearrange("p (c f i) -> p c f i", c=8, f=2)
            for n, slab, u, dst in ((1, "q", PB, qn), (2, "k", PA, kn)):
                slab_done(dve, slab)
                for t in range(NT):
                    x = pt[u][:, 512 * t:512 * (t + 1)].rearrange("p (c f i) -> p c f i", c=8, f=2)
                    y = dst[:, t].rearrange("p (c f i) -> p c f i", c=8, f=2)
                    cb = cos[:, t].unsqueeze(1).unsqueeze(1).to_broadcast([P, 8, 2, 32])
                    sb_ = sin[:, t].unsqueeze(1).unsqueeze(1).to_broadcast([P, 8, 2, 32])
                    dve.tensor_tensor(rt1, x, cb, ALU.mult)
                    link(dve.tensor_tensor(rt2, x, sb_, ALU.mult))
                    dve.tensor_tensor(y[:, :, 0], rt1[:, :, 0], rt2[:, :, 1], ALU.subtract)
                    last = dve.tensor_tensor(y[:, :, 1], rt1[:, :, 1], rt2[:, :, 0], ALU.add)
                    if t < NT - 1:
                        link(last)
                last.then_inc(S["rope"], 1)
                dve.wait_ge(S["rope"], n)
            dve.memset(big[0:DH, 0:1024], 0.0)
            dve.memset(t3[DH:P, 0:1024], 0.0).then_inc(S["kz"], 1)

            dve.wait_ge(S["taba"], 1)
            for c in range(2):
                dve.tensor_copy(ipow[0:NS, c, 0:7], wpow[0:NS, c, 6::-1])
                dve.tensor_copy(ipow[NS:P, c, 1:8], wpow[NS:P, c, 7:0:-1])
                dve.memset(ipow[0:NS, c, 7], 1.0 - c)
                link(dve.memset(ipow[NS:P, c, 0], 1.0 - c))
            dve.wait_ge(s_bc, 128)
            cfr, cfi = (lam8[:, c * G:(c + 1) * G].unsqueeze(2).to_broadcast([P, G, HG]) for c in range(2))
            link(dve.tensor_tensor(tmp_v, braw[:, 0], cfr, ALU.mult))
            link(dve.tensor_tensor(bbar[:, 0], braw[:, 1], cfi, ALU.mult))
            link(dve.tensor_tensor(bbar[:, 0], tmp_v, bbar[:, 0], ALU.subtract))
            link(dve.tensor_tensor(tmp_v, braw[:, 1], cfr, ALU.mult))
            link(dve.tensor_tensor(bbar[:, 1], braw[:, 0], cfi, ALU.mult))
            link(dve.tensor_tensor(bbar[:, 1], tmp_v, bbar[:, 1], ALU.add))
            link(dve.memset(ring[:, 20480:22528], 0.0))
            for c in range(2):
                dve.tensor_copy(bsplit[0:NS, c, :, 1], bbar[0:NS, c])
                last = dve.tensor_copy(bsplit[NS:P, c, :, 0], bbar[NS:P, c])
            last.then_inc(S["bspl"], 1)
            l8 = lam8[:, 0:128].rearrange("p (f c g) -> p f c g", f=2, c=2)
            for lo, hi, t in ((0, NS, TC - 1), (NS, P, 0)):
                dve.tensor_copy(l8[lo:hi, 0, 0], wpow[lo:hi, 0, t])
                dve.tensor_copy(l8[lo:hi, 1, 1], wpow[lo:hi, 0, t])
                dve.tensor_copy(l8[lo:hi, 0, 1], wpow[lo:hi, 1, t])
                link(dve.tensor_scalar(l8[lo:hi, 1, 0], wpow[lo:hi, 1, t], -1.0, None, ALU.mult))
            dve.wait_ge(S["laml"], 1)
            dve.wait_ge(s_par, 96)
            link(dve.tensor_tensor(st[:, 45:46], st[:, 44:45], st[:, 43:44], ALU.subtract))
            link(dve.tensor_scalar(st[:, 45:46], st[:, 45:46], LAMBDA_INIT, None, ALU.subtract))
            link(dve.tensor_scalar(st[:, 33:34], st[:, 32:33], 1.0 - LAMBDA_INIT, None, ALU.mult))

            def row_max(h):
                dve.wait_ge(S["scp"], h + 1)
                link(dve.tensor_reduce(sm[:, 4:8], pt[PD][:, :].rearrange("p (i l) -> p i l", i=4), AX.X, ALU.max))
                dve.tensor_scalar(sm[:, 0:4], sm[:, 4:8], -DH ** -0.5, None, ALU.mult).then_inc(S["smx"], 1)

            def weigh(h):
                dve.wait_ge(S["pex"], 4 * (h + 1))
                link(dve.reciprocal(sm[:, 16:20], sm[:, 8:12]))
                link(dve.tensor_scalar(sm[:, 20:22], sm[:, 18:20], st[:, 45:46], None, ALU.mult))
                for t in range(NT):
                    link(dve.tensor_scalar(prob[:, 1, t], prob[:, 1, t], sm[:, 20 + t:21 + t], None, ALU.mult))
                for t in range(NT):
                    last = dve.scalar_tensor_tensor(prob[:, 0, t], prob[:, 0, t], sm[:, 16 + t:17 + t], prob[:, 1, t],
                                                    ALU.mult, ALU.add)
                last.then_inc(S["pwv"], 1)

            def way_in(times):
                for t in times:
                    last = way_in_step(dve, t, tmp_v, link)
                    if t < WAY_IN_SPLIT - 1:
                        link(last)
                    else:
                        last.then_inc(S["bp"], 1)

            def lag0():
                dve.wait_ge(S["k0p"], 1)
                k0 = tmp_v.rearrange("p (j a) h -> p j a h", j=4)
                bm = con[:, C_BLK:C_BLK + P].rearrange("p (a h) -> p a h", a=8).unsqueeze(1).to_broadcast([P, 4, 8, HG])
                link(dve.tensor_tensor(k0, pt[PA][:, 0:512].rearrange("p (j a h) -> p j a h", j=4, a=8), bm, ALU.mult))
                k0s = lamb[:, 0:64].rearrange("p (j h) -> p j h", j=4)
                link(dve.tensor_reduce(k0s, k0.rearrange("p j a h -> p j h a"), AX.X, ALU.add))
                for j in range(4):
                    last = dve.scalar_tensor_tensor(tap0[:, j], con[:, C_M16:C_M16 + HG], st[:, 36 + j:37 + j],
                                                    k0s[:, j], ALU.mult, ALU.add)
                last.then_inc(S["kse"], 1)
                dve.wait_ge(S["kse"], 1)

            dve.wait_ge(S["tabp"], 1)
            for h, times in enumerate((range(0, 2), range(2, 4), range(4, WAY_IN_SPLIT), ())):
                row_max(h)
                weigh(h)
                if h == 0:
                    lag0()
                way_in(times)
            for r in range(1, 8, 2):
                dve.wait_ge(S["ltp"], r + 1)
                dve.tensor_copy(ring[:, 8192 + 1024 * r:8192 + 1024 * (r + 1)], pt[PD][:, :]).then_inc(S["ltv"], 1)
            normed(1, mn, mn)
            dve.wait_ge(S["pvp"], HEADS)
            dve.wait_ge(S["wtp"], HEADS)
            dve.wait_ge(s_tapw, 8 * 16)
            dve.tensor_copy(t1[:, 1024:2048], pt[PA][:, :]).then_inc(S["on"], 1)
            dve.wait_ge(S["on"], 1)
            dve.wait_ge(S["zp"], 2)
            dve.tensor_copy(ring[:, 23552:24576], pt[PD][:, :]).then_inc(S["zkv"], 1)
            dve.wait_ge(S["wta"], HEADS)
            gained(1, 0, PC, memT)
            for i, u in enumerate((PB, PD)):
                if i == 1:
                    gained(1, 1, PA, memT)
                dve.wait_ge(S["ztp"], i + 1)
                for c in range(2):
                    src = pt[u][NS:P, :].rearrange("p (a c j k) -> p c k j a", a=4, c=2, j=4)[:, c]
                    dst = zst[NS:P, :, c, :].rearrange("p k (j a) -> p k j a", j=4)[:, :, :, 4 * i:4 * i + 4]
                    dve.tensor_copy(dst, src[:, ::-1]).then_inc(S["zvv"], 1)
            link(dve.tensor_tensor(t1[:, 0:1024], t1[:, 1024:2048], t1[:, 1024:2048], ALU.mult))
            dve.tensor_reduce(st[:, 20:28], t1[:, 0:1024].rearrange("p (i e) -> p i e", i=8), AX.X, ALU.add).then_inc(S["ssq"], 1)
            dve.wait_ge(S["root"], 3)
            link(dve.reciprocal(st[:, 46:54], st[:, 46:54]))
            dve.tensor_tensor(on, on, st[:, 46:54].rearrange("p (t h) -> p t h", t=NT).unsqueeze(3)
                              .to_broadcast([P, NT, HEADS, P]), ALU.mult).then_inc(S["on"], 1)
            dve.wait_ge(S["zva"], 4)
            dve.wait_ge(S["zvv"], 4)
            link(dve.tensor_copy(xst[:, 0], zst[:, 0]))
            prod = lam8[:, 128:256].rearrange("p (f c g) -> p f c g", f=2, c=2)
            for k in range(1, NC):
                link(dve.tensor_tensor(prod, l8, xst[:, k - 1].unsqueeze(2).to_broadcast([P, 2, 2, G]), ALU.mult))
                link(dve.tensor_tensor(prod[:, 0], prod[:, 0], prod[:, 1], ALU.add))
                last = dve.tensor_tensor(xst[:, k], prod[:, 0], zst[:, k], ALU.add)
                if k < NC - 1:
                    link(last)
            last.then_inc(S["scan"], 1)
            dve.wait_ge(S["scan"], 1)
            dve.memset(enter[0:NS, :, :, 0:1], 0.0)
            dve.memset(enter[NS:P, :, :, NC - 1:NC], 0.0)
            for c in range(2):
                last = dve.tensor_copy(enter[NS:P, c, :, 0:NC - 1],
                                       xst[NS:P, NC - 2::-1, c, :].rearrange("p k g -> p g k"))
            last.then_inc(S["entv"], 1)
            dve.wait_ge(S["sgm"], 1)

            def gate_attention(i, u):
                slab_done(dve, f"ba{i}")
                dve.tensor_tensor(a1[:, 1024 * i:1024 * (i + 1)], a1[:, 1024 * i:1024 * (i + 1)], pt[u][:, :],
                                  ALU.mult).then_inc(S["bav"], 1)

            gate_attention(0, PB)
            dve.wait_ge(S["gls"], 1)
            dve.tensor_tensor(uT_[:, :], glu_flat, pt[PC][:, :], ALU.mult).then_inc(S["osv"], 1)
            gate_attention(1, PA)
            for i, u in enumerate((PB, PC)):
                slab_done(dve, f"bs{i}")
                dve.wait_ge(S["bav"], i + 1)
                dve.tensor_tensor(a2[:, 1024 * i:1024 * (i + 1)], a2[:, 1024 * i:1024 * (i + 1)], pt[u][:, :],
                                  ALU.mult).then_inc(S["bsv"], 1)
                dve.wait_ge(S["bsv"], 2 * i + 1)
                dve.tensor_tensor(a1[:, 1024 * i:1024 * (i + 1)], a1[:, 1024 * i:1024 * (i + 1)],
                                  a2[:, 1024 * i:1024 * (i + 1)], ALU.add).then_inc(S["bsv"], 1)

            residual_tile(0, PD, "mh")
            norm_tile(2, 0)
            gained_tile(2, 0, PB)
            residual_tile(1, PA, "mh")
            norm_tile(2, 1)
            gained_tile(2, 1, PA)
            for i, u in enumerate((PA, PB)):
                dve.wait_ge(S["xsp"], i + 1)
                link(dve.tensor_reduce(sm[:, 24:28], pt[u][:, :].rearrange("p (i l) -> p i l", i=4), AX.X, ALU.max))
                dve.tensor_scalar(sm[:, 4 * i:4 * i + 4], sm[:, 24:28], -(D // HEADS) ** -0.5, None, ALU.mult).then_inc(S["xmx"], 1)
                dve.wait_ge(S["xmx"], i + 1)
            for h in range(HEADS):
                dve.wait_ge(S["xex"], 2 * (h + 1))
                link(dve.reciprocal(sm[:, 16 + 2 * h:18 + 2 * h], sm[:, 8 + 2 * h:10 + 2 * h]))
                for t in range(NT):
                    last = dve.tensor_scalar(p2[:, h, t], p2[:, h, t], sm[:, 16 + 2 * h + t:17 + 2 * h + t], None, ALU.mult)
                last.then_inc(S["xpn"], 1)
            residual_tile(0, PC, "xh")
            norm_tile(3, 0)
            gained_tile(3, 0, PA)
            residual_tile(1, PD, "xh")
            norm_tile(3, 1)
            dve.memset(part(1104, NT * 3 * SLOTS), 0.0)
            dve.memset(gT, 0.0)
            dve.memset(idx[:, NE:], 0)
            dve.tensor_copy(idx[:, 0:NE], con[:, C_IOTA:C_IOTA + NE])
            link(dve.memset(offs, 0.0))

            def top(t):
                dve.wait_ge(S["lgp"], t + 1)
                dve.tensor_tensor(lg[:, t], pt[PB][:, 512 * t:512 * t + NE], brt, ALU.add).then_inc(S["lgv"], 1)
                dve.wait_ge(S["lgv"], t + 1)
                link(dve.max(top8[:, t], lg[:, t]))
                link(dve.tensor_scalar(pse[:, 0, t:t + 1], top8[:, t, 0:1], -1.0, None, ALU.mult))
                link(dve.memset(top8[:, t, TOPK:8], 3.0e38))
                link(dve.match_replace(rep[:, t], top8[:, t], lg[:, t], -3.0e38))
                dve.tensor_tensor(msk[:, t], lg[:, t], rep[:, t], ALU.not_equal).then_inc(S["msk"], 1)
                dve.wait_ge(S["msk"], t + 1)

            top(0)
            gained_tile(3, 1, PC)
            top(1)
            for t in range(NT):
                dve.wait_ge(S["lex"], t + 1)
                link(dve.tensor_tensor(gate[:, t], gate[:, t], msk[:, t], ALU.mult))
                link(dve.tensor_reduce(pse[:, 1, t:t + 1], gate[:, t], AX.X, ALU.add))
                link(dve.reciprocal(pse[:, 1, t:t + 1], pse[:, 1, t:t + 1]))
                dve.tensor_scalar(gate[:, t], gate[:, t], pse[:, 1, t:t + 1], None, ALU.mult).then_inc(S["gdv"], 1)
            dve.wait_ge(S["rkp"], 1)
            link(dve.scalar_tensor_tensor(posn, pt[PD][:, 0:NT * NE].rearrange("p (t e) -> p t e", t=NT), 1.0, msk,
                                          ALU.add, ALU.mult))
            link(dve.tensor_scalar(posn, posn, 1.0, None, ALU.subtract))
            io = con[:, C_IOTA:C_IOTA + SLOTS]

            def place(it, e, chain):
                dve.tensor_copy(pse[:, 1, :], gate[:, :, bass.ds(e, 1)].rearrange("p t e -> p (t e)"))
                chain(dve.tensor_tensor(pse[:, 0, :], posn[:, :, bass.ds(e, 1)].rearrange("p t e -> p (t e)"),
                                        offs[:, bass.ds(it, 1)].to_broadcast([P, NT]), ALU.subtract))
                for t in range(NT):
                    dve.tensor_scalar(sel[:, t], io, pse[:, 0, t:t + 1], None, ALU.is_equal)
                dve.tensor_copy(ecol, con[:, bass.ds(e, 1)].to_broadcast([P, SLOTS])).then_inc(m_sel, 1)

            place(0, 0, link)
            cnt = pt[PD][0:NE, 512:513]
            link(dve.tensor_scalar(nbx[:, 0:1], cnt, float(SLOTS), None, ALU.is_gt))
            for b in range(2, MAXB):
                last = dve.scalar_tensor_tensor(nbx[:, 0:1], cnt, float(SLOTS * b), nbx[:, 0:1], ALU.is_gt, ALU.add)
                if b < MAXB - 1:
                    link(last)
            last.then_inc(S["rkv"], 1)
            dve.wait_ge(S["rkv"], 1)
            dve.wait_ge(m_x, 1)
            dve.tensor_copy(xgn, pt[PD][:, 0:512]).then_inc(m_xn, 1)
            dve.wait_ge(S["cup"], 1)
            link(dve.tensor_copy(nbx[:, 1:2], pt[PD][0:NE, 513:514]))
            link(dve.tensor_scalar(blk[:, 0:EXTRA], con[0:NE, C_IOTA:C_IOTA + EXTRA], nbx[:, 1:2], None, ALU.is_ge))
            link(dve.tensor_scalar(blk[:, EXTRA:2 * EXTRA], blk[:, 0:EXTRA], nbx[:, 0:1], None, ALU.mult))
            dve.tensor_copy(blk[:, 2 * EXTRA:2 * EXTRA + 1], nbx[:, 0:1]).then_inc(S["cuv"], 1)
            dve.wait_ge(m_xt, 1)
            dve.tensor_copy(xT_flat, pt[PD][:, 0:512]).then_inc(m_xT, 1)
            dve.wait_ge(S["ovp"], 1)
            tab = pt[PD][:, 512:512 + 2 * EXTRA + 1]
            link(dve.tensor_tensor(offs[:, NE:NE + EXTRA], con[:, C_IOTA:C_IOTA + EXTRA], tab[:, EXTRA:2 * EXTRA], ALU.subtract))
            link(dve.tensor_scalar(offs[:, NE:NE + EXTRA], offs[:, NE:NE + EXTRA], 1.0, float(SLOTS), ALU.add, ALU.mult))
            link(dve.tensor_scalar(ovf[:, 0:EXTRA], tab[:, 0:EXTRA], float(NE - 1), None, ALU.min))
            dve.tensor_copy(idx[:, NE:NE + EXTRA], ovf[:, 0:EXTRA])
            dve.tensor_copy(idx[:, NE + EXTRA + 1:], tab[:, 2 * EXTRA:]).then_inc(S["ovi"], 1)
            dve.wait_ge(S["ovi"], 1)
            STEPS = 3

            def block_of(it):
                n = [0]

                def chain(ins):
                    n[0] += 1
                    ins.then_inc(m_v, 1)
                    dve.wait_ge(m_v, it * STEPS + n[0])

                for t in range(NT):
                    last = dve.tensor_scalar(selw[:, t, SLOTS:2 * SLOTS], io, pse[:, 0, t:t + 1], pse[:, 1, t:t + 1],
                                             ALU.is_equal, ALU.mult)
                last.then_inc(m_selw, 1)
                dve.wait_ge(m_selw, it + 1)
                dve.wait_ge(m_w1u, KD * it + 2)
                place(it + 1, dve.value_load(idx[0:1, bass.ds(it + 1, 1)], min_val=0, max_val=NE - 1), chain)
                dve.wait_ge(m_w1u, KD * (it + 1))
                dve.tensor_scalar(hg, pt[PC][:, 0:512], GATE_MAX, None, ALU.min).then_inc(m_g2, 1)
                chain(dve.tensor_scalar(hl, pt[PC][:, 512:1024], GATE_MAX, -GATE_MAX, ALU.min, ALU.max))
                chain(dve.scalar_tensor_tensor(hgl, hl, 1.0, hg, ALU.add, ALU.mult))
                dve.wait_ge(m_sig, it + 1)
                dve.tensor_tensor(hact, hgl, hsg, ALU.mult).then_inc(m_act, 1)
                dve.wait_ge(m_x, it + 2)
                dve.tensor_copy(xgn, pt[PD][:, 0:512]).then_inc(m_xn, 1)
                dve.wait_ge(m_xt, it + 2)
                dve.tensor_copy(xT_flat, pt[PD][:, 0:512]).then_inc(m_xT, 1)
                assert n[0] == STEPS

            with dve.Fori(0, NE) as e:
                block_of(e)
            n_extra = dve.value_load(idx[0:1, NE + EXTRA + 1:NE + EXTRA + 2], min_val=0, max_val=EXTRA)
            with dve.If(n_extra > 0):
                with dve.Fori(0, EXTRA) as j:
                    with dve.If(n_extra > j):
                        block_of(NE + j)

            dve.wait_ge(s_gf, 32)
            for t in range(NT):
                dve.wait_ge(S["root"], 8 + t)
                link(dve.reciprocal(st[:, 18 + t:19 + t], st[:, 18 + t:19 + t]))
                dve.scalar_tensor_tensor(h3[:, t], pt[(PA, PB)[t]][:, :], st[:, 18 + t:19 + t], gfin, ALU.mult,
                                         ALU.mult).then_inc(S["gfin"], 1)


_INS = ["x", "mem", "norm_mix_g", "w_in", "lambda_q1", "lambda_k1", "lambda_q2", "lambda_k2", "subln_g",
        "ssm_a_re", "ssm_a_im", "ssm_log_dt", "ssm_b_re", "ssm_b_im", "ssm_c_re", "ssm_c_im", "ssm_d", "w_glu",
        "w_branch_attn", "w_branch_ssm", "w_mix_out", "norm_cross_g", "norm_mem_g", "w_xq", "w_xkv", "w_xo",
        "norm_ffn_g", "w_router", "b_router", "w_e1", "b_e1", "w_e2", "b_e2", "norm_final_g"]


def kernel(**inputs):
    import numpy as _np
    import concourse.bacc as _bacc
    from concourse import mybir as _mybir
    from concourse.bass_utils import run_bass_kernel_spmd as _run

    nc = _bacc.Bacc("TRN2", target_bir_lowering=False, num_devices=1)
    arrays, T = {}, {}
    for name in _INS:
        a = _np.ascontiguousarray(inputs[name])
        arrays[f"in_{name}"] = a
        T[name] = nc.dram_tensor(f"in_{name}", a.shape, _mybir.dt.from_np(a.dtype), kind="ExternalInput").ap()
    arrays["consts"] = constants()
    T["consts"] = nc.dram_tensor("consts", (P, C_END), F32, kind="ExternalInput").ap()
    out = nc.dram_tensor("out_dram", (1, L, D), F32, kind="ExternalOutput").ap()
    build(nc, T, out)
    r = _run(nc, [arrays], core_ids=[0])
    return r.results[0]["out_dram"]
```
